# Optimizing a Trainium2 kernel written in Bass

```python
import math
import jax, jax.numpy as jnp
from jax import lax
import numpy as np

D_MODEL = 1024
BATCH = 1
SEQ = 1024
DEPTH = 1
DEC_BATCH = 8
DEC_SEQ = 1
PAST_LEN = 8192
PAGE_SIZE = 128

N_META = 16
LN_EPS = 1e-5
GLA_HEADS = 4
GLA_DK = (D_MODEL // 2) // GLA_HEADS
GLA_DV = D_MODEL // GLA_HEADS
GLA_RANK = 16
GLA_TAU = 16.0
GLA_CHUNK = 64
HEAD_DIM = 64
ATT_HEADS = D_MODEL // HEAD_DIM
ATT_KV_HEADS = 4
GQA_GROUP = ATT_HEADS // ATT_KV_HEADS
WINDOW = 128
ATT_BLOCK = 128
REL_BUCKETS = 32
REL_MAX_DIST = 128
N_GROUPS = 4
EXPERTS_PER_GROUP = 8
N_EXPERTS = N_GROUPS * EXPERTS_PER_GROUP
TOP_K = 2
D_EXPERT = D_MODEL // 2
MOE_BLOCK = 128
ALPHA = (2.0 * DEPTH) ** 0.25
BETA = (8.0 * DEPTH) ** -0.25
PROJ_SIZES = (GLA_HEADS * GLA_DK, GLA_HEADS * GLA_DK, GLA_HEADS * GLA_DV, GLA_HEADS * GLA_DV, GLA_RANK,
              ATT_HEADS * HEAD_DIM, ATT_KV_HEADS * HEAD_DIM, ATT_KV_HEADS * HEAD_DIM, D_MODEL, D_MODEL)
PROJ_WIDTH = sum(PROJ_SIZES)

kernel_name = "hybrid_gla_swa_sink_hmoe_step"

def layer_norm(x, g, b):
    xf = x.astype(jnp.float32)
    mu = jnp.mean(xf, -1, keepdims=True)
    var = jnp.mean(jnp.square(xf - mu), -1, keepdims=True)
    return ((xf - mu) * lax.rsqrt(var + LN_EPS) * g.astype(jnp.float32) + b.astype(jnp.float32)).astype(x.dtype)

def rel_bucket(dist):
    max_exact = REL_BUCKETS // 2
    d = jnp.maximum(dist, 0)
    large = max_exact + (jnp.log(jnp.maximum(d, 1).astype(jnp.float32) / max_exact)
                         / math.log(REL_MAX_DIST / max_exact) * (REL_BUCKETS - max_exact)).astype(jnp.int32)
    large = jnp.minimum(large, REL_BUCKETS - 1)
    return jnp.where(d < max_exact, d, large)

def rel_bias_for(dist, table):
    b = table[rel_bucket(dist)].astype(jnp.float32)
    b = b.reshape(dist.shape + (ATT_KV_HEADS, GQA_GROUP))
    return jnp.moveaxis(b, (-2, -1), (0, 1))

def sink_softmax(scores, mask, sinks):
    sink = sinks.astype(jnp.float32).reshape(ATT_KV_HEADS, GQA_GROUP, 1, 1)
    s = jnp.where(mask, scores, -jnp.inf)
    m = jnp.maximum(jnp.max(s, -1, keepdims=True), sink)
    p = jnp.exp(s - m)
    return p / (jnp.sum(p, -1, keepdims=True) + jnp.exp(sink - m))

def combined_projection(h, w_in, gk_up, gk_bias):
    n, t, _ = h.shape
    idx = np.cumsum(PROJ_SIZES)[:-1].tolist()
    q_g, k_g, v_g, r_g, lr_g, q_a, k_a, v_a, gate_a, gate_b = jnp.split(h @ w_in, idx, axis=-1)
    q_g = q_g.reshape(n, t, GLA_HEADS, GLA_DK) * (GLA_DK ** -0.5)
    k_g = k_g.reshape(n, t, GLA_HEADS, GLA_DK)
    v_g = v_g.reshape(n, t, GLA_HEADS, GLA_DV)
    log_a = (jax.nn.log_sigmoid((lr_g @ gk_up + gk_bias).astype(jnp.float32)) / GLA_TAU)
    log_a = log_a.reshape(n, t, GLA_HEADS, GLA_DK)
    q_a = q_a.reshape(n, t, ATT_HEADS, HEAD_DIM)
    k_a = k_a.reshape(n, t, ATT_KV_HEADS, HEAD_DIM)
    v_a = v_a.reshape(n, t, ATT_KV_HEADS, HEAD_DIM)
    return q_g, k_g, v_g, r_g, log_a, q_a, k_a, v_a, gate_a, gate_b

def gla_chunked(q, k, v, log_a, s0, chunk):
    n, t, h, dk = q.shape
    dv = v.shape[-1]
    nc = t // chunk

    def to_chunks(x):
        return x.astype(jnp.float32).reshape(n, nc, chunk, h, x.shape[-1]).transpose(1, 0, 3, 2, 4)

    causal = jnp.tril(jnp.ones((chunk, chunk), dtype=bool))

    def step(s, inp):
        qc, kc, vc, gc = inp
        b = jnp.cumsum(gc, axis=2)
        o_inter = jnp.einsum('nhid,nhde->nhie', qc * jnp.exp(b), s)
        diff = b[:, :, :, None, :] - b[:, :, None, :, :]
        decay = jnp.exp(jnp.where(causal[:, :, None], diff, -jnp.inf))
        attn = jnp.einsum('nhid,nhjd,nhijd->nhij', qc, kc, decay)
        o = o_inter + jnp.einsum('nhij,nhje->nhie', attn, vc)
        b_last = b[:, :, -1:, :]
        s_new = jnp.exp(b_last[:, :, 0, :])[..., None] * s + jnp.einsum('nhjd,nhje->nhde', kc * jnp.exp(b_last - b), vc)
        return s_new, o

    s_fin, o = lax.scan(step, s0, (to_chunks(q), to_chunks(k), to_chunks(v), to_chunks(log_a)))
    o = o.transpose(1, 0, 3, 2, 4).reshape(n, t, h, dv)
    return o, s_fin

def gla_run(q, k, v, log_a, s0, chunk, pad_front):
    t = q.shape[1]
    pad_back = (-(t + pad_front)) % chunk
    padt = lambda x: jnp.pad(x, ((0, 0), (pad_front, pad_back), (0, 0), (0, 0)))
    o, s = gla_chunked(padt(q), padt(k), padt(v), padt(log_a), s0, chunk)
    return o[:, pad_front:pad_front + t], s

def gla_output(o, r, g):
    o = o * lax.rsqrt(jnp.mean(jnp.square(o), -1, keepdims=True) + LN_EPS) * g.astype(jnp.float32)
    n, t = o.shape[:2]
    return (o.reshape(n, t, -1) * jax.nn.silu(r.astype(jnp.float32))).astype(r.dtype)

def swa_prompt(q, k, v, rel_bias, sinks):
    n, l = q.shape[:2]
    pad = (-l) % ATT_BLOCK
    nb = (l + pad) // ATT_BLOCK
    padt = lambda x: jnp.pad(x, ((0, 0), (pad, 0), (0, 0), (0, 0)))
    qb = padt(q).reshape(n, nb, ATT_BLOCK, ATT_KV_HEADS, GQA_GROUP, HEAD_DIM)
    kb = padt(k).reshape(n, nb, ATT_BLOCK, ATT_KV_HEADS, HEAD_DIM)
    vb = padt(v).reshape(n, nb, ATT_BLOCK, ATT_KV_HEADS, HEAD_DIM)
    prev = lambda x: jnp.pad(x, ((0, 0), (1, 0), (0, 0), (0, 0), (0, 0)))[:, :-1]
    kk = jnp.concatenate([prev(kb), kb], axis=2)
    vv = jnp.concatenate([prev(vb), vb], axis=2)
    dist = ATT_BLOCK + jnp.arange(ATT_BLOCK)[:, None] - jnp.arange(2 * ATT_BLOCK)[None, :]
    k_pos = (jnp.arange(nb)[:, None] - 1) * ATT_BLOCK + jnp.arange(2 * ATT_BLOCK)[None, :] - pad
    mask = ((dist >= 0) & (dist < WINDOW))[None] & (k_pos >= 0)[:, None, :]
    scores = jnp.einsum('nbqkgd,nbckd->nbkgqc', qb, kk).astype(jnp.float32) * (HEAD_DIM ** -0.5)
    scores = scores + rel_bias_for(dist, rel_bias)
    p = sink_softmax(scores, mask[None, :, None, None], sinks)
    o = jnp.einsum('nbkgqc,nbckd->nbqkgd', p.astype(v.dtype), vv)
    return o.reshape(n, nb * ATT_BLOCK, ATT_HEADS * HEAD_DIM)[:, pad:]

def swa_sample(q, k, v, cache_k, cache_v, rel_bias, sinks):
    n, s = q.shape[:2]
    wb = cache_k.shape[1]
    kk = jnp.concatenate([cache_k.astype(k.dtype), k], axis=1)
    vv = jnp.concatenate([cache_v.astype(v.dtype), v], axis=1)
    qg = q.reshape(n, s, ATT_KV_HEADS, GQA_GROUP, HEAD_DIM)
    dist = wb + jnp.arange(s)[:, None] - jnp.arange(wb + s)[None, :]
    mask = (dist >= 0) & (dist < WINDOW)
    scores = jnp.einsum('nqkgd,nckd->nkgqc', qg, kk).astype(jnp.float32) * (HEAD_DIM ** -0.5)
    scores = scores + rel_bias_for(dist, rel_bias)
    p = sink_softmax(scores, mask, sinks)
    o = jnp.einsum('nkgqc,nckd->nqkgd', p.astype(v.dtype), vv).reshape(n, s, ATT_HEADS * HEAD_DIM)
    return o, kk[:, -wb:], vv[:, -wb:]

def hier_moe(x, w_rg, b_rg, w_re, b_re, w_gate, w_up, w_down):
    t = x.shape[0]
    xf = x.astype(jnp.float32)
    g_logits = xf @ w_rg.astype(jnp.float32) + b_rg.astype(jnp.float32)
    g_prob = jax.nn.softmax(g_logits, axis=-1)
    grp = jnp.argmax(g_logits, axis=-1)
    p_grp = jnp.take_along_axis(g_prob, grp[:, None], axis=1)[:, 0]
    e_logits = (xf @ w_re.astype(jnp.float32) + b_re.astype(jnp.float32)).reshape(t, N_GROUPS, EXPERTS_PER_GROUP)
    e_in = jnp.take_along_axis(e_logits, grp[:, None, None], axis=1)[:, 0]
    top_v, top_i = lax.top_k(e_in, TOP_K)
    w_top = jax.nn.softmax(top_v, axis=-1) * p_grp[:, None]
    expert = grp[:, None] * EXPERTS_PER_GROUP + top_i

    a = t * TOP_K
    e_flat = expert.reshape(a).astype(jnp.int32)
    tok_flat = jnp.repeat(jnp.arange(t, dtype=jnp.int32), TOP_K)
    w_flat = w_top.reshape(a)
    order = jnp.argsort(e_flat)
    e_s, tok_s, w_s = e_flat[order], tok_flat[order], w_flat[order]
    counts = jnp.zeros((N_EXPERTS,), jnp.int32).at[e_flat].add(1)
    starts = jnp.cumsum(counts) - counts
    padded = (counts + MOE_BLOCK - 1) // MOE_BLOCK * MOE_BLOCK
    pend = jnp.cumsum(padded)
    pstart = pend - padded
    dest = pstart[e_s] + (jnp.arange(a, dtype=jnp.int32) - starts[e_s])
    n_blocks = -(-a // MOE_BLOCK) + N_EXPERTS
    buf = jnp.zeros((n_blocks * MOE_BLOCK, x.shape[1]), x.dtype).at[dest].set(x[tok_s])
    block_start = jnp.arange(n_blocks, dtype=jnp.int32) * MOE_BLOCK
    block_e = jnp.minimum(jnp.searchsorted(pend, block_start, side='right'), N_EXPERTS - 1)

    def expert_block(args):
        xb, e = args
        hb = jax.nn.silu(xb @ w_gate[e]) * (xb @ w_up[e])
        return hb @ w_down[e]

    out = lax.map(expert_block, (buf.reshape(n_blocks, MOE_BLOCK, -1), block_e)).reshape(n_blocks * MOE_BLOCK, -1)
    return jax.ops.segment_sum(out[dest] * w_s[:, None].astype(out.dtype), tok_s, num_segments=t)

def layer_forward(h, gla_s0, win_k, win_v, rel_bias, w_in, gk_up, gk_bias, gla_norm_g, sinks, w_out,
                  ln1_g, ln1_b, w_rg, b_rg, w_re, b_re, w_gate, w_up, w_down, ln2_g, ln2_b, state_dtype):
    n, t, d = h.shape
    q_g, k_g, v_g, r_g, log_a, q_a, k_a, v_a, gate_a, gate_b = combined_projection(h, w_in, gk_up, gk_bias)
    if win_k is None:
        s0 = jnp.zeros((n, GLA_HEADS, GLA_DK, GLA_DV), jnp.float32)
        o_g, s_new = gla_run(q_g, k_g, v_g, log_a, s0, GLA_CHUNK, (-N_META) % GLA_CHUNK)
        o_a = swa_prompt(q_a, k_a, v_a, rel_bias, sinks)
        wb = min(WINDOW, t)
        k_new, v_new = k_a[:, -wb:], v_a[:, -wb:]
    else:
        o_g, s_new = gla_run(q_g, k_g, v_g, log_a, gla_s0.astype(jnp.float32), min(GLA_CHUNK, t), 0)
        o_a, k_new, v_new = swa_sample(q_a, k_a, v_a, win_k, win_v, rel_bias, sinks)
    y_g = gla_output(o_g, r_g, gla_norm_g)
    merged = jax.nn.sigmoid(gate_a) * y_g + jax.nn.sigmoid(gate_b) * o_a.astype(h.dtype)
    h1 = layer_norm(ALPHA * h + merged @ w_out, ln1_g, ln1_b)
    f = hier_moe(h1.reshape(n * t, d), w_rg, b_rg, w_re, b_re, w_gate, w_up, w_down).reshape(n, t, d)
    h2 = layer_norm(ALPHA * h1 + f, ln2_g, ln2_b)
    return h2, s_new.astype(state_dtype), k_new.astype(state_dtype), v_new.astype(state_dtype)

def setup_inputs(seed: int = 0) -> dict:
    key = jax.random.key(seed)
    ks = jax.random.split(key, 32)
    nrm = lambda k, shape, scale: jax.random.normal(k, shape, jnp.float32) * scale
    wb = min(WINDOW, PAST_LEN)
    L = DEPTH
    return {
        "x_prompt": nrm(ks[0], (BATCH, SEQ, D_MODEL), 1.0),
        "x_sample": nrm(ks[1], (DEC_BATCH, DEC_SEQ, D_MODEL), 1.0),
        "state_gla": nrm(ks[2], (L, DEC_BATCH, GLA_HEADS, GLA_DK, GLA_DV), 1.0),
        "cache_swa_k": nrm(ks[3], (L, DEC_BATCH, wb, ATT_KV_HEADS, HEAD_DIM), 1.0),
        "cache_swa_v": nrm(ks[4], (L, DEC_BATCH, wb, ATT_KV_HEADS, HEAD_DIM), 1.0),
        "meta_tokens": nrm(ks[5], (N_META, D_MODEL), 1.0),
        "ln_emb_g": 1.0 + nrm(ks[6], (D_MODEL,), 0.02),
        "ln_emb_b": nrm(ks[7], (D_MODEL,), 0.02),
        "rel_bias": nrm(ks[8], (REL_BUCKETS, ATT_HEADS), 0.1),
        "w_in": nrm(ks[9], (L, D_MODEL, PROJ_WIDTH), D_MODEL ** -0.5),
        "gk_up": nrm(ks[10], (L, GLA_RANK, GLA_HEADS * GLA_DK), GLA_RANK ** -0.5),
        "gk_bias": nrm(ks[11], (L, GLA_HEADS * GLA_DK), 0.1),
        "gla_norm_g": 1.0 + nrm(ks[12], (L, GLA_DV), 0.02),
        "sinks": nrm(ks[13], (L, ATT_HEADS), 0.5),
        "w_out": nrm(ks[14], (L, D_MODEL, D_MODEL), BETA * D_MODEL ** -0.5),
        "ln1_g": 1.0 + nrm(ks[15], (L, D_MODEL), 0.02),
        "ln1_b": nrm(ks[16], (L, D_MODEL), 0.02),
        "w_router_group": nrm(ks[17], (L, D_MODEL, N_GROUPS), D_MODEL ** -0.5),
        "b_router_group": nrm(ks[18], (L, N_GROUPS), 0.01),
        "w_router_expert": nrm(ks[19], (L, D_MODEL, N_EXPERTS), D_MODEL ** -0.5),
        "b_router_expert": nrm(ks[20], (L, N_EXPERTS), 0.01),
        "w_gate": nrm(ks[21], (L, N_EXPERTS, D_MODEL, D_EXPERT), D_MODEL ** -0.5),
        "w_up": nrm(ks[22], (L, N_EXPERTS, D_MODEL, D_EXPERT), D_MODEL ** -0.5),
        "w_down": nrm(ks[23], (L, N_EXPERTS, D_EXPERT, D_MODEL), BETA * D_EXPERT ** -0.5),
        "ln2_g": 1.0 + nrm(ks[24], (L, D_MODEL), 0.02),
        "ln2_b": nrm(ks[25], (L, D_MODEL), 0.02),
    }

def reference(x_prompt, x_sample, state_gla, cache_swa_k, cache_swa_v, meta_tokens, ln_emb_g, ln_emb_b,
              rel_bias, w_in, gk_up, gk_bias, gla_norm_g, sinks, w_out, ln1_g, ln1_b, w_router_group,
              b_router_group, w_router_expert, b_router_expert, w_gate, w_up, w_down, ln2_g, ln2_b):
    b = x_prompt.shape[0]
    meta = jnp.broadcast_to(meta_tokens.astype(x_prompt.dtype)[None], (b, N_META, x_prompt.shape[-1]))
    hp = layer_norm(jnp.concatenate([meta, x_prompt], axis=1), ln_emb_g, ln_emb_b)
    hs = layer_norm(x_sample, ln_emb_g, ln_emb_b)
    sd = state_gla.dtype
    gp, kp, vp, gs, kss, vss = [], [], [], [], [], []
    for l in range(DEPTH):
        lp = (w_in[l], gk_up[l], gk_bias[l], gla_norm_g[l], sinks[l], w_out[l], ln1_g[l], ln1_b[l],
              w_router_group[l], b_router_group[l], w_router_expert[l], b_router_expert[l],
              w_gate[l], w_up[l], w_down[l], ln2_g[l], ln2_b[l])
        hp, s_p, k_p, v_p = layer_forward(hp, None, None, None, rel_bias, *lp, sd)
        hs, s_s, k_s, v_s = layer_forward(hs, state_gla[l], cache_swa_k[l], cache_swa_v[l], rel_bias, *lp, sd)
        gp.append(s_p); kp.append(k_p); vp.append(v_p)
        gs.append(s_s); kss.append(k_s); vss.append(v_s)
    y_prompt = hp[:, N_META:]
    return (y_prompt, hs, jnp.stack(gp), jnp.stack(kp), jnp.stack(vp), jnp.stack(gs), jnp.stack(kss), jnp.stack(vss))


_drawn_inputs = setup_inputs


def setup_inputs(seed=0):
    import zlib

    import numpy as np

    out = dict(_drawn_inputs(seed))
    spreads = {}
    factors = {'meta_tokens': 2.769,
     'rel_bias': 58.2,
     'gla_norm_g': 21.331,
     'sinks': 200.0,
     'b_router_group': 7.424,
     'b_router_expert': 18.057,
     'ln2_g': 22.422,
     'ln2_b': 22.262}
    for name, (base, spread) in spreads.items():
        noise = np.random.default_rng([zlib.crc32(name.encode()), seed]).standard_normal(out[name].shape)
        drawn = base * np.exp(spread * noise) if base else spread * noise
        out[name] = __import__('jax').numpy.asarray(drawn.astype(out[name].dtype))
    for name, factor in factors.items():
        out[name] = (out[name] * factor).astype(out[name].dtype)
    return out
```

```python
from contextlib import ExitStack

import concourse.bass as bass
from concourse import mybir

F32 = mybir.dt.float32
F32R = mybir.dt.float32r
I32 = mybir.dt.int32
U32 = mybir.dt.uint32
ACT = mybir.ActivationFunctionType
ALU = mybir.AluOpType
X = mybir.AxisListType.X
ds = bass.ds

P = 128
D = 1024
KC = D // P
META = 16
NB = 9
NS = 8
PAD0 = P - META
G = 4
DK, DV, RANK, HD, HPG = 128, 256, 16, 64, 4
HEADS = 16
WIN = 128
ALPHA = 2.0 ** 0.25
EPS = 1e-5
TAU = 16.0
NEG = -1.0e30
NE = 32
DE = 512
MAXBLK = 50
CREDIT = 4
IN_Q, IN_K, IN_V, IN_R, IN_LR, IN_QA, IN_KA, IN_VA, IN_GA, IN_GB = (
    0, 512, 1024, 2048, 3072, 3088, 4112, 4368, 4624, 5648)
W_KA, W_VA, W_Q, W_K, W_QA, W_NARROW = 0, 128, 192, 320, 448, 704
W_V, W_R, W_GA, W_GB, W_WIDE = 0, 256, 512, 768, 1024
WIDE = 4
RAW_BASE = (G, G, G, G, 2, 2)
LROW = 384


def upto(n):
    return n + 1 + CREDIT


def build(nc, A, R):
    ctx = ExitStack()

    def sem(name):
        return ctx.enter_context(nc.semaphore(name))

    step_sems = []

    def ssem(name):
        s = sem(name)
        step_sems.append(s)
        return s

    h_dram = nc.dram_tensor("h_dram", (NB, P, D), F32).ap()
    hT_dram = nc.dram_tensor("hT_dram", (NB, P, D), F32).ap()
    mg_dram = nc.dram_tensor("mg_dram", (NB, P, D), F32).ap()
    h1_dram = nc.dram_tensor("h1_dram", (NB * P, D), F32).ap()
    brow_dram = nc.dram_tensor("brow_dram", (HEADS, P * LROW), F32).ap()
    stash_dram = nc.dram_tensor("stash_dram", (NS, G, 3, DV), F32).ap()
    obuf_dram = nc.dram_tensor("obuf_dram", (MAXBLK * P, D), F32).ap()
    prime_dram = nc.dram_tensor("prime_dram", (16, 16, 8), F32).ap()

    def sb(stack, name, shape, dt=F32):
        return stack.enter_context(nc.sbuf_tensor(name, shape, dt))

    both = ctx
    PS = ctx.enter_context(nc.psum_tensor("PS", [P, 8, 512], F32))
    ident = sb(both, "ident", [P, P])
    causal = sb(both, "causal", [P, P])
    strict = sb(both, "strict", [P, P])
    ones = sb(both, "ones", [P, P])
    eps_c = sb(both, "eps_c", [P, 1])
    lg = sb(both, "lg", [P, NB, 4 + NE])
    gsq = sb(both, "gsq", [P, G, NS])
    gsk = sb(both, "gsk", [P, G, NS])
    gse = sb(both, "gse", [P, G, NS])
    asq = sb(both, "asq", [P, G, 2, NS])
    ska = sb(both, "ska", [P, G, NS])
    sva = sb(both, "sva", [NS, G, HD])
    wts = sb(both, "wts", [P, NB, 2])
    ridx = sb(both, "ridx", [P, 2 * NB], U32)
    etab = sb(both, "etab", [P, MAXBLK], I32)
    novr = sb(both, "novr", [P, 1], I32)
    idx_all = sb(both, "idx_all", [P, MAXBLK], I32)

    sB = ExitStack()
    hTs = [sb(sB, f"hT{s}", [P, D]) for s in range(2)]
    hT_hl = sb(sB, "hT_hl", [P, 2, D], F32R)
    lrT = sb(sB, "lrT", [RANK, NB * P])
    s0 = ExitStack()
    x_t = [sb(s0, f"x_t{s}", [P, D]) for s in range(2)]
    hn = [sb(s0, f"hn{s}", [P, D]) for s in range(2)]
    lne_g = sb(s0, "lne_g", [P, D])
    lne_b = sb(s0, "lne_b", [P, D])
    st0 = [sb(s0, f"st0{s}", [P, 16]) for s in range(2)]
    wlr = sb(s0, "wlr", [P, KC, RANK])
    lr_t = sb(s0, "lr_t", [P, RANK])
    onehot = sb(s0, "onehot", [32, WIN])
    relb = sb(s0, "relb", [32, HEADS])
    relw = sb(s0, "relw", [32, HEADS, P])
    brow = sb(s0, "brow", [P, HEADS, LROW])
    prime = sb(s0, "prime", [16, 8])
    s0.close()
    wn = sb(sB, "wn", [P, KC, W_NARROW])
    w_hi = sb(sB, "w_hi", [P, KC, W_WIDE], F32R)
    w_lo = sb(sB, "w_lo", [P, KC, W_WIDE], F32R)
    braw = sb(sB, "braw", [P, WIDE, KC, 256])
    bias = sb(sB, "bias", [P, 2, HPG, 2 * P])
    sink = sb(sB, "sink", [P, HEADS])
    gkup = sb(sB, "gkup", [RANK, DK])
    gkb = sb(sB, "gkb", [P, 1])
    gn = sb(sB, "gn", [P, DV])
    xg = sb(sB, "xg", [P, P])
    ax = sb(sB, "ax", [P, P])
    mn = sb(sB, "mn", [P, P])
    g16 = sb(sB, "g16", [P, P])
    b16 = sb(sB, "b16", [P, P])
    bm = sb(sB, "bm", [P, 2])
    eq = sb(sB, "eq", [P, P])
    ek = sb(sB, "ek", [P, P])
    ebm = sb(sB, "ebm", [P, 1])
    e2 = sb(sB, "e2", [P, 1])
    kk = sb(sB, "kk", [P, P])
    qq = sb(sB, "qq", [P, P])
    At = sb(sB, "At", [P, P])
    kd = sb(sB, "kd", [P, P])
    Sm = sb(sB, "Sm", [P, DV])
    Tn = sb(sB, "Tn", [P, DV])
    kout = sb(sB, "kout", [P, HD])
    qa = sb(sB, "qa", [P, 2, P])
    ka = [sb(sB, f"ka{s}", [P, P]) for s in range(2)]
    va = [sb(sB, f"va{s}", [P, HD]) for s in range(2)]
    vr = sb(sB, "vr", [P, 2 * DV])
    Et = sb(sB, "Et", [P, 3, DV])
    Rt = sb(sB, "Rt", [P, 2, DV])
    rr = sb(sB, "rr", [P, DV])
    yg = sb(sB, "yg", [P, DV])
    oa = sb(sB, "oa", [P, DV])
    mgo = [sb(sB, f"mgo{s}", [P, DV]) for s in range(2)]
    Sc = sb(sB, "Sc", [P, HPG, 2 * P])
    Pt = sb(sB, "Pt", [P, 2, HPG, P])
    mx = sb(sB, "mx", [P, HPG])
    nmx = sb(sB, "nmx", [P, HPG])
    sk = sb(sB, "sk", [P, HPG])
    es = sb(sB, "es", [P, HPG])
    su = sb(sB, "su", [P, HPG])
    rden = sb(sB, "rden", [P, HPG])
    ssq = sb(sB, "ssq", [P, 1])
    lnv = sb(sB, "lnv", [P, 1])
    rstd = sb(sB, "rstd", [P, 1])
    sB.close()

    sE = ExitStack()
    raw = sb(sE, "raw", [P, 6, 2048])
    st = raw[:, 0:4].rearrange("p g (n e) -> p g n e", n=NS)
    sC = ExitStack()
    wo_hi = sb(sC, "wo_hi", [P, KC, D], F32R)
    wo_lo = sb(sC, "wo_lo", [P, KC, D], F32R)
    sS = ExitStack()
    Kd = sb(sS, "Kd", [P, NS, G, 2, HD])
    Vw = sb(sS, "Vw", [P, NS, G, HD])
    KT = sb(sS, "KT", [P, G, NS, P])
    km = [sb(sS, f"km{i}", [NS, NS, P]) for i in range(2)]
    kt8 = sb(sS, "kt8", [NS, G, P])
    qm = sb(sS, "qm", [P, G, NS, NS])
    knew = sb(sS, "knew", [NS, G, HD])
    gath = sb(sS, "gath", [NS, G, 3, DV])
    sT = sb(sS, "sT", [P, P])
    sS2 = sb(sS, "sS2", [P, P])
    sbias = sb(sS, "sbias", [P, P])
    ssink = sb(sS, "ssink", [P, 1])
    sm8 = sb(sS, "sm8", [P, 8])
    sPT = sb(sS, "sPT", [P, P])
    oT = sb(sS, "oT", [HD, HPG, G, NS])
    oS = sb(sS, "oS", [NS, G, DV])
    oQ = sb(sS, "oQ", [NS, G, DV])
    s8 = sb(sS, "s8", [NS, 3, G])
    sS.close()
    mg = [sb(sC, f"mg{s}", [P, D]) for s in range(2)]
    hh = [sb(sC, f"hh{s}", [P, D]) for s in range(2)]
    mT_hi = sb(sC, "mT_hi", [P, D], F32R)
    mT_lo = sb(sC, "mT_lo", [P, D], F32R)
    h1T = sb(sC, "h1T", [P, D])
    ln1_g = sb(sC, "ln1_g", [P, D])
    ln1_b = sb(sC, "ln1_b", [P, D])
    st1 = [sb(sC, f"st1{s}", [P, 16]) for s in range(2)]
    wr = sb(sC, "wr", [P, KC, 4 + NE])
    br = sb(sC, "br", [P, 4 + NE])
    sC.close()
    sD = ExitStack()
    iot = sb(sD, "iot", [P, P + 1])
    ioti = sb(sD, "ioti", [P, P + 1], I32)
    toki = sb(sD, "toki", [P, NB], I32)
    tok = sb(sD, "tok", [P, NB])
    oh_r = sb(sD, "oh_r", [P, 2 * NB, P])
    oh_b = sb(sD, "oh_b", [P, 2 * NB, MAXBLK])
    rt = {n: sb(sD, "rt_" + n, [P, NB]) for n in ("gm", "sg", "pg", "m1", "m2", "mi", "d", "e", "s", "r")}
    gq = [sb(sD, f"gq{i}", [P, NB, 4]) for i in range(3)]
    em = sb(sD, "em", [P, NB, NE])
    em2 = sb(sD, "em2", [P, NB, NE])
    tt_ = sb(sD, "tt_", [P, NB, NE])
    O = [sb(sD, f"O{i}", [P, NB, NE]) for i in range(3)]
    pre = sb(sD, "pre", [P, NB, NE])
    tot = sb(sD, "tot", [P, NB, NE])
    cum = sb(sD, "cum", [P, NE])
    ov = sb(sD, "ov", [P, NE])
    ove = sb(sD, "ove", [P, NE])
    ovs = sb(sD, "ovs", [P, NE])
    cmp_ = sb(sD, "cmp_", [P, 18, NE])
    ef = sb(sD, "ef", [P, 18])
    valid = sb(sD, "valid", [P, 2])
    sl = {n: sb(sD, "sl_" + n, [P, 2 * NB]) for n in ("rk", "bs", "ie", "k", "k1", "b", "r", "w")}
    sD.close()
    xw = [sb(sE, f"xw{s}", [P, D]) for s in range(2)]
    xi = [sb(sE, f"xi{s}", [P, 1], U32) for s in range(2)]
    wm_hi = sb(sE, "wm_hi", [P, 6, 2048], F32R)
    wm_lo = sb(sE, "wm_lo", [P, 6, 2048], F32R)
    xT_hi = sb(sE, "xT_hi", [P, D], F32R)
    xT_lo = sb(sE, "xT_lo", [P, D], F32R)
    sg_t = sb(sE, "sg_t", [P, DE])
    hm = sb(sE, "hm", [P, DE])
    hT_hi = sb(sE, "hT_hi", [P, DE], F32R)
    hT_lo = sb(sE, "hT_lo", [P, DE], F32R)
    yb = [sb(sE, f"yb{s}", [P, D]) for s in range(2)]
    sE.close()
    sF = ExitStack()
    ya = [sb(sF, f"ya{s}", [P, D]) for s in range(2)]
    yc = [sb(sF, f"yc{s}", [P, D]) for s in range(2)]
    h1l = [sb(sF, f"h1l{s}", [P, D]) for s in range(2)]
    zz = [sb(sF, f"zz{s}", [P, D]) for s in range(2)]
    st2 = [sb(sF, f"st2{s}", [P, 16]) for s in range(2)]
    fi = [sb(sF, f"fi{s}", [P, 2], U32) for s in range(2)]
    fw = [sb(sF, f"fw{s}", [P, 2]) for s in range(2)]
    ln2_g = sb(sF, "ln2_g", [P, D])
    ln2_b = sb(sF, "ln2_b", [P, D])
    sF.close()

    primed = []

    def dsem(name):
        s = sem(name)
        primed.append(s)
        return s

    c_id = sem("c_id")
    c_in = sem("c_in")
    c_rel = sem("c_rel")
    c_brow = sem("c_brow")
    c_z0 = sem("c_z0")
    e_x = [sem(f"e_x{s}") for s in range(2)]
    n_sa = ssem("n_sa")
    n_st = ssem("n_st")
    n_ln = ssem("n_ln")
    n_rs = ssem("n_rs")
    n_nm = ssem("n_nm")
    n_xn = ssem("n_xn")
    n_hg = ssem("n_hg")
    n_h = ssem("n_h")
    h_out = [dsem(f"h_out{s}") for s in range(2)]
    t_T = ssem("t_T")
    t_hi = ssem("t_hi")
    t_lo = ssem("t_lo")
    e_hTo = [dsem(f"e_hTo{s}") for s in range(2)]
    e_lr = ssem("e_lr")
    e_lrc = ssem("e_lrc")
    e_lrT = ssem("e_lrT")
    e_lrd = ssem("e_lrd")

    b_gn = sem("b_gn")
    b_gk = sem("b_gk")
    b_bi = sem("b_bi")
    b_wn = sem("b_wn")
    b_hs = ssem("b_hs")
    b_hl = ssem("b_hl")
    b_bv = ssem("b_bv")
    w_raw = [sem(f"w_raw{j}") for j in range(6)]
    b_hi = ssem("b_hi")
    b_lo = ssem("b_lo")
    b_hT = [sem(f"b_hT{s}") for s in range(2)]
    b_p5 = ssem("b_p5")
    b_p4 = ssem("b_p4")
    b_vr = ssem("b_vr")
    b_gg = ssem("b_gg")
    b_sc = ssem("b_sc")
    b_A = ssem("b_A")
    b_pt = ssem("b_pt")
    b_up = ssem("b_up")
    b_o = ssem("b_o")
    b_xg = ssem("b_xg")
    b_ka = ssem("b_ka")
    b_ax = ssem("b_ax")
    b_ex = ssem("b_ex")
    b_lx = ssem("b_lx")
    b_mn = ssem("b_mn")
    b_g16 = ssem("b_g16")
    b_b16 = ssem("b_b16")
    b_bmn = ssem("b_bmn")
    b_eq = ssem("b_eq")
    b_qa = ssem("b_qa")
    b_kk = ssem("b_kk")
    b_qq = ssem("b_qq")
    b_vrc = ssem("b_vrc")
    b_er = ssem("b_er")
    b_eg = ssem("b_eg")
    b_bs = ssem("b_bs")
    b_sz = sem("b_sz")
    b_mx = ssem("b_mx")
    b_mx2 = ssem("b_mx2")
    b_nmx = ssem("b_nmx")
    b_P = ssem("b_P")
    b_At = ssem("b_At")
    b_Sm = ssem("b_Sm")
    b_pc = ssem("b_pc")
    b_pd = ssem("b_pd")
    b_T = ssem("b_T")
    b_e2 = ssem("b_e2")
    b_den = ssem("b_den")
    b_rden = ssem("b_rden")
    b_E1 = ssem("b_E1")
    b_E2 = ssem("b_E2")
    b_R = ssem("b_R")
    b_rr = ssem("b_rr")
    b_rg = ssem("b_rg")
    b_sq = ssem("b_sq")
    b_lv = ssem("b_lv")
    b_rs = ssem("b_rs")
    b_yg = ssem("b_yg")
    b_oa = ssem("b_oa")
    b_ob = ssem("b_ob")
    b_mg = ssem("b_mg")
    b_mo = [dsem(f"b_mo{s}") for s in range(2)]
    b_sta = ssem("b_sta")
    b_std = sem("b_std")
    b_stg = sem("b_stg")
    b_fin = ssem("b_fin")
    b_kT = ssem("b_kT")
    b_ko = ssem("b_ko")
    b_gout = sem("b_gout")
    b_gfree = ssem("b_gfree")

    act_s, dve_s, pool_s = sem("act_s"), sem("dve_s"), sem("pool_s")
    s_pe = sem("s_pe")
    S_KT8, S_OUTER, S_OG, S_KT, S_SC, S_TR, S_PT, S_PV, S_OT = 1, (2, 3, 4, 5), 6, 7, 15, 16, 17, 18, 19
    s_dve = sem("s_dve")
    S_KNEW, S_KM, S_STATE, S_SSQ, S_ST, S_NMX, S_PROB, S_PTC, S_OTC, S_MERGED = (
        1, (2, 3, 5, 7), (4, 6, 8, 9), 11, 12, 13, 14, 15, 16, 17)
    s_qm = sem("s_qm")
    d_g, d_O, d_pre, d_route = (sem(n) for n in ("d_g", "d_O", "d_pre", "d_route"))
    s_in = sem("s_in")
    s_shift = sem("s_shift")
    s_new = sem("s_new")
    s_win = sem("s_win")
    s_out = sem("s_out")
    s_mg = sem("s_mg")

    o_small = sem("o_small")
    h_in = [sem(f"h_in{s}") for s in range(2)]
    o_z = ssem("o_z")
    o_zz = ssem("o_zz")
    u_T = ssem("u_T")
    u_c = ssem("u_c")
    o_rl = ssem("o_rl")
    o_lg = ssem("o_lg")

    d_table = sem("d_table")

    m_hi = [ssem(f"m_hi{i}") for i in range(2)]
    m_loD = [ssem(f"m_loD{i}") for i in range(2)]
    m_loP = [ssem(f"m_loP{i}") for i in range(2)]
    m_used = [ssem(f"m_used{i}") for i in range(2)]
    m_xi = ssem("m_xi")
    m_x = [sem(f"m_x{s}") for s in range(2)]
    m_sg = ssem("m_sg")
    m_hm = ssem("m_hm")
    m_hlo = ssem("m_hlo")
    m_ya = ssem("m_ya")
    m_yd = ssem("m_yd")
    m_yo = [dsem(f"m_yo{s}") for s in range(2)]

    f_small = sem("f_small")
    f_i = ssem("f_i")
    f_y = [sem(f"f_y{s}") for s in range(2)]
    f_w = ssem("f_w")
    f_a = ssem("f_a")
    f_b = ssem("f_b")
    f_z = ssem("f_z")
    s_fill = sem("s_fill")

    BF = lambda t: t.bitcast(F32)
    w_in = A["w_in"][0].rearrange("(k p) n -> p k n", p=P)

    def per_use(s, g, i):
        return 5 * g + i + 1 if s == 0 else 4 * g + i

    def pipelined(eng, first, second):
        first(0, 0)
        with eng.Fori(0, 4) as i:
            first(2 * i + 1, 1)
            second(2 * i, 0)
            first(2 * i + 2, 0)
            second(2 * i + 1, 1)
        second(8, 0)

    def use(b, s):
        return b // 2 if isinstance(b, int) else (b - s) // 2

    def wait_apart(eng, s, value):
        if not isinstance(value, int):
            value = eng.to_reg(value)
        eng.wait_ge(c_id, 3)
        eng.wait_ge(s, value)

    def piece_hi(t, j):
        return (m_hi[0], upto(4 * t + j)) if j < 4 else (m_hi[1], upto(2 * t + j - 4))

    def piece_lo(t, j):
        if j in (1, 5):
            return m_loP[j // 4], upto(t)
        return (m_loD[0], upto(3 * t + (0, None, 1, 2)[j])) if j < 4 else (m_loD[1], upto(t))

    def piece_used(t, j):
        return (m_used[0], upto(4 * t + j)) if j < 4 else (m_used[1], upto(2 * t + j - 4))

    def stored(stage, s, uses):
        return 16 * (1 + stage * (5 - s) + uses)

    def stage0_done(eng):
        for s in range(2):
            eng.wait_ge(e_hTo[s], 16 * (1 + 5 - s))
            eng.wait_ge(h_out[s], stored(0, s, 5 - s))
        eng.wait_ge(c_brow, 16)
        eng.wait_ge(e_lrd, upto(8))
        for s in primed:
            eng.wait_ge(s, 16)

    def stageB_done(eng):
        eng.wait_ge(b_gfree, upto(G - 1))
        eng.wait_ge(b_sta, upto(G - 1))
        eng.wait_ge(b_mg, upto(G * NB - 1))
        for s in range(2):
            eng.wait_ge(b_mo[s], 16 * (1 + (5 - s) * G))

    def stats(dve, z, t, s_a, s_b, n):
        dve.bn_stats(t[:, 0:6], z[:, 0:512])
        dve.bn_stats(t[:, 6:12], z[:, 512:1024]).then_inc(s_a, 1)
        wait_apart(dve, s_a, n)
        dve.bn_aggr(t[:, 12:14], t[:, 0:12]).then_inc(s_b, 1)

    block = ctx.enter_context(nc.Block())

    @block.sync
    def _(sp):
        sp.dma_start(relb[:], A["rel_bias"]).then_inc(c_in, 16)
        sp.dma_start(onehot[:], A["onehot"]).then_inc(c_in, 16)
        sp.wait_ge(c_z0, 1)
        sp.dma_start(x_t[0][0:NS, :], A["x_sample"].rearrange("n o d -> (n o) d")).then_inc(e_x[0], 16)
        sp.dma_start(x_t[0][PAD0:P, :], A["meta_tokens"]).then_inc(e_x[0], 16)
        sp.dma_start(x_t[1][:], A["x_prompt"][0, 0:P, :]).then_inc(e_x[1], 16)
        sp.dma_start(wlr[:], w_in[:, :, IN_LR:IN_LR + RANK], allow_slow_non_contiguous=True).then_inc(c_in, 16)
        sp.dma_start(lne_g[:], A["ln_emb_g"].rearrange("(o n) -> o n", o=1).to_broadcast([P, D])).then_inc(c_in, 16)
        sp.dma_start(lne_b[:], A["ln_emb_b"].rearrange("(o n) -> o n", o=1).to_broadcast([P, D])).then_inc(c_in, 16)
        sp.dma_start(R["swa_k_sample"][0, :, 0:WIN - 1], A["cache_swa_k"][0, :, 1:WIN]).then_inc(s_shift, 16)
        sp.dma_start(R["swa_v_sample"][0, :, 0:WIN - 1], A["cache_swa_v"][0, :, 1:WIN]).then_inc(s_shift, 16)
        sp.wait_ge(c_id, 6)
        for i, s in enumerate(primed):
            if s in b_mo:
                continue
            sp.dma_start(prime_dram[i], prime[:]).then_inc(s, 16)

        def first(b, s):
            if isinstance(b, int) and b == 0:
                return
            if not (isinstance(b, int) and b < 2):
                sp.wait_ge(n_xn, upto(b - 2))
                sp.dma_start(x_t[s][:], A["x_prompt"][0, ds((b - 1) * P, P), :]).then_inc(e_x[s], 16)

        def second(b, s):
            sp.wait_ge(n_h, upto(b))
            sp.dma_start(h_dram[ds(b, 1)].rearrange("o p n -> p (o n)"), hn[s][:]).then_inc(h_out[s], 16)
            sp.wait_ge(t_hi, upto(b))
            sp.dma_start(hT_dram[ds(b, 1)].rearrange("o p n -> p (o n)"), hTs[s][:]).then_inc(e_hTo[s], 16)

        first(2, 0)
        second(0, 0)
        with sp.Fori(0, 3) as i:
            first(2 * i + 3, 1)
            second(2 * i + 1, 1)
            first(2 * i + 4, 0)
            second(2 * i + 2, 0)
        second(7, 1)
        second(8, 0)
        sp.wait_ge(c_rel, 9)
        sp.dma_start(brow_dram.rearrange("h (p j) -> p h j", p=P), brow[:]).then_inc(c_brow, 16)

        stage0_done(sp)
        for a in range(2):
            sp.dma_start(obuf_dram[(NE + a * NB) * P:(NE + (a + 1) * NB) * P, :],
                         h_dram.rearrange("b p n -> (b p) n")).then_inc(s_fill, 16)
        sp.dma_start(sink[:], A["sinks"][0:1, :].to_broadcast([P, HEADS])).then_inc(b_gn, 16)
        sp.dma_start(gn[:], A["gla_norm_g"][0:1, :].to_broadcast([P, DV])).then_inc(b_gn, 16)
        with sp.Fori(0, G) as g:
            n0 = g * NB

            def hT_load(n, b, s):
                last = n - 1 if isinstance(b, int) else n - 2
                sp.wait_ge(b_p4, upto(last))
                sp.wait_ge(b_hl, upto(last))
                sp.dma_start(hTs[s][:], hT_dram[ds(b, 1)].rearrange("o p n -> p (o n)")).then_inc(b_hT[s], 16)

            wait_apart(sp, b_p5, upto(n0 - 1))
            sp.wait_ge(b_xg, upto(n0 - 1))
            sp.dma_start(gkup[:], A["gk_up"][0][:, ds(g * DK, DK)]).then_inc(b_gk, 16)
            sp.dma_start(gkb[:], A["gk_bias"][0, ds(g * DK, DK)].rearrange("(p o) -> p o", o=1)).then_inc(b_gk, 16)
            hT_load(n0, 0, 0)
            for c, w, src in ((W_KA, HD, g * HD + IN_KA), (W_KA + HD, HD, g * HD + IN_KA), (W_VA, HD, g * HD + IN_VA),
                              (W_Q, DK, g * DK + IN_Q), (W_K, DK, g * DK + IN_K), (W_QA, DV, g * DV + IN_QA)):
                sp.dma_start(wn[:, :, c:c + w], w_in[:, :, ds(src, w)]).then_inc(b_wn, 16)
            for j, c in enumerate((IN_V, IN_R, IN_GA, IN_GB)):
                wait_apart(sp, b_lo, upto(g * WIDE + j - WIDE))
                sp.dma_start(braw[:, j], w_in[:, :, ds(g * DV + c, DV)]).then_inc(w_raw[j], 16)
            wait_apart(sp, b_bs, upto(n0 - 1))
            for h in range(HPG):
                sp.dma_start(bias[:, 0, h], bass.AP(tensor=brow_dram.tensor,
                                                    offset=brow_dram.offset + (g * HPG + h) * (P * LROW) + 127,
                                                    ap=[[LROW - 1, P], [1, 2 * P]])).then_inc(b_bi, 16)
            with sp.Fori(0, 4) as i:
                hT_load(n0 + 2 * i + 1, 2 * i + 1, 1)
                hT_load(n0 + 2 * i + 2, 2 * i + 2, 0)

        stageB_done(sp)
        wout = A["w_out"][0].rearrange("(k p) n -> p k n", p=P)
        for c in range(4):
            if c >= 2:
                sp.wait_ge(b_lo, upto(G * WIDE - 1 + c - 1))
            sp.dma_start(raw[:, 4 + c % 2].rearrange("p (k n) -> p k n", k=2),
                         wout[:, 2 * c:2 * c + 2, :]).then_inc(w_raw[4 + c % 2], 16)
            if c == 1:
                for g in range(G):
                    sp.dma_start(st[:, g], A["state_gla"][0, :, g].rearrange("n k e -> k n e")).then_inc(s_in, 16)
                sp.dma_start(gath[:].rearrange("n g c e -> n (g c e)"),
                             stash_dram.rearrange("n g c e -> n (g c e)")).then_inc(s_in, 16)
                for half in range(2):
                    for c2 in range(2):
                        row = 64 * half + 32 * c2
                        sp.dma_start(sbias[row:row + 32, :],
                                     bass.AP(tensor=brow_dram.tensor,
                                             offset=brow_dram.offset + (2 * c2 + half) * P * LROW + WIN,
                                             ap=[[HPG * P * LROW, G], [0, NS], [1, WIN]])).then_inc(s_in, 16)
                        sp.dma_start(ssink[row:row + 32, :],
                                     bass.AP(tensor=A["sinks"].tensor, offset=A["sinks"].offset + 2 * c2 + half,
                                             ap=[[HPG, G], [0, NS], [1, 1]])).then_inc(s_in, 16)
        sp.wait_ge(s_dve, S_KNEW)
        sp.dma_start(R["swa_k_sample"][0, :, WIN - 1], knew[:]).then_inc(s_new, 16)
        sp.dma_start(R["swa_v_sample"][0, :, WIN - 1], sva[:]).then_inc(s_new, 16)
        sp.wait_ge(s_new, 32)
        sp.wait_ge(s_shift, 32)
        for n in range(NS):
            for d in range(2):
                sp.dma_start(Kd[:, n, :, d], R["swa_k_sample"][0, n]).then_inc(s_win, 16)
        sp.dma_start(Vw[:], R["swa_v_sample"][0].rearrange("n j g d -> j n g d")).then_inc(s_win, 16)
        sp.wait_ge(s_dve, S_STATE[G - 1])
        for g in range(G):
            sp.dma_start(R["gla_state_sample"][0, :, g].rearrange("n k e -> k n e"), st[:, g]).then_inc(s_out, 16)
        sp.wait_ge(s_dve, S_MERGED)
        sp.dma_start(mg_dram[0, 0:NS, :], oS[:].rearrange("n g e -> n (g e)")).then_inc(s_mg, 16)
        sp.wait_ge(s_mg, 16)
        sp.dma_start(ln1_g[:], A["ln1_g"][0:1, :].to_broadcast([P, D])).then_inc(o_small, 16)
        sp.dma_start(ln1_b[:], A["ln1_b"][0:1, :].to_broadcast([P, D])).then_inc(o_small, 16)
        sp.dma_start(wr[:, :, 0:4], A["w_router_group"][0].rearrange("(k p) n -> p k n", p=P)).then_inc(o_small, 16)
        sp.dma_start(wr[:, :, 4:], A["w_router_expert"][0].rearrange("(k p) n -> p k n", p=P)).then_inc(o_small, 16)
        sp.dma_start(br[:, 0:4], A["b_router_group"][0:1, :].to_broadcast([P, 4])).then_inc(o_small, 16)
        sp.dma_start(br[:, 4:], A["b_router_expert"][0:1, :].to_broadcast([P, NE])).then_inc(o_small, 16)

        def o_first(b, s):
            if not (isinstance(b, int) and b < 2):
                sp.wait_ge(u_T, upto(b - 2))
                sp.wait_ge(h_out[s], stored(1, s, use(b, s)))
            sp.dma_start(mg[s][:], mg_dram[ds(b, 1)].rearrange("o p n -> p (o n)")).then_inc(h_in[s], 16)
            sp.dma_start(hh[s][:], h_dram[ds(b, 1)].rearrange("o p n -> p (o n)")).then_inc(h_in[s], 16)

        def o_second(b, s):
            sp.wait_ge(n_h, upto(NB + b))
            sp.dma_start(h1_dram[ds(b * P, P), :], hh[s][:]).then_inc(h_out[s], 16)

        def m_load(t, e, j):
            src = A[("w_gate", "w_up", "w_down")[j // 2]][0]
            kc, half = (KC, j % 2) if j < 4 else (DE // P, j % 2)
            v = src[ds(e, 1)].rearrange("o (k p) n -> p (o k) n", p=P)
            v = v[:, half * kc // 2:(half + 1) * kc // 2, :]
            sp.dma_start(raw[:, j].rearrange("p (k n) -> p k n", k=kc // 2), v).then_inc(w_raw[j], 16)

        o_first(0, 0)
        with sp.Fori(0, 4) as i:
            o_first(2 * i + 1, 1)
            o_second(2 * i, 0)
            o_first(2 * i + 2, 0)
            o_second(2 * i + 1, 1)
        sp.wait_ge(s_out, 16 * G)
        for j in range(4):
            m_load(0, 0, j)
        o_second(8, 0)

        sp.wait_ge(d_route, 1)
        iters = 15 + (sp.value_load(novr[0:1, 0:1], min_val=0, max_val=16) + 1) // 2

        def m_step(t):
            e = sp.value_load(etab[0:1, ds(t, 1)], min_val=0, max_val=NE - 1)
            for j in range(4):
                sp.wait_ge(*piece_lo(t - 1, j))
                m_load(t, e, j)
            m_down(t - 1)

        def m_down(t):
            e = sp.value_load(etab[0:1, ds(t, 1)], min_val=0, max_val=NE - 1)
            for j in (4, 5):
                sp.wait_ge(*piece_lo(t - 1, j))
                m_load(t, e, j)

        with sp.Fori(0, iters) as i:
            m_step(2 * i + 1)
            m_step(2 * i + 2)
        m_step(2 * iters + 1)
        m_down(2 * iters + 1)

        sp.wait_ge(m_yd, upto(2 * iters + 1))
        sp.wait_ge(m_yo[0], 16 * (iters + 2))
        sp.wait_ge(m_yo[1], 16 * (iters + 2))
        sp.dma_start(ln2_g[:], A["ln2_g"][0:1, :].to_broadcast([P, D])).then_inc(f_small, 16)
        sp.dma_start(ln2_b[:], A["ln2_b"][0:1, :].to_broadcast([P, D])).then_inc(f_small, 16)

        def f_first(b, s):
            if not (isinstance(b, int) and b < 2):
                sp.wait_ge(f_z, upto(b - 2))
            sp.dma_start(h1l[s][:], h1_dram[ds(b * P, P), :]).then_inc(h_in[s], 16)

        def f_second(b, s):
            sp.wait_ge(n_h, upto(2 * NB + b))
            if isinstance(b, int) and b == 0:
                sp.dma_start(R["y_sample"].rearrange("n o d -> (n o) d"), zz[0][0:NS, :]).then_inc(h_out[0], 16)
            else:
                sp.dma_start(R["y_prompt"][0, ds((b - 1) * P, P), :], zz[s][:]).then_inc(h_out[s], 16)

        f_first(0, 0)
        f_first(1, 1)
        f_second(0, 0)
        with sp.Fori(0, 3) as i:
            f_first(2 * i + 2, 0)
            f_second(2 * i + 1, 1)
            f_first(2 * i + 3, 1)
            f_second(2 * i + 2, 0)
        f_first(8, 0)
        f_second(7, 1)
        f_second(8, 0)
        for s in range(2):
            sp.wait_ge(h_out[s], stored(2, s, 5 - s))
        sp.wait_ge(s_out, 16 * G)
        sp.wait_ge(b_gout, 16 * 3 * G)

    @block.gpsimd
    def _(pool):
        for s in step_sems:
            pool.sem_inc(s, CREDIT)
        pool.memset(ones[:], 1.0).then_inc(c_id, 1)
        pool.memset(prime[:], 0.0).then_inc(c_id, 1)
        pool.memset(eps_c[:], EPS).then_inc(c_id, 1)
        pool.wait_ge(c_id, 3)
        pool.affine_select(out=ident[:], in_=ones[:], compare_op=ALU.is_equal, fill=0.0, base=0,
                           pattern=[[1, P]], channel_multiplier=-1).then_inc(c_id, 1)
        pool.affine_select(out=causal[:], in_=ones[:], compare_op=ALU.is_ge, fill=0.0, base=0,
                           pattern=[[1, P]], channel_multiplier=-1).then_inc(c_id, 1)
        pool.affine_select(out=strict[:], in_=ones[:], compare_op=ALU.is_gt, fill=0.0, base=0,
                           pattern=[[1, P]], channel_multiplier=-1).then_inc(c_id, 1)
        pool.wait_ge(c_id, 6)
        for s in range(2):
            pool.dma_start(prime_dram[14 + s], prime[:]).then_inc(b_mo[s], 16)
        pool.memset(brow[:], NEG).then_inc(c_id, 1)
        pool.wait_ge(c_in, 80)

        def first(b, s):
            pool.wait_ge(n_hg, upto(b))
            pool.tensor_tensor(hn[s][:], hn[s][:], lne_b[:], ALU.add).then_inc(n_h, 1)

        pipelined(pool, first, lambda b, s: None)

        stage0_done(pool)
        pool.wait_ge(b_gn, 32)

        with pool.Fori(0, G) as g:
            pool.wait_ge(b_bi, 16 * HPG * (g + 1))
            wait_apart(pool, b_bs, upto(g * NB - 1))
            pool.tensor_copy(bias[:, 1], bias[:, 0]).then_inc(b_stg, 1)
            wait_apart(pool, b_stg, 2 * g + 1)
            pool.memset(bias[:, 1, :, 0:PAD0], NEG).then_inc(b_bv, 1)

            def step(n, s, uses, first):
                pool.wait_ge(b_rr, upto(n))
                if first:
                    pool.wait_ge(b_rg, upto(n - 1))
                pool.tensor_tensor(rr[:], rr[:], gn[:], ALU.mult).then_inc(b_rg, 1)
                if first:
                    wait_apart(pool, b_rg, upto(n))
                    pool.wait_ge(b_ka, upto(n))
                    pool.wait_ge(b_qa, upto(n))
                    pool.wait_ge(b_vrc, upto(n))
                    pool.tensor_copy(asq[:, ds(g, 1)].rearrange("p o c n -> p (o c) n"), qa[:, :, 0:NS])
                    pool.tensor_copy(ska[:, ds(g, 1)].rearrange("p o n -> p (o n)"), ka[0][:, 0:NS])
                    pool.tensor_copy(sva[:, ds(g, 1)].rearrange("p o n -> p (o n)"), va[0][0:NS, :]).then_inc(b_stg, 1)
                    for j, t in enumerate((vr[0:NS, 0:DV], rr[0:NS, :], Rt[0:NS, 1, :])):
                        pool.dma_start(stash_dram[:, ds(g, 1), j].rearrange("n o e -> n (o e)"), t).then_inc(b_std, 16)
                    pool.wait_ge(b_std, 48 * (g + 1))
                    pool.wait_ge(b_stg, 2 * g + 2)
                    pool.sem_inc(b_sta, 1)
                pool.wait_ge(b_oa, upto(n))
                pool.tensor_tensor(oa[:], oa[:], Rt[:, 1], ALU.mult).then_inc(b_ob, 1)
                pool.wait_ge(b_ob, upto(n))
                pool.wait_ge(b_mo[s], 16 * (1 + uses))
                pool.tensor_tensor(mgo[s][:], yg[:], oa[:], ALU.add).then_inc(b_mg, 1)
                wait_apart(pool, b_mg, upto(n))

            step(g * NB, 0, 5 * g, True)
            pool.dma_start(mg_dram[0, :, ds(g * DV, DV)], mgo[0][:]).then_inc(b_mo[0], 16)
            with pool.Fori(0, 4) as i:
                for s in (1, 0):
                    b = 2 * i + 1 + (1 - s)
                    step(g * NB + b, s, 4 * g + i if s else 5 * g + i + 1, False)
                    pool.dma_start(mg_dram[ds(b, 1), :, ds(g * DV, DV)].rearrange("o p n -> p (o n)"),
                                   mgo[s][:]).then_inc(b_mo[s], 16)
            wait_apart(pool, b_fin, upto(g))
            pool.dma_start(R["gla_state_prompt"][0, 0, ds(g, 1)].rearrange("o k e -> k (o e)"), Sm[:]).then_inc(b_gout, 16)
            wait_apart(pool, b_ko, upto(g))
            pool.dma_start(R["swa_k_prompt"][0, 0, :, ds(g, 1), :].rearrange("j o d -> j (o d)"), kout[:]).then_inc(b_gout, 16)
            pool.dma_start(R["swa_v_prompt"][0, 0, :, ds(g, 1), :].rearrange("j o d -> j (o d)"), va[0][:]).then_inc(b_gout, 16)
            pool.wait_ge(b_gout, 48 * (g + 1))
            pool.sem_inc(b_gfree, 1)

        stageB_done(pool)
        pool.memset(qm[:], 0.0).then_inc(s_qm, 1)
        pool.wait_ge(o_small, 96)

        def o_first(b, s):
            pool.wait_ge(n_hg, upto(NB + b))
            pool.tensor_tensor(hh[s][:], hh[s][:], ln1_b[:], ALU.add).then_inc(n_h, 1)

        pipelined(pool, o_first, lambda b, s: None)

        pool.wait_ge(o_lg, upto(8))
        pool.iota(ioti[:, 0:P], [[1, P]], base=0, channel_multiplier=0).then_inc(pool_s, 1)
        pool.iota(ioti[:, P:P + 1], [[0, 1]], base=0, channel_multiplier=1).then_inc(pool_s, 1)
        pool.iota(toki[:], [[P, NB]], base=0, channel_multiplier=1).then_inc(pool_s, 1)
        pool.iota(etab[:, 0:NE], [[1, NE]], base=0, channel_multiplier=0).then_inc(pool_s, 1)

        pool.wait_ge(d_route, 1)
        for s in range(2):
            pool.wait_ge(h_out[s], stored(1, s, 5 - s))
        iters = 15 + (pool.value_load(novr[0:1, 0:1], min_val=0, max_val=16) + 1) // 2

        def gather(t, s, free):
            if free:
                pool.wait_ge(t_T, upto(2 * NB + t - 2))
            wait_apart(pool, m_xi, upto(t - 1))
            pool.tensor_copy(xi[s][:], idx_all[:, ds(t, 1)]).then_inc(m_xi, 1)
            wait_apart(pool, m_xi, upto(t))
            pool.indirect_dma_start(out=xw[s][:], out_offset=None, in_=h1_dram,
                                    in_offset=bass.IndirectOffsetOnAxis(ap=xi[s][:, 0:1], axis=0)).then_inc(m_x[s], 16)

        def low(t, j):
            pool.wait_ge(*piece_hi(t, j))
            pool.tensor_tensor(wm_lo[:, j], raw[:, j], BF(wm_hi[:, j]), ALU.subtract).then_inc(m_loP[j // 4], 1)

        gather(0, 0, False)
        gather(1, 1, False)
        low(0, 1)
        low(1, 1)
        gather(2, 0, True)
        low(0, 5)
        with pool.Fori(0, iters) as i:
            for s in (1, 0):
                t = 2 * i + 1 + (1 - s)
                low(t + 1, 1)
                gather(t + 2, s, True)
                low(t, 5)
        low(2 * iters + 1, 5)

        last = 2 * iters + 1
        pool.wait_ge(m_yd, upto(last))
        wait_apart(pool, m_yo[0], 16 * (iters + 2))
        pool.wait_ge(m_yo[1], 16 * (iters + 2))
        pool.wait_ge(f_small, 32)
        pool.wait_ge(m_x[0], 16 * (iters + 2))

        def f_first(b, s):
            wait_apart(pool, f_b, upto(b - 2))
            for c in range(2):
                pool.tensor_copy(fi[s][:, c:c + 1], ridx[:, ds(b + c * NB, 1)]).then_inc(f_i, 1)
            wait_apart(pool, f_i, upto(2 * b + 1))
            for c, t in enumerate((ya[s], yc[s])):
                pool.indirect_dma_start(out=t[:], out_offset=None, in_=obuf_dram,
                                        in_offset=bass.IndirectOffsetOnAxis(ap=fi[s][:, c:c + 1], axis=0)).then_inc(f_y[s], 16)

        def f_second(b, s):
            pool.wait_ge(n_hg, upto(2 * NB + b))
            pool.tensor_tensor(zz[s][:], zz[s][:], ln2_b[:], ALU.add).then_inc(n_h, 1)

        pipelined(pool, f_first, f_second)

    @block.scalar
    def _(act):
        def rsqrt(src, tmp, dst, s_a, s_b, n, scale=1.0):
            act.activation(tmp, src, ACT.Ln, bias=eps_c[0:src.shape[0], :], scale=scale).then_inc(s_a, 1)
            act.wait_ge(s_a, n)
            act.activation(dst, tmp, ACT.Exp, scale=-0.5).then_inc(s_b, 1)

        act.preload_act_table_set("natural_log_exp_and_others")
        act.wait_ge(c_id, 6)
        act.wait_ge(c_in, 80)

        def first(b, s):
            act.wait_ge(n_st, upto(b))
            rsqrt(st0[s][:, 13:14], st0[s][:, 14:15], st0[s][:, 15:16], n_ln, n_rs, upto(b))
            act.wait_ge(n_nm, upto(b))
            act.wait_ge(n_rs, upto(b))
            act.wait_ge(t_T, upto(b - 2))
            act.wait_ge(h_out[s], stored(0, s, use(b, s)))
            act.activation(hn[s][:], x_t[s][:], ACT.Identity, bias=st0[s][:, 14:15], scale=st0[s][:, 15:16]).then_inc(n_xn, 1)

        def second(b, s):
            act.wait_ge(t_T, upto(b))
            act.wait_ge(e_hTo[s], 16 * (1 + use(b, s)))
            act.wait_ge(e_lr, upto(b - 2))
            act.copy(hTs[s][:], PS[:, 0:2].rearrange("p a n -> p (a n)")).then_inc(t_hi, 1)
            act.wait_ge(e_lr, upto(b))
            act.wait_ge(e_lrT, upto(b - 1))
            act.copy(lr_t[:], PS[:, 2, 0:RANK]).then_inc(e_lrc, 1)
            act.wait_ge(e_lrT, upto(b))
            act.copy(lrT[:, ds(b * P, P)], PS[0:RANK, 3, 0:P]).then_inc(e_lrd, 1)

        pipelined(act, first, second)

        stage0_done(act)
        act.wait_ge(b_gn, 32)
        with act.Fori(0, G) as g:
            n0 = g * NB

            def wide(j):
                act.wait_ge(w_raw[j], 16 * (g + 1))
                if j < 2:
                    act.wait_ge(b_vr, upto(n0 - 1))
                else:
                    act.wait_ge(b_gg, upto(n0 - 1))
                act.copy(w_hi[:, :, j * DV:(j + 1) * DV], braw[:, j]).then_inc(b_hi, 1)

            def step(n, s, uses, first):
                if first:
                    act.wait_ge(b_gk, 32 * (g + 1))
                    wide(0)
                    wide(1)
                act.wait_ge(b_gg, upto(n - 1))
                act.wait_ge(b_hT[s], 16 * (uses + 1))
                act.copy(hT_hl[:, 0], hTs[s][:]).then_inc(b_hs, 1)
                act.wait_ge(b_p5, upto(n))
                act.wait_ge(b_mn, upto(n - 1))
                if first:
                    act.wait_ge(b_gfree, upto(g - 1))
                else:
                    act.wait_ge(b_sta, upto(g))
                act.wait_ge(b_o, upto(n - 1))
                act.activation(xg[:], PS[:, 5, P:2 * P], ACT.Identity, bias=gkb[:, 0:1]).then_inc(b_xg, 1)
                act.copy(ka[s][:], PS[:, 5, 0:P])
                act.copy(va[s][:], PS[:, 5, 2 * P:2 * P + HD]).then_inc(b_ka, 1)
                act.wait_ge(b_xg, upto(n))
                act.wait_ge(b_g16, upto(n - 1))
                act.activation(ax[:], xg[:], ACT.Abs).then_inc(b_ax, 1)
                act.wait_ge(b_ax, upto(n))
                act.activation(ax[:], ax[:], ACT.Exp, scale=-1.0).then_inc(b_ex, 1)
                act.wait_ge(b_ex, upto(n))
                act.activation(ax[:], ax[:], ACT.Ln, bias=1.0).then_inc(b_lx, 1)
                act.wait_ge(b_bmn, upto(n))
                act.wait_ge(b_qq, upto(n - 1))
                act.wait_ge(b_Sm, upto(n - 1))
                act.wait_ge(b_e2, upto(n - 1))
                if first:
                    act.activation(gse[:, ds(g, 1)].rearrange("p o n -> p (o n)"), g16[:, 0:NS], ACT.Exp, scale=1.0 / TAU)
                act.activation(ek[:], b16[:], ACT.Exp, bias=bm[:, 0:1], scale=-1.0 / TAU)
                act.activation(ebm[:], bm[:, 0:1], ACT.Exp)
                act.activation(eq[:], b16[:], ACT.Exp, bias=bm[:, 1:2], scale=1.0 / TAU).then_inc(b_eq, 1)
                if first:
                    wide(2)
                    wide(3)
                act.wait_ge(b_vr, upto(n))
                act.wait_ge(b_rr, upto(n - 1))
                act.copy(vr[:], PS[:, 2]).then_inc(b_vrc, 1)
                act.wait_ge(b_vrc, upto(n))
                act.wait_ge(b_E2, upto(n - 1))
                act.activation(Et[:, 0], vr[:, DV:2 * DV], ACT.Exp, scale=-1.0).then_inc(b_er, 1)
                act.wait_ge(b_nmx, upto(n))
                act.wait_ge(b_den, upto(n - 1))
                lo = P if first else 0
                for h in range(HPG):
                    act.activation(Sc[:, h, lo:], Sc[:, h, lo:], ACT.Exp, bias=nmx[:, h:h + 1], accum_out=su[:, h:h + 1])
                act.activation(es[:], sk[:], ACT.Exp).then_inc(b_P, 1)
                act.wait_ge(b_gg, upto(n))
                act.wait_ge(b_R, upto(n - 1))
                act.activation(Et[:, 1:3].rearrange("p a n -> p (a n)"), PS[:, 3], ACT.Exp, scale=-1.0).then_inc(b_eg, 1)
                act.wait_ge(b_pt, upto(n))
                if first:
                    act.sem_inc(b_pc, 1)
                else:
                    act.copy(Pt[:, 0].rearrange("p h q -> p (h q)"), PS[:, 0]).then_inc(b_pc, 1)
                act.wait_ge(b_o, upto(n))
                act.wait_ge(b_E2, upto(n))
                act.activation(Et[:, 0], PS[:, 7, 0:DV], ACT.Square, accum_out=ssq[:]).then_inc(b_sq, 1)
                act.wait_ge(b_sq, upto(n))
                act.wait_ge(b_yg, upto(n - 1))
                rsqrt(ssq[:], lnv[:], rstd[:], b_lv, b_rs, upto(n), scale=1.0 / DV)

            step(n0, 0, 5 * g, True)
            with act.Fori(0, 4) as i:
                step(n0 + 2 * i + 1, 1, 4 * g + i, False)
                step(n0 + 2 * i + 2, 0, 5 * g + i + 1, False)

        stageB_done(act)
        for c in range(4):
            act.wait_ge(w_raw[4 + c % 2], 16 * (c // 2 + 1))
            act.copy(wo_hi[:, 2 * c:2 * c + 2].rearrange("p k n -> p (k n)"), raw[:, 4 + c % 2]).then_inc(b_hi, 1)

        for a in range(8):
            act.wait_ge(s_pe, S_KT + a)
            act.copy(KT[:].rearrange("p g n k -> p (g n k)")[:, a * 512:(a + 1) * 512], PS[:, 6 + a % 2]).then_inc(act_s, 1)
        act.wait_ge(s_dve, S_NMX)
        act.activation(sS2[:], sS2[:], ACT.Exp, bias=sm8[:, 1:2], accum_out=sm8[:, 3:4]).then_inc(act_s, 1)
        act.activation(sm8[:, 4:5], sm8[:, 2:3], ACT.Exp).then_inc(act_s, 1)
        act.wait_ge(s_dve, S_SSQ)
        act.activation(s8[:, 1], s8[:, 0], ACT.Ln, bias=eps_c[0:NS, :], scale=1.0 / DV).then_inc(act_s, 1)
        act.wait_ge(act_s, 11)
        act.activation(s8[:, 2], s8[:, 1], ACT.Exp, scale=-0.5).then_inc(act_s, 1)

        act.wait_ge(s_dve, S_MERGED)

        def o_first(b, s):
            act.wait_ge(t_T, upto(NB + b))
            act.wait_ge(o_z, upto(b - 1))
            act.copy(mT_hi[:], PS[:, 0:2].rearrange("p a n -> p (a n)")).then_inc(t_hi, 1)
            act.wait_ge(n_st, upto(NB + b))
            rsqrt(st1[s][:, 13:14], st1[s][:, 14:15], st1[s][:, 15:16], n_ln, n_rs, upto(NB + b))
            act.wait_ge(n_nm, upto(NB + b))
            act.activation(hh[s][:], hh[s][:], ACT.Identity, bias=st1[s][:, 14:15], scale=st1[s][:, 15:16]).then_inc(n_xn, 1)

        def o_second(b, s):
            act.wait_ge(u_T, upto(b))
            act.wait_ge(o_rl, upto(b - 1))
            act.copy(h1T[:], PS[:, 4:6].rearrange("p a n -> p (a n)")).then_inc(u_c, 1)

        pipelined(act, o_first, o_second)

        act.wait_ge(d_g, 1)
        act.activation(gq[0][:], gq[0][:], ACT.Exp).then_inc(act_s, 1)
        act.wait_ge(d_g, 2)
        act.activation(rt["e"][:], rt["d"][:], ACT.Exp).then_inc(act_s, 1)

        act.wait_ge(d_route, 1)
        act.wait_ge(s_fill, 32)
        iters = 15 + (act.value_load(novr[0:1, 0:1], min_val=0, max_val=16) + 1) // 2

        def high(t, j):
            act.wait_ge(w_raw[j], 16 * (RAW_BASE[j] + t + 1))
            act.wait_ge(*piece_used(t - 1, j))
            act.wait_ge(*piece_lo(t - 1, j))
            act.copy(wm_hi[:, j], raw[:, j]).then_inc(m_hi[j // 4], 1)

        def x_high(t):
            act.wait_ge(t_T, upto(2 * NB + t))
            act.wait_ge(*piece_used(t - 1, 3))
            act.copy(xT_hi[:], PS[:, 0:2].rearrange("p a n -> p (a n)")).then_inc(t_hi, 1)

        def m_step(t, s, uses, prev, more):
            if more:
                high(t + 1, 0)
            act.wait_ge(*piece_used(t, 1))
            act.wait_ge(m_hm, upto(t - 1))
            act.activation(sg_t[:], PS[:, 2], ACT.Silu).then_inc(m_sg, 1)
            if more:
                high(t + 1, 1)
                high(t + 1, 2)
                x_high(t + 1)
                high(t + 1, 3)
            high(t, 4)
            high(t, 5)
            act.wait_ge(u_T, upto(NB + t))
            act.copy(hT_hi[:], PS[:, 4]).then_inc(u_c, 1)
            if prev:
                y_out(t - 1, 1 - s, uses)

        def y_out(t, s, uses):
            act.wait_ge(*piece_used(t, 5))
            act.wait_ge(m_yo[s], 16 * (1 + uses))
            act.copy(yb[s][:, 0:512], PS[:, 5]).then_inc(m_ya, 1)
            act.wait_ge(m_ya, upto(t))
            act.wait_ge(m_yd, upto(t))
            act.dma_start(obuf_dram[ds(t * P, P), :], yb[s][:]).then_inc(m_yo[s], 16)

        for j in range(4):
            high(0, j)
        x_high(0)
        m_step(0, 0, 0, False, True)
        with act.Fori(0, iters) as i:
            m_step(2 * i + 1, 1, i, True, True)
            m_step(2 * i + 2, 0, i, True, True)
        m_step(2 * iters + 1, 1, iters, True, False)
        y_out(2 * iters + 1, 1, iters)

        act.preload_act_table_set("natural_log_exp_and_others")
        act.wait_ge(m_yo[0], 16 * (iters + 2))
        act.wait_ge(m_yo[1], 16 * (iters + 2))

        def f_first(b, s):
            act.wait_ge(f_w, upto(b))
            act.wait_ge(f_y[s], 32 * (use(b, s) + 1))
            act.activation(ya[s][:], ya[s][:], ACT.Copy, scale=fw[s][:, 0:1]).then_inc(f_a, 1)
            act.wait_ge(n_st, upto(2 * NB + b))
            rsqrt(st2[s][:, 13:14], st2[s][:, 14:15], st2[s][:, 15:16], n_ln, n_rs, upto(2 * NB + b))
            act.wait_ge(n_nm, upto(2 * NB + b))
            act.activation(zz[s][:], zz[s][:], ACT.Identity, bias=st2[s][:, 14:15], scale=st2[s][:, 15:16]).then_inc(n_xn, 1)

        pipelined(act, f_first, lambda b, s: None)

    @block.vector
    def _(dve):
        count = [0]

        def link(ins):
            count[0] += 1
            ins.then_inc(dve_s, 1)
            dve.wait_ge(dve_s, count[0])

        dve.memset(x_t[0][:], 0.0).then_inc(c_z0, 1)
        dve.wait_ge(c_in, 80)
        dve.tensor_copy(relw[:], relb[:].rearrange("p (h o) -> p h o", o=1).to_broadcast([32, HEADS, P])).then_inc(c_rel, 1)
        dve.wait_ge(c_id, 7)
        for a in range(4):
            dve.wait_ge(c_rel, 2 + 2 * a)
            dve.tensor_copy(brow[:, 4 * a:4 * a + 4, WIN:2 * WIN],
                            PS[:, 4].rearrange("p (h n) -> p h n", h=4)).then_inc(c_rel, 1)

        def first(b, s):
            if isinstance(b, int) and b == 0:
                dve.wait_ge(e_x[0], 32)
            else:
                dve.wait_ge(e_x[s], 16 * (2 - s + use(b, s)))
            dve.wait_ge(n_xn, upto(b - 2))
            stats(dve, x_t[s], st0[s], n_sa, n_st, upto(b))
            dve.wait_ge(n_rs, upto(b))
            dve.scalar_tensor_tensor(st0[s][:, 14:15], st0[s][:, 12:13], -1.0, st0[s][:, 15:16],
                                     ALU.mult, ALU.mult).then_inc(n_nm, 1)
            dve.wait_ge(n_xn, upto(b))
            dve.tensor_tensor(hn[s][:], hn[s][:], lne_g[:], ALU.mult).then_inc(n_hg, 1)

        pipelined(dve, first, lambda b, s: None)

        stage0_done(dve)
        dve.wait_ge(b_gn, 32)
        with dve.Fori(0, G) as g:
            n0 = g * NB

            def wide(j):
                dve.wait_ge(b_hi, upto(g * WIDE + j))
                c = slice(j * DV, (j + 1) * DV)
                dve.tensor_tensor(w_lo[:, :, c], braw[:, j], BF(w_hi[:, :, c]), ALU.subtract).then_inc(b_lo, 1)

            def step(n, s, first, variant):
                lo = P if first else 0
                if first:
                    wide(0)
                    wide(1)
                dve.wait_ge(b_hs, upto(n))
                dve.tensor_tensor(hT_hl[:, 1], hTs[s][:], BF(hT_hl[:, 0]), ALU.subtract).then_inc(b_hl, 1)
                dve.wait_ge(b_xg, upto(n))
                dve.wait_ge(b_g16, upto(n - 1))
                dve.tensor_scalar(mn[:], xg[:], 0.0, None, ALU.min).then_inc(b_mn, 1)
                dve.wait_ge(b_mn, upto(n))
                dve.wait_ge(b_lx, upto(n))
                dve.wait_ge(b_eq, upto(n - 1))
                dve.tensor_tensor(g16[:], mn[:], ax[:], ALU.subtract).then_inc(b_g16, 1)
                dve.wait_ge(b_g16, upto(n))
                dve.tensor_tensor_scan(b16[:], ones[:], g16[:], 0.0, ALU.mult, ALU.add).then_inc(b_b16, 1)
                dve.wait_ge(b_b16, upto(n))
                dve.tensor_scalar(bm[:, 0:1], b16[:, P // 2 - 1:P // 2], 1.0 / TAU, None, ALU.mult)
                dve.tensor_scalar(bm[:, 1:2], b16[:, P // 2 - 1:P // 2], -1.0 / TAU, None, ALU.mult).then_inc(b_bmn, 1)
                dve.wait_ge(b_p4, upto(n))
                dve.wait_ge(b_sc, upto(n - 1))
                if not first:
                    dve.wait_ge(b_sta, upto(g))
                dve.tensor_copy(qa[:].rearrange("p c n -> p (c n)"), PS[:, 4, 2 * P:4 * P]).then_inc(b_qa, 1)
                if first:
                    dve.tensor_scalar(gsq[:, ds(g, 1)].rearrange("p o n -> p (o n)"), PS[:, 4, 0:NS],
                                      DK ** -0.5, None, ALU.mult)
                    dve.tensor_copy(gsk[:, ds(g, 1)].rearrange("p o n -> p (o n)"), PS[:, 4, P:P + NS])
                dve.wait_ge(b_eq, upto(n))
                dve.wait_ge(b_o, upto(n - 1))
                dve.tensor_tensor(kk[:], PS[:, 4, P:2 * P], ek[:], ALU.mult).then_inc(b_kk, 1)
                if first:
                    dve.wait_ge(b_kk, upto(n))
                    dve.memset(kk[:, 0:PAD0], 0.0)
                dve.scalar_tensor_tensor(qq[:], PS[:, 4, 0:P], DK ** -0.5, eq[:], ALU.mult, ALU.mult).then_inc(b_qq, 1)
                if first:
                    wide(2)
                    wide(3)
                if first:
                    dve.wait_ge(b_gfree, upto(g - 1))
                    dve.memset(Sm[:], 0.0).then_inc(b_Sm, 1)
                else:
                    dve.wait_ge(b_T, upto(n - 1))
                    dve.tensor_scalar(Sm[:], Tn[:], e2[:, 0:1], ebm[:, 0:1], ALU.mult, ALU.mult).then_inc(b_Sm, 1)
                    dve.wait_ge(b_Sm, upto(n))
                dve.tensor_copy(e2[:], eq[:, P - 1:P]).then_inc(b_e2, 1)
                wait_apart(dve, b_sc, upto(n))
                dve.wait_ge(b_pt, upto(n - 1))
                dve.wait_ge(b_bv, upto(g))
                for half in range(2):
                    dst = Sc[:].rearrange("p (c f) k -> p c f k", f=2)[:, :, half, lo:]
                    if isinstance(variant, int):
                        bs = bias[:, variant].rearrange("p (c f) k -> p c f k", f=2)[:, :, half, lo:]
                    else:
                        bs = bias[:, ds(variant, 1)].rearrange("p o (c f) k -> p (o c) f k", f=2)[:, :, half, lo:]
                    last = dve.scalar_tensor_tensor(dst, PS[:, half].rearrange("p (c k) -> p c k", c=2)[:, :, lo:],
                                                    HD ** -0.5, bs, ALU.mult, ALU.add)
                last.then_inc(b_bs, 1)
                dve.wait_ge(b_bs, upto(n))
                if first:
                    dve.memset(Sc[:, :, P:P + PAD0], NEG).then_inc(b_sz, 1)
                    dve.wait_ge(b_sz, g + 1)
                dve.wait_ge(b_P, upto(n - 1))
                dve.reduce_max(mx[:], Sc[:, :, lo:], X).then_inc(b_mx, 1)
                dve.wait_ge(b_mx, upto(n))
                dve.tensor_tensor(mx[:], mx[:], sink[:, ds(g * HPG, HPG)], ALU.max).then_inc(b_mx2, 1)
                dve.wait_ge(b_mx2, upto(n))
                dve.tensor_tensor(sk[:], sink[:, ds(g * HPG, HPG)], mx[:], ALU.subtract)
                dve.tensor_scalar(nmx[:], mx[:], -1.0, None, ALU.mult).then_inc(b_nmx, 1)
                dve.wait_ge(b_A, upto(n))
                dve.tensor_tensor(At[:], PS[:, 6, 0:P], causal[:], ALU.mult)
                dve.tensor_copy(kd[:], PS[:, 6, P:2 * P]).then_inc(b_At, 1)
                dve.wait_ge(b_pt, upto(n))
                dve.tensor_copy(Pt[:, 1].rearrange("p h q -> p (h q)"), PS[:, 1]).then_inc(b_pd, 1)
                dve.wait_ge(b_up, upto(n))
                dve.tensor_tensor(Tn[:], PS[:, 6, DV:2 * DV], Sm[:], ALU.add).then_inc(b_T, 1)
                dve.wait_ge(b_eg, upto(n))
                dve.tensor_scalar(Et[:, 1:3], Et[:, 1:3], 1.0, None, ALU.add).then_inc(b_E1, 1)
                dve.wait_ge(b_E1, upto(n))
                dve.scalar_tensor_tensor(Et[:, 1], Et[:, 0], 1.0, Et[:, 1], ALU.add, ALU.mult).then_inc(b_E2, 1)
                dve.wait_ge(b_E2, upto(n))
                dve.wait_ge(b_ob, upto(n - 1))
                if not first:
                    dve.wait_ge(b_sta, upto(g))
                dve.reciprocal(Rt[:], Et[:, 1:3]).then_inc(b_R, 1)
                dve.wait_ge(b_R, upto(n))
                dve.tensor_tensor(rr[:], vr[:, DV:2 * DV], Rt[:, 0], ALU.mult).then_inc(b_rr, 1)
                dve.wait_ge(b_P, upto(n))
                dve.tensor_tensor(su[:], su[:], es[:], ALU.add).then_inc(b_den, 1)
                dve.wait_ge(b_den, upto(n))
                dve.reciprocal(rden[:], su[:]).then_inc(b_rden, 1)
                dve.wait_ge(b_rs, upto(n))
                dve.wait_ge(b_rg, upto(n))
                dve.wait_ge(b_mg, upto(n - 1))
                dve.scalar_tensor_tensor(yg[:], PS[:, 7, 0:DV], rstd[:, 0:1], rr[:], ALU.mult, ALU.mult).then_inc(b_yg, 1)
                dve.wait_ge(b_rden, upto(n))
                dve.tensor_tensor(oa[:].rearrange("p (h d) -> p h d", h=HPG),
                                  PS[:, 7, DV:2 * DV].rearrange("p (h d) -> p h d", h=HPG),
                                  rden[:].rearrange("p (h o) -> p h o", o=1).to_broadcast([P, HPG, HD]),
                                  ALU.mult).then_inc(b_oa, 1)

            step(n0, 0, True, 0)
            with dve.Fori(0, 4) as i:
                step(n0 + 2 * i + 1, 1, False, (3 - i) // 3)
                step(n0 + 2 * i + 2, 0, False, 0)
            dve.wait_ge(b_T, upto(n0 + 8))
            dve.wait_ge(b_o, upto(n0 + 8))
            dve.wait_ge(b_e2, upto(n0 + 8))
            dve.tensor_scalar(Sm[:], Tn[:], e2[:, 0:1], None, ALU.mult).then_inc(b_fin, 1)
            dve.wait_ge(b_kT, upto(g))
            dve.tensor_copy(kout[:], PS[:, 4, 0:HD]).then_inc(b_ko, 1)

        stageB_done(dve)
        for c in range(4):
            dve.wait_ge(b_hi, upto(G * WIDE - 1 + c + 1))
            dve.tensor_tensor(wo_lo[:, 2 * c:2 * c + 2].rearrange("p k n -> p (k n)"), raw[:, 4 + c % 2],
                              BF(wo_hi[:, 2 * c:2 * c + 2].rearrange("p k n -> p (k n)")), ALU.subtract).then_inc(b_lo, 1)

        def mark(ins, s):
            ins.then_inc(s, 1)

        dve.wait_ge(s_pe, S_KT8)
        link(dve.tensor_copy(kt8[:].rearrange("n g k -> n (g k)"), PS[0:NS, 0]))
        mark(dve.tensor_copy(knew[:].rearrange("n g d -> n (g d)"), PS[0:NS, 1, 0:G * HD]), s_dve)
        dve.wait_ge(s_qm, 1)
        for g in range(G):
            last = dve.tensor_copy(qm[:].rearrange("p g n m -> p g (n m)")[:, g, 0:NS * NS:NS + 1], gsq[:, g])
        mark(last, s_qm)
        dve.wait_ge(s_in, 16 * 13)

        def key_masks(g):
            if g >= 2:
                dve.wait_ge(s_pe, S_OUTER[g - 2])
            mark(dve.tensor_tensor(km[g % 2][:], kt8[:, g:g + 1, :].to_broadcast([NS, NS, P]),
                                   ident[0:NS, 0:NS].rearrange("t (n o) -> t n o", o=1).to_broadcast([NS, NS, P]),
                                   ALU.mult), s_dve)

        key_masks(0)
        key_masks(1)
        for g in range(G):
            dve.wait_ge(s_pe, S_OUTER[g])
            for n in range(NS):
                last = dve.scalar_tensor_tensor(st[:, g, n], st[:, g, n], gse[:, g, n:n + 1],
                                                PS[:, 2 + n // 2, (n % 2) * DV:(n % 2 + 1) * DV], ALU.mult, ALU.add)
            mark(last, s_dve)
            if g + 2 < G:
                key_masks(g + 2)
        dve.wait_ge(s_pe, S_OG)
        link(dve.tensor_copy(oS[:].rearrange("n (a g) e -> n a (g e)", a=2), PS[0:NS, 0:2]))
        mark(dve.tensor_tensor(oQ[:], oS[:], oS[:], ALU.mult), s_dve)
        dve.wait_ge(s_dve, S_SSQ - 1)
        mark(dve.reduce_sum(s8[:, 0], oQ[:], X), s_dve)
        dve.wait_ge(s_pe, S_SC)
        for half in range(2):
            last = dve.tensor_copy(sT[:, half * 64:half * 64 + 64], PS[:, 2 + half, 0:64])
        mark(last, s_dve)
        dve.wait_ge(s_pe, S_TR)
        link(dve.scalar_tensor_tensor(sS2[:], PS[:, 4, 0:P], HD ** -0.5, sbias[:], ALU.mult, ALU.add))
        link(dve.reduce_max(sm8[:, 0:1], sS2[:], X))
        link(dve.tensor_tensor(sm8[:, 0:1], sm8[:, 0:1], ssink[:], ALU.max))
        link(dve.tensor_tensor(sm8[:, 2:3], ssink[:], sm8[:, 0:1], ALU.subtract))
        mark(dve.tensor_scalar(sm8[:, 1:2], sm8[:, 0:1], -1.0, None, ALU.mult), s_dve)
        dve.wait_ge(act_s, 10)
        link(dve.tensor_tensor(sm8[:, 5:6], sm8[:, 3:4], sm8[:, 4:5], ALU.add))
        link(dve.reciprocal(sm8[:, 6:7], sm8[:, 5:6]))
        mark(dve.tensor_scalar(sS2[:], sS2[:], sm8[:, 6:7], None, ALU.mult), s_dve)
        dve.wait_ge(s_pe, S_PT)
        mark(dve.tensor_copy(sPT[:], PS[:, 4, 0:P]), s_dve)
        dve.wait_ge(s_pe, S_PV)
        for c in range(2):
            for half in range(2):
                last = dve.tensor_copy(oT[:, 2 * c + half].rearrange("d g n -> d (g n)"),
                                       PS[0:HD, 5, 0:P].rearrange("d (m q) -> d m q", q=4)[:, :, 2 * half + c])
        mark(last, s_dve)
        dve.wait_ge(act_s, 12)
        link(dve.tensor_tensor(oS[:], oS[:], s8[:, 2].rearrange("n (g o) -> n g o", o=1).to_broadcast([NS, G, DV]), ALU.mult))
        link(dve.tensor_tensor(oS[:], oS[:], gath[:, :, 1], ALU.mult))
        dve.wait_ge(s_pe, S_OT)
        link(dve.tensor_tensor(oQ[:], PS[0:NS, 0:2].rearrange("n a (g e) -> n (a g) e", e=DV), gath[:, :, 2], ALU.mult))
        mark(dve.tensor_tensor(oS[:], oS[:], oQ[:], ALU.add), s_dve)

        dve.wait_ge(s_dve, S_MERGED)
        dve.wait_ge(o_small, 96)

        def o_first(b, s):
            dve.wait_ge(t_hi, upto(NB + b))
            dve.tensor_tensor(mT_lo[:], PS[:, 0:2].rearrange("p a n -> p (a n)"), BF(mT_hi[:]), ALU.subtract).then_inc(t_lo, 1)
            dve.wait_ge(o_z, upto(b))
            dve.scalar_tensor_tensor(hh[s][:], hh[s][:], ALPHA, PS[:, 2:4].rearrange("p a n -> p (a n)"),
                                     ALU.mult, ALU.add).then_inc(o_zz, 1)
            dve.wait_ge(o_zz, upto(b))
            stats(dve, hh[s], st1[s], n_sa, n_st, upto(NB + b))
            dve.wait_ge(n_rs, upto(NB + b))
            dve.scalar_tensor_tensor(st1[s][:, 14:15], st1[s][:, 12:13], -1.0, st1[s][:, 15:16],
                                     ALU.mult, ALU.mult).then_inc(n_nm, 1)
            dve.wait_ge(n_xn, upto(NB + b))
            dve.tensor_tensor(hh[s][:], hh[s][:], ln1_g[:], ALU.mult).then_inc(n_hg, 1)

        def o_second(b, s):
            dve.wait_ge(o_rl, upto(b))
            dve.tensor_tensor(lg[:, ds(b, 1)].rearrange("p o n -> p (o n)"), PS[:, 6, 0:4 + NE], br[:], ALU.add).then_inc(o_lg, 1)

        pipelined(dve, o_first, o_second)

        def bc(t, n):
            return t.rearrange("p (a o) -> p a o", o=1).to_broadcast([P, t.shape[1], n])

        def row(t, a):
            return t.rearrange("p (o n) -> p o n", o=1).to_broadcast([P, a, t.shape[1]])

        def first_max(x, m, n, iota, out, tmp):
            link(dve.tensor_tensor(out, x, bc(m, n), ALU.is_equal))
            link(dve.scalar_tensor_tensor(tmp, out, -100.0, row(iota, NB), ALU.mult, ALU.add))
            link(dve.tensor_reduce(rt["mi"][:], tmp, X, ALU.min))
            link(dve.tensor_tensor(out, tmp, bc(rt["mi"][:], n), ALU.is_equal))

        dve.wait_ge(o_lg, upto(8))
        dve.wait_ge(n_h, upto(NB + 8))
        for s in range(2):
            dve.wait_ge(h_out[s], stored(1, s, 5 - s))
        dve.wait_ge(pool_s, 4)
        link(dve.tensor_copy(iot[:], ioti[:]))
        link(dve.tensor_copy(tok[:], toki[:]))
        i4, i18, i32, i50, i128 = (iot[:, 0:n] for n in (4, 18, NE, MAXBLK, P))
        ip = iot[:, P:P + 1]
        gl, el = lg[:, :, 0:4], lg[:, :, 4:]
        link(dve.reduce_max(rt["gm"][:], gl, X))
        mark(dve.tensor_tensor(gq[0][:], gl, bc(rt["gm"][:], 4), ALU.subtract), d_g)
        first_max(gl, rt["gm"][:], 4, i4, gq[1][:], gq[2][:])
        dve.wait_ge(act_s, 13)
        link(dve.reduce_sum(rt["sg"][:], gq[0][:], X))
        link(dve.reciprocal(rt["pg"][:], rt["sg"][:]))
        link(dve.tensor_scalar(gq[2][:], gq[1][:], -NEG, NEG, ALU.mult, ALU.add))
        link(dve.tensor_tensor(em[:].rearrange("p b (g e) -> p b g e", g=G), el.rearrange("p b (g e) -> p b g e", g=G),
                               gq[2][:].rearrange("p b (g o) -> p b g o", o=1).to_broadcast([P, NB, G, NE // G]), ALU.add))
        link(dve.reduce_max(rt["m1"][:], em[:], X))
        first_max(em[:], rt["m1"][:], NE, i32, O[1][:], tt_[:])
        link(dve.scalar_tensor_tensor(em2[:], O[1][:], 2 * NEG, em[:], ALU.mult, ALU.add))
        link(dve.reduce_max(rt["m2"][:], em2[:], X))
        first_max(em2[:], rt["m2"][:], NE, i32, O[2][:], tt_[:])
        mark(dve.tensor_tensor(rt["d"][:], rt["m2"][:], rt["m1"][:], ALU.subtract), d_g)
        link(dve.tensor_scalar(valid[:, 0:1], ip, float(NS), None, ALU.is_lt))
        link(dve.tensor_scalar(valid[:, 1:2], ip, float(PAD0), None, ALU.is_ge))
        link(dve.tensor_tensor(valid[:, 0:1], valid[:, 0:1], valid[:, 1:2], ALU.add))
        for c in (1, 2):
            link(dve.tensor_scalar(O[c][:, 0], O[c][:, 0], valid[:, 0:1], None, ALU.mult))
        mark(dve.tensor_tensor(O[0][:], O[1][:], O[2][:], ALU.add), d_O)
        dve.wait_ge(act_s, 14)
        link(dve.tensor_scalar(rt["s"][:], rt["e"][:], 1.0, None, ALU.add))
        link(dve.reciprocal(rt["r"][:], rt["s"][:]))
        link(dve.tensor_tensor(wts[:, :, 0], rt["r"][:], rt["pg"][:], ALU.mult))
        link(dve.tensor_tensor(wts[:, :, 1], wts[:, :, 0], rt["e"][:], ALU.mult))
        dve.wait_ge(d_pre, 1)
        link(dve.tensor_copy(pre[:].rearrange("p b e -> p (b e)"), PS[:, 0, 0:NB * NE]))
        link(dve.tensor_copy(tot[:].rearrange("p b e -> p (b e)"), PS[:, 1, 0:NB * NE]))
        link(dve.tensor_copy(cum[:], tot[:, 0]))
        for b in range(1, NB):
            link(dve.tensor_tensor(pre[:, b], pre[:, b], cum[:], ALU.add))
            link(dve.tensor_tensor(cum[:], cum[:], tot[:, b], ALU.add))
        link(dve.tensor_scalar(ov[:], cum[:], float(P), None, ALU.is_gt))
        for k in range(2, NB):
            link(dve.scalar_tensor_tensor(ov[:], cum[:], float(P * k), ov[:], ALU.is_gt, ALU.add))
        link(dve.tensor_tensor_scan(ove[:], ones[:, 0:NE], ov[:], 0.0, ALU.mult, ALU.add))
        link(dve.tensor_tensor(ovs[:], ove[:], ov[:], ALU.subtract))
        for c in range(2):
            oc = O[c + 1][:]
            for src, name in ((pre[:], "rk"), (row(ovs[:], NB), "bs"), (row(i32, NB), "ie")):
                link(dve.tensor_tensor(tt_[:], oc, src, ALU.mult))
                link(dve.reduce_sum(sl[name][:, c * NB:(c + 1) * NB], tt_[:], X))
        v = {n: t[:] for n, t in sl.items()}
        link(dve.tensor_scalar(v["k1"], v["rk"], float(P), None, ALU.is_ge))
        link(dve.tensor_copy(v["k"], v["k1"]))
        for k in range(2, NB):
            link(dve.scalar_tensor_tensor(v["k"], v["rk"], float(P * k), v["k"], ALU.is_ge, ALU.add))
        link(dve.tensor_tensor(v["b"], v["bs"], v["k"], ALU.add))
        link(dve.scalar_tensor_tensor(v["b"], v["b"], float(NE - 1), v["ie"], ALU.add, ALU.subtract))
        link(dve.tensor_tensor(v["b"], v["b"], v["k1"], ALU.mult))
        link(dve.tensor_tensor(v["b"], v["b"], v["ie"], ALU.add))
        link(dve.scalar_tensor_tensor(v["r"], v["k"], -float(P), v["rk"], ALU.mult, ALU.add))
        link(dve.scalar_tensor_tensor(v["w"], v["b"], float(P), v["r"], ALU.mult, ALU.add))
        link(dve.tensor_copy(ridx[:], v["w"]))
        link(dve.tensor_tensor(oh_r[:], bc(v["r"], P), row(i128, 2 * NB), ALU.is_equal))
        link(dve.tensor_tensor(oh_b[:], bc(v["b"], MAXBLK), row(i50, 2 * NB), ALU.is_equal))
        link(dve.tensor_scalar(tok[:, 0:1], tok[:, 0:1], valid[:, 0:1], None, ALU.mult))
        for c in range(2):
            last = dve.tensor_tensor(oh_b[:, c * NB:(c + 1) * NB], oh_b[:, c * NB:(c + 1) * NB], bc(tok[:], MAXBLK), ALU.mult)
        mark(last, d_O)
        link(dve.tensor_tensor(cmp_[:], row(ove[:], 18), bc(i18, NE), ALU.is_le))
        link(dve.reduce_sum(ef[:], cmp_[:], X))
        link(dve.tensor_scalar(ef[:], ef[:], float(NE - 1), None, ALU.min))
        link(dve.tensor_copy(etab[:, NE:MAXBLK], ef[:]))
        link(dve.tensor_copy(novr[:], ove[:, NE - 1:NE]))
        dve.wait_ge(d_table, 1)
        mark(dve.tensor_copy(idx_all[:], PS[:, 2, 0:MAXBLK]), d_route)

        dve.wait_ge(d_route, 1)
        iters = 15 + (dve.value_load(novr[0:1, 0:1], min_val=0, max_val=16) + 1) // 2

        def low(t, j):
            dve.wait_ge(*piece_hi(t, j))
            dve.tensor_tensor(wm_lo[:, j], raw[:, j], BF(wm_hi[:, j]), ALU.subtract).then_inc(m_loD[j // 4], 1)

        def y_half(t, s, uses):
            dve.wait_ge(*piece_used(t, 5))
            dve.wait_ge(m_yo[s], 16 * (1 + uses))
            dve.tensor_copy(yb[s][:, 512:1024], PS[:, 6]).then_inc(m_yd, 1)

        def x_low(t):
            dve.wait_ge(t_hi, upto(2 * NB + t))
            dve.tensor_tensor(xT_lo[:], PS[:, 0:2].rearrange("p a n -> p (a n)"), BF(xT_hi[:]), ALU.subtract).then_inc(t_lo, 1)

        def m_step(t, s, uses, prev, more):
            if more:
                low(t + 1, 0)
                low(t + 1, 2)
            dve.wait_ge(m_sg, upto(t))
            dve.wait_ge(*piece_used(t, 3))
            dve.wait_ge(u_T, upto(NB + t - 1))
            dve.tensor_tensor(hm[:], PS[:, 3], sg_t[:], ALU.mult).then_inc(m_hm, 1)
            if more:
                x_low(t + 1)
                low(t + 1, 3)
            low(t, 4)
            dve.wait_ge(u_c, upto(NB + t))
            dve.tensor_tensor(hT_lo[:], PS[:, 4], BF(hT_hi[:]), ALU.subtract).then_inc(m_hlo, 1)
            if prev:
                y_half(t - 1, 1 - s, uses)

        low(0, 0)
        low(0, 2)
        low(0, 3)
        x_low(0)
        m_step(0, 0, 0, False, True)
        with dve.Fori(0, iters) as i:
            m_step(2 * i + 1, 1, i, True, True)
            m_step(2 * i + 2, 0, i, True, True)
        m_step(2 * iters + 1, 1, iters, True, False)
        y_half(2 * iters + 1, 1, iters)

        dve.wait_ge(m_yo[0], 16 * (iters + 2))
        dve.wait_ge(m_yo[1], 16 * (iters + 2))
        dve.wait_ge(*piece_lo(2 * iters + 1, 5))
        dve.wait_ge(f_small, 32)

        def f_first(b, s):
            dve.wait_ge(f_b, upto(b - 2))
            dve.tensor_copy(fw[s][:], wts[:, ds(b, 1)].rearrange("p o c -> p (o c)")).then_inc(f_w, 1)
            dve.wait_ge(f_a, upto(b))
            dve.wait_ge(f_w, upto(b))
            dve.wait_ge(h_out[s], stored(2, s, use(b, s)))
            dve.scalar_tensor_tensor(zz[s][:], yc[s][:], fw[s][:, 1:2], ya[s][:], ALU.mult, ALU.add).then_inc(f_b, 1)
            dve.wait_ge(f_b, upto(b))
            dve.wait_ge(h_in[s], 32 * (5 - s) + 16 * (use(b, s) + 1))
            dve.scalar_tensor_tensor(zz[s][:], h1l[s][:], ALPHA, zz[s][:], ALU.mult, ALU.add).then_inc(f_z, 1)
            dve.wait_ge(f_z, upto(b))
            stats(dve, zz[s], st2[s], n_sa, n_st, upto(2 * NB + b))
            dve.wait_ge(n_rs, upto(2 * NB + b))
            dve.scalar_tensor_tensor(st2[s][:, 14:15], st2[s][:, 12:13], -1.0, st2[s][:, 15:16],
                                     ALU.mult, ALU.mult).then_inc(n_nm, 1)
            dve.wait_ge(n_xn, upto(2 * NB + b))
            dve.tensor_tensor(zz[s][:], zz[s][:], ln2_g[:], ALU.mult).then_inc(n_hg, 1)

        pipelined(dve, f_first, lambda b, s: None)

    @block.tensor
    def _(pe):
        def split_product(out, x_hi, x_lo, w_hi_, w_lo_, start, stop):
            pe.matmul(out, x_hi, w_hi_, start=start, stop=False)
            pe.matmul(out, x_hi, w_lo_, start=False, stop=False)
            return pe.matmul(out, x_lo, w_hi_, start=False, stop=stop)

        def transposes(bank, src, count):
            for k in range(count):
                last = pe.transpose(PS[:, bank + k // 4, (k % 4) * P:(k % 4 + 1) * P], src[:, k * P:(k + 1) * P], ident[:])
            return last

        pe.wait_ge(c_id, 6)
        pe.wait_ge(c_in, 80)
        for a in range(4):
            pe.wait_ge(c_rel, 1 + 2 * a)
            for h in range(4):
                last = pe.matmul(PS[:, 4, h * P:(h + 1) * P], relw[:, 4 * a + h, :], onehot[:], start=True, stop=True)
            last.then_inc(c_rel, 1)

        def second(b, s):
            pe.wait_ge(n_h, upto(b))
            pe.wait_ge(t_hi, upto(b - 1))
            transposes(0, hn[s], KC).then_inc(t_T, 1)
            pe.wait_ge(t_hi, upto(b))
            pe.wait_ge(e_lrc, upto(b - 1))
            for k in range(KC):
                last = pe.matmul(PS[:, 2, 0:RANK], hTs[s][:, k * P:(k + 1) * P], wlr[:, k], start=(k == 0), stop=(k == KC - 1))
            last.then_inc(e_lr, 1)
            pe.wait_ge(e_lrc, upto(b))
            pe.wait_ge(e_lrd, upto(b - 1))
            pe.transpose(PS[0:RANK, 3, 0:P], lr_t[:], ident[:]).then_inc(e_lrT, 1)

        pipelined(pe, lambda b, s: None, second)

        pe.wait_ge(e_lrd, upto(8))
        with pe.Fori(0, G) as g:
            n0 = g * NB

            def step(n, b, s, uses, first):
                hT = lambda k: hTs[s][:, k * P:(k + 1) * P]

                def feature_major(out, c):
                    for k in range(KC):
                        last = pe.matmul(out, wn[:, k, c:c + P], hT(k), start=(k == 0), stop=(k == KC - 1))
                    return last

                def wide(out, c):
                    for k in range(KC):
                        cols = slice(c, c + 2 * DV)
                        last = split_product(out, hT_hl[:, 0, k * P:(k + 1) * P], hT_hl[:, 1, k * P:(k + 1) * P],
                                             w_hi[:, k, cols], w_lo[:, k, cols], k == 0, k == KC - 1)
                    return last

                if first:
                    pe.wait_ge(b_gk, 32 * (g + 1))
                    pe.wait_ge(b_wn, 96 * (g + 1))
                pe.wait_ge(b_hT[s], 16 * (uses + 1))
                pe.wait_ge(b_ka, upto(n - 1))
                pe.matmul(PS[:, 5, P:2 * P], gkup[:], lrT[:, ds(b * P, P)], start=True, stop=True)
                feature_major(PS[:, 5, 0:P], W_KA)
                for k in range(KC):
                    last = pe.matmul(PS[:, 5, 2 * P:2 * P + HD], hT(k), wn[:, k, W_VA:W_VA + HD], start=(k == 0), stop=(k == KC - 1))
                last.then_inc(b_p5, 1)
                pe.wait_ge(b_qq, upto(n - 1))
                if first:
                    pe.wait_ge(b_ko, upto(g - 1))
                feature_major(PS[:, 4, 0:P], W_Q)
                feature_major(PS[:, 4, P:2 * P], W_K)
                feature_major(PS[:, 4, 2 * P:3 * P], W_QA)
                feature_major(PS[:, 4, 3 * P:4 * P], W_QA + P).then_inc(b_p4, 1)
                pe.wait_ge(b_hl, upto(n))
                if first:
                    pe.wait_ge(b_lo, upto(g * WIDE + 1))
                pe.wait_ge(b_vrc, upto(n - 1))
                wide(PS[:, 2], W_V).then_inc(b_vr, 1)
                pe.wait_ge(b_qa, upto(n))
                pe.wait_ge(b_ka, upto(n))
                pe.wait_ge(b_pc, upto(n - 1))
                pe.wait_ge(b_pd, upto(n - 1))
                for half in range(2):
                    r = slice(half * HD, (half + 1) * HD)
                    for c in range(2):
                        if not first:
                            pe.matmul(PS[:, half, c * 2 * P:c * 2 * P + P], qa[r, c, :], ka[1 - s][r, :], start=True, stop=True)
                        last = pe.matmul(PS[:, half, c * 2 * P + P:(c + 1) * 2 * P], qa[r, c, :], ka[s][r, :], start=True, stop=True)
                last.then_inc(b_sc, 1)
                pe.wait_ge(b_qq, upto(n))
                pe.wait_ge(b_T, upto(n - 1))
                pe.matmul(PS[:, 6, 0:P], kk[:], qq[:], start=True, stop=True)
                pe.transpose(PS[:, 6, P:2 * P], kk[:], ident[:]).then_inc(b_A, 1)
                if first:
                    pe.wait_ge(b_lo, upto(g * WIDE + 3))
                pe.wait_ge(b_eg, upto(n - 1))
                wide(PS[:, 3], W_GA).then_inc(b_gg, 1)
                pe.wait_ge(b_P, upto(n))
                pe.wait_ge(b_bs, upto(n))
                for h in range(HPG):
                    if not first:
                        pe.transpose(PS[:, 0, h * P:(h + 1) * P], Sc[:, h, 0:P], ident[:])
                    last = pe.transpose(PS[:, 1, h * P:(h + 1) * P], Sc[:, h, P:2 * P], ident[:])
                last.then_inc(b_pt, 1)
                pe.wait_ge(b_oa, upto(n - 1))
                pe.wait_ge(b_At, upto(n))
                pe.wait_ge(b_vrc, upto(n))
                pe.wait_ge(b_Sm, upto(n))
                pe.matmul(PS[:, 6, DV:2 * DV], kd[:], vr[:, 0:DV], start=True, stop=True).then_inc(b_up, 1)
                pe.matmul(PS[:, 7, 0:DV], At[:], vr[:, 0:DV], start=True, stop=False)
                pe.matmul(PS[:, 7, 0:DV], qq[:], Sm[:], start=False, stop=True)
                pe.wait_ge(b_pc, upto(n))
                pe.wait_ge(b_pd, upto(n))
                for h in range(HPG):
                    o = PS[:, 7, DV + h * HD:DV + (h + 1) * HD]
                    if not first:
                        pe.matmul(o, Pt[:, 0, h], va[1 - s][:], start=True, stop=False)
                    last = pe.matmul(o, Pt[:, 1, h], va[s][:], start=first, stop=True)
                last.then_inc(b_o, 1)

            step(n0, 0, 0, 5 * g, True)
            with pe.Fori(0, 4) as i:
                step(n0 + 2 * i + 1, 2 * i + 1, 1, 4 * g + i, False)
                step(n0 + 2 * i + 2, 2 * i + 2, 0, 5 * g + i + 1, False)
            wait_apart(pe, b_qq, upto(n0 + 8))
            pe.transpose(PS[:, 4, 0:HD], ka[0][0:HD, :], ident[0:HD, 0:HD]).then_inc(b_kT, 1)

        stageB_done(pe)
        pe.wait_ge(b_ko, upto(G - 1))
        for g in range(G):
            pe.transpose(PS[0:NS, 0, g * P:(g + 1) * P], gsk[:, g, :], ident[:])
        for g in range(G):
            last = pe.transpose(PS[0:NS, 1, g * HD:(g + 1) * HD], ska[0:HD, g, :], ident[0:HD, 0:HD])
        last.then_inc(s_pe, 1)

        def outer(g):
            pe.wait_ge(s_dve, S_KM[g])
            if g:
                pe.wait_ge(s_dve, S_STATE[g - 1])
            for n in range(NS):
                last = pe.matmul(PS[:, 2 + n // 2, (n % 2) * DV:(n % 2 + 1) * DV], km[g % 2][:, n, :], gath[:, g, 0, :],
                                 start=True, stop=True)
            last.then_inc(s_pe, 1)

        def read_out(g):
            pe.wait_ge(s_dve, S_STATE[g])
            for n in range(NS):
                last = pe.matmul(PS[0:NS, g // 2, (g % 2) * DV:(g % 2 + 1) * DV], qm[:, g, n, :], st[:, g, n],
                                 start=(n == 0), stop=(n == NS - 1))
            return last

        pe.wait_ge(s_qm, 2)
        pe.wait_ge(s_in, 16 * 13)
        outer(0)
        for g in range(1, G):
            outer(g)
            read_out(g - 1)
        read_out(G - 1).then_inc(s_pe, 1)
        pe.wait_ge(s_win, 16 * 17)
        for a in range(8):
            if a >= 2:
                pe.wait_ge(act_s, a - 1)
            for m in range(4):
                g, n = (4 * a + m) // NS, (4 * a + m) % NS
                last = pe.transpose(PS[:, 6 + a % 2, m * P:(m + 1) * P], Kd[:, n, g].rearrange("j t d -> j (t d)"), ident[:])
            last.then_inc(s_pe, 1)
        pe.wait_ge(act_s, 8)
        for half in range(2):
            r = slice(half * HD, (half + 1) * HD)
            for g in range(G):
                for n in range(NS):
                    m = g * NS + n
                    last = pe.matmul(PS[:, 2 + half, m:m + 33:32], KT[r, g, n, :], asq[r, g, :, n], start=True, stop=True)
        last.then_inc(s_pe, 1)
        pe.wait_ge(s_dve, S_ST)
        pe.transpose(PS[:, 4, 0:P], sT[:], ident[:]).then_inc(s_pe, 1)
        pe.wait_ge(s_dve, S_PROB)
        pe.transpose(PS[:, 4, 0:P], sS2[:], ident[:]).then_inc(s_pe, 1)
        pe.wait_ge(s_dve, S_PTC)
        for g in range(G):
            for n in range(NS):
                m = g * NS + n
                last = pe.matmul(PS[0:HD, 5, 4 * m:4 * m + 4], Vw[:, n, g, :],
                                 sPT[:].rearrange("k (q m) -> k q m", q=4)[:, :, m], start=True, stop=True)
        last.then_inc(s_pe, 1)
        pe.wait_ge(s_dve, S_OTC)
        for g in range(G):
            for h in range(HPG):
                c = (g % 2) * DV + h * HD
                last = pe.transpose(PS[0:NS, g // 2, c:c + HD], oT[:, h, g, :], ident[0:HD, 0:HD])
        last.then_inc(s_pe, 1)

        pe.wait_ge(b_lo, upto(G * WIDE - 1 + 4))
        pe.wait_ge(s_dve, S_MERGED)
        pe.wait_ge(o_small, 96)

        def o_first(b, s):
            pe.wait_ge(h_in[s], 32 * (use(b, s) + 1))
            pe.wait_ge(t_lo, upto(b - 1))
            transposes(0, mg[s], KC).then_inc(t_T, 1)
            pe.wait_ge(t_lo, upto(b))
            pe.wait_ge(o_zz, upto(b - 1))
            for half in range(2):
                c = slice(half * 512, half * 512 + 512)
                for k in range(KC):
                    last = split_product(PS[:, 2 + half], mT_hi[:, k * P:(k + 1) * P], mT_lo[:, k * P:(k + 1) * P],
                                         wo_hi[:, k, c], wo_lo[:, k, c], k == 0, k == KC - 1)
            last.then_inc(o_z, 1)

        def o_second(b, s):
            pe.wait_ge(n_h, upto(NB + b))
            pe.wait_ge(u_c, upto(b - 1))
            transposes(4, hh[s], KC).then_inc(u_T, 1)
            pe.wait_ge(u_c, upto(b))
            pe.wait_ge(o_lg, upto(b - 1))
            for k in range(KC):
                last = pe.matmul(PS[:, 6, 0:4 + NE], h1T[:, k * P:(k + 1) * P], wr[:, k, :], start=(k == 0), stop=(k == KC - 1))
            last.then_inc(o_rl, 1)

        pipelined(pe, o_first, o_second)

        pe.wait_ge(d_O, 1)
        pe.matmul(PS[:, 0, 0:NB * NE], strict[:], O[0][:].rearrange("p b e -> p (b e)"), start=True, stop=True)
        pe.matmul(PS[:, 1, 0:NB * NE], ones[:], O[0][:].rearrange("p b e -> p (b e)"), start=True, stop=True).then_inc(d_pre, 1)

        pe.wait_ge(d_O, 2)
        for a in range(2 * NB):
            last = pe.matmul(PS[:, 2, 0:MAXBLK], oh_r[:, a], oh_b[:, a], start=(a == 0), stop=(a == 2 * NB - 1))
        last.then_inc(d_table, 1)

        pe.wait_ge(d_route, 1)
        iters = 15 + (pe.value_load(novr[0:1, 0:1], min_val=0, max_val=16) + 1) // 2

        def up(t, bank, j0):
            for k in range(KC):
                j, c = j0 + k // 4, (k % 4) * DE
                if k % 4 == 0:
                    pe.wait_ge(*piece_lo(t, j))
                last = split_product(PS[:, bank], xT_hi[:, k * P:(k + 1) * P], xT_lo[:, k * P:(k + 1) * P],
                                     wm_hi[:, j, c:c + DE], wm_lo[:, j, c:c + DE], k == 0, k == KC - 1)
                if k % 4 == 3:
                    last.then_inc(m_used[j // 4], 1)

        def down(t):
            pe.wait_ge(m_hlo, upto(t))
            pe.wait_ge(m_ya, upto(t - 1))
            pe.wait_ge(m_yd, upto(t - 1))
            for k in range(DE // P):
                j = 4 + k // 2
                if k % 2 == 0:
                    pe.wait_ge(*piece_lo(t, j))
                for half in range(2):
                    c = (k % 2) * D + half * 512
                    last = split_product(PS[:, 5 + half], hT_hi[:, k * P:(k + 1) * P], hT_lo[:, k * P:(k + 1) * P],
                                         wm_hi[:, j, c:c + 512], wm_lo[:, j, c:c + 512], k == 0, k == DE // P - 1)
                if k % 2 == 1:
                    last.then_inc(m_used[j // 4], 1)

        def x_transposes(t, s, uses):
            pe.wait_ge(m_x[s], 16 * (uses + 1))
            pe.wait_ge(t_lo, upto(NB + t - 1))
            transposes(0, xw[s], KC).then_inc(t_T, 1)

        def m_step(t, s, uses, prev, more):
            pe.wait_ge(t_lo, upto(NB + t))
            pe.wait_ge(m_sg, upto(t - 1))
            up(t, 2, 0)
            pe.wait_ge(m_hm, upto(t - 1))
            up(t, 3, 2)
            if more:
                x_transposes(t + 1, 1 - s, uses)
            if prev:
                down(t - 1)
            pe.wait_ge(m_hm, upto(t))
            pe.wait_ge(m_hlo, upto(t - 1))
            transposes(4, hm, DE // P).then_inc(u_T, 1)

        x_transposes(0, 0, 0)
        m_step(0, 0, 0, False, True)
        with pe.Fori(0, iters) as i:
            m_step(2 * i + 1, 1, i + 1, True, True)
            m_step(2 * i + 2, 0, i + 1, True, True)
        m_step(2 * iters + 1, 1, None, True, False)
        down(2 * iters + 1)

    ctx.close()


INPUTS = ("x_prompt", "x_sample", "state_gla", "cache_swa_k", "cache_swa_v", "meta_tokens", "ln_emb_g", "ln_emb_b",
          "rel_bias", "w_in", "gk_up", "gk_bias", "gla_norm_g", "sinks", "w_out", "ln1_g", "ln1_b", "w_router_group",
          "b_router_group", "w_router_expert", "b_router_expert", "w_gate", "w_up", "w_down", "ln2_g", "ln2_b")
RESULTS = (("y_prompt", (1, 1024, D)), ("y_sample", (NS, 1, D)), ("gla_state_prompt", (1, 1, G, DK, DV)),
           ("swa_k_prompt", (1, 1, WIN, G, HD)), ("swa_v_prompt", (1, 1, WIN, G, HD)),
           ("gla_state_sample", (1, NS, G, DK, DV)), ("swa_k_sample", (1, NS, WIN, G, HD)),
           ("swa_v_sample", (1, NS, WIN, G, HD)))


def bucket_onehot():
    import math

    import numpy as np

    dist = np.arange(WIN - 1, -1, -1)
    large = 16 + (np.log(np.maximum(dist, 1).astype(np.float32) / 16) / math.log(128 / 16) * 16).astype(np.int32)
    bucket = np.where(dist < 16, dist, np.minimum(large, 31))
    return (np.arange(32)[:, None] == bucket[None, :]).astype(np.float32)


def kernel(**inputs):
    import numpy as np
    import concourse.bacc as bacc
    from concourse.bass_utils import run_bass_kernel_spmd

    nc = bacc.Bacc("TRN2", target_bir_lowering=False, num_devices=1)
    arrays = {name: np.ascontiguousarray(inputs[name]) for name in INPUTS}
    arrays["onehot"] = bucket_onehot()
    A = {n: nc.dram_tensor(f"in_{n}", a.shape, F32, kind="ExternalInput").ap() for n, a in arrays.items()}
    R = {n: nc.dram_tensor(f"out_{n}", shape, F32, kind="ExternalOutput").ap() for n, shape in RESULTS}
    build(nc, A, R)
    r = run_bass_kernel_spmd(nc, [{f"in_{n}": a for n, a in arrays.items()}], core_ids=[0])
    return tuple(r.results[0][f"out_{n}"] for n, _ in RESULTS)
```

```python
from contextlib import ExitStack

import concourse.bass as bass
from concourse import mybir

F32 = mybir.dt.float32
F32R = mybir.dt.float32r
I32 = mybir.dt.int32
U32 = mybir.dt.uint32
ACT = mybir.ActivationFunctionType
ALU = mybir.AluOpType
X = mybir.AxisListType.X
ds = bass.ds

P = 128
D = 1024
KC = D // P
META = 16
NB = 9
NS = 8
PAD0 = P - META
G = 4
DK, DV, RANK, HD, HPG = 128, 256, 16, 64, 4
HEADS = 16
WIN = 128
ALPHA = 2.0 ** 0.25
EPS = 1e-5
TAU = 16.0
NEG = -1.0e30
NE = 32
DE = 512
MAXBLK = 50
CREDIT = 4
IN_Q, IN_K, IN_V, IN_R, IN_LR, IN_QA, IN_KA, IN_VA, IN_GA, IN_GB = (
    0, 512, 1024, 2048, 3072, 3088, 4112, 4368, 4624, 5648)
W_KV, W_Q, W_K, W_QA, W_NARROW = 0, 128, 256, 384, 640
W_V, W_R, W_GA, W_GB, W_WIDE = 0, 256, 512, 768, 1024
WIDE = 4
RAW_BASE = (G, G, G, G, 2, 2)
LROW = 384


def upto(n):
    return n + 1 + CREDIT


def build(nc, A, R):
    ctx = ExitStack()

    def sem(name):
        return ctx.enter_context(nc.semaphore(name))

    step_sems = []

    def ssem(name):
        s = sem(name)
        step_sems.append(s)
        return s

    h_dram = nc.dram_tensor("h_dram", (NB, P, D), F32).ap()
    hT_dram = nc.dram_tensor("hT_dram", (NB, P, D), F32).ap()
    mg_dram = nc.dram_tensor("mg_dram", (NB, P, D), F32).ap()
    h1_dram = nc.dram_tensor("h1_dram", (NB * P, D), F32).ap()
    brow_dram = nc.dram_tensor("brow_dram", (HEADS, P * LROW), F32).ap()
    stash_dram = nc.dram_tensor("stash_dram", (NS, G, 3, DV), F32).ap()
    obuf_dram = nc.dram_tensor("obuf_dram", (MAXBLK * P, D), F32).ap()
    prime_dram = nc.dram_tensor("prime_dram", (16, 16, 8), F32).ap()

    def sb(stack, name, shape, dt=F32):
        return stack.enter_context(nc.sbuf_tensor(name, shape, dt))

    both = ctx
    PS = ctx.enter_context(nc.psum_tensor("PS", [P, 8, 512], F32))
    ident = sb(both, "ident", [P, P])
    causal = sb(both, "causal", [P, P])
    strict = sb(both, "strict", [P, P])
    ones = sb(both, "ones", [P, P])
    eps_c = sb(both, "eps_c", [P, 1])
    lg = sb(both, "lg", [P, NB, 4 + NE])
    gsq = sb(both, "gsq", [P, G, NS])
    gsk = sb(both, "gsk", [P, G, NS])
    gse = sb(both, "gse", [P, G, NS])
    asq = sb(both, "asq", [P, G, 2, NS])
    ska = sb(both, "ska", [HD, G, NS])
    sva = sb(both, "sva", [NS, G, HD])
    wts = sb(both, "wts", [P, NB + 1, 2])
    ridx = sb(both, "ridx", [P, 2 * NB], U32)
    etab = sb(both, "etab", [P, MAXBLK], I32)
    novr = sb(both, "novr", [P, 1], I32)
    idx_all = sb(both, "idx_all", [P, MAXBLK], I32)

    sB = ExitStack()
    hTs = [sb(sB, f"hT{s}", [P, D]) for s in range(2)]
    hT_hl = sb(sB, "hT_hl", [P, 2, D], F32R)
    lrT = sb(sB, "lrT", [RANK, NB * P])
    wn = sb(sB, "wn", [P, KC, W_NARROW])
    braw = sb(sB, "braw", [P, WIDE, KC, 256])
    bias = sb(sB, "bias", [P, 2, HPG, 2 * P])
    sink = sb(sB, "sink", [P, HEADS])
    gkup = sb(sB, "gkup", [RANK, DK])
    gkb = sb(sB, "gkb", [P, 1])
    gn = sb(sB, "gn", [P, DV])
    xg = sb(sB, "xg", [P, P])
    ax = sb(sB, "ax", [P, P])
    mn = sb(sB, "mn", [P, P])
    g16 = sb(sB, "g16", [P, P])
    b16 = sb(sB, "b16", [P, P])
    bm = sb(sB, "bm", [P, 2])
    eq = sb(sB, "eq", [P, P])
    ek = sb(sB, "ek", [P, P])
    ebm = sb(sB, "ebm", [P, 1])
    e2 = sb(sB, "e2", [P, 1])
    kk = sb(sB, "kk", [P, P])
    qq = sb(sB, "qq", [P, P])
    At = sb(sB, "At", [P, P])
    kd = sb(sB, "kd", [P, P])
    Sm = sb(sB, "Sm", [P, DV])
    Tn = sb(sB, "Tn", [P, DV])
    kout = sb(sB, "kout", [P, HD])
    qa = sb(sB, "qa", [P, 2, P])
    ka = [sb(sB, f"ka{s}", [P, P]) for s in range(2)]
    vT = sb(sB, "vT", [P, P])
    va = [sb(sB, f"va{s}", [P, HD]) for s in range(2)]
    vr = sb(sB, "vr", [P, 2 * DV])
    Et = sb(sB, "Et", [P, 3, DV])
    Rt = sb(sB, "Rt", [P, 2, DV])
    rr = sb(sB, "rr", [P, DV])
    yg = sb(sB, "yg", [P, DV])
    oa = sb(sB, "oa", [P, DV])
    mgo = [sb(sB, f"mgo{s}", [P, DV]) for s in range(2)]
    Sc = sb(sB, "Sc", [P, HPG, 2 * P])
    Pt = sb(sB, "Pt", [P, 2, HPG, P])
    mx = sb(sB, "mx", [P, HPG])
    nmx = sb(sB, "nmx", [P, HPG])
    sk = sb(sB, "sk", [P, HPG])
    es = sb(sB, "es", [P, HPG])
    su = sb(sB, "su", [P, HPG])
    rden = sb(sB, "rden", [P, HPG])
    ssq = sb(sB, "ssq", [P, 1])
    lnv = sb(sB, "lnv", [P, 1])
    rstd = sb(sB, "rstd", [P, 1])
    s0 = ExitStack()
    x_t = [sb(s0, f"x_t{s}", [P, D]) for s in range(2)]
    hn = [sb(s0, f"hn{s}", [P, D]) for s in range(2)]
    lne_g = sb(s0, "lne_g", [P, D])
    lne_b = sb(s0, "lne_b", [P, D])
    st0 = [sb(s0, f"st0{s}", [P, 16]) for s in range(2)]
    wlr = sb(s0, "wlr", [P, KC, RANK])
    onehot = sb(s0, "onehot", [32, WIN])
    relb = sb(s0, "relb", [32, HEADS])
    relw = sb(s0, "relw", [32, HEADS, P])
    brow = sb(s0, "brow", [P, HEADS, LROW])
    prime = sb(s0, "prime", [16, 8])
    s0.close()
    w_hi = sb(sB, "w_hi", [P, KC, W_WIDE], F32R)
    w_lo = sb(sB, "w_lo", [P, KC, W_WIDE], F32R)
    sB.close()

    sE = ExitStack()
    sC = ExitStack()
    wo_hi = sb(sC, "wo_hi", [P, KC, D], F32R)
    wo_lo = sb(sC, "wo_lo", [P, KC, D], F32R)
    ln1_g = sb(sC, "ln1_g", [P, D])
    ln1_b = sb(sC, "ln1_b", [P, D])
    wr = sb(sC, "wr", [P, KC, 4 + NE])
    br = sb(sC, "br", [P, 4 + NE])
    mg = [sb(sC, f"mg{s}", [P, D]) for s in range(2)]
    sS = ExitStack()
    Kw = sb(sS, "Kw", [P, NS, G, HD])
    Vw = sb(sS, "Vw", [P, NS, G, HD])
    KT = sb(sS, "KT", [HD, G, NS, P])
    aqo = sb(sS, "aqo", [HD, G, 2, NS])
    aq4 = sb(sS, "aq4", [HD, G, NS, HPG])
    km = [sb(sS, f"km{i}", [NS, NS, P]) for i in range(2)]
    kt8 = sb(sS, "kt8", [NS, G, P])
    qm = sb(sS, "qm", [P, G, NS, NS])
    knew = sb(sS, "knew", [NS, G, HD])
    gath = sb(sS, "gath", [NS, G, 3, DV])
    sT = sb(sS, "sT", [P, P])
    sS2 = sb(sS, "sS2", [P, P])
    sbias = sb(sS, "sbias", [P, P])
    ssink = sb(sS, "ssink", [P, 1])
    sm8 = sb(sS, "sm8", [P, 8])
    sPT = sb(sS, "sPT", [P, P])
    oT = sb(sS, "oT", [HD, HPG, G, NS])
    oS, oQ = (k[:].rearrange("t (g c) k -> t g (c k)", g=G) for k in km)
    s8 = sb(sS, "s8", [NS, 3, G])
    sS.close()
    hh = [sb(sC, f"hh{s}", [P, D]) for s in range(2)]
    mT_hi = [sb(sC, f"mT_hi{s}", [P, D], F32R) for s in range(2)]
    mT_lo = [sb(sC, f"mT_lo{s}", [P, D], F32R) for s in range(2)]
    h1T = sb(sC, "h1T", [P, D])
    st1 = [sb(sC, f"st1{s}", [P, 16]) for s in range(2)]
    sC.close()
    sD = ExitStack()
    iot = sb(sD, "iot", [P, P + 1])
    ioti = sb(sD, "ioti", [P, P + 1], I32)
    toki = sb(sD, "toki", [P, NB], I32)
    tok = sb(sD, "tok", [P, NB])
    oh_r = sb(sD, "oh_r", [P, 2 * NB, P])
    oh_b = sb(sD, "oh_b", [P, 2 * NB, MAXBLK])
    rt = {n: sb(sD, "rt_" + n, [P, NB]) for n in ("gm", "sg", "pg", "m1", "m2", "mi", "d", "e", "s", "r")}
    gq = [sb(sD, f"gq{i}", [P, NB, 4]) for i in range(3)]
    em = sb(sD, "em", [P, NB, NE])
    em2 = sb(sD, "em2", [P, NB, NE])
    tt_ = sb(sD, "tt_", [P, NB, NE])
    O = [sb(sD, f"O{i}", [P, NB, NE]) for i in range(3)]
    pre = sb(sD, "pre", [P, NB, NE])
    tot = sb(sD, "tot", [P, NB, NE])
    again = sb(sD, "again", [P, NE, NB])
    cumb = sb(sD, "cumb", [P, NE * NB])
    cum = sb(sD, "cum", [P, NE])
    ov = sb(sD, "ov", [P, NE])
    ove = sb(sD, "ove", [P, NE])
    ovs = sb(sD, "ovs", [P, NE])
    cmp_ = sb(sD, "cmp_", [P, 18, NE])
    ef = sb(sD, "ef", [P, 18])
    valid = sb(sD, "valid", [P, 2])
    sl = {n: sb(sD, "sl_" + n, [P, 2 * NB]) for n in ("rk", "bs", "ie", "k", "k1", "b", "r", "w")}
    sD.close()
    xw = [sb(sE, f"xw{s}", [P, D]) for s in range(2)]
    xi = [sb(sE, f"xi{s}", [P, 1], U32) for s in range(2)]
    xT_hi = sb(sE, "xT_hi", [P, D], F32R)
    xT_lo = sb(sE, "xT_lo", [P, D], F32R)
    sg_t = sb(sE, "sg_t", [P, DE])
    hm = sb(sE, "hm", [P, DE])
    hT_hi = sb(sE, "hT_hi", [P, DE], F32R)
    hT_lo = sb(sE, "hT_lo", [P, DE], F32R)
    yb = [sb(sE, f"yb{s}", [P, D]) for s in range(2)]
    wm_hi = sb(sE, "wm_hi", [P, 6, 2048], F32R)
    wm_lo = sb(sE, "wm_lo", [P, 6, 2048], F32R)
    pad = sb(sE, "pad", [P, 4000])
    raw = sb(sE, "raw", [P, 6, 2048])
    st = raw[:, 0:4].rearrange("p g (n e) -> p g n e", n=NS)
    sE.close()
    sF = ExitStack()
    ya = [sb(sF, f"ya{s}", [P, D]) for s in range(2)]
    yc = [sb(sF, f"yc{s}", [P, D]) for s in range(2)]
    h1l = [sb(sF, f"h1l{s}", [P, D]) for s in range(2)]
    zz = [sb(sF, f"zz{s}", [P, D]) for s in range(2)]
    zo = [sb(sF, f"zo{s}", [P, D]) for s in range(2)]
    st2 = [sb(sF, f"st2{s}", [P, 16]) for s in range(2)]
    fi = [sb(sF, f"fi{s}", [P, 2], U32) for s in range(2)]
    fw = [sb(sF, f"fw{s}", [P, 2]) for s in range(2)]
    ln2_g = sb(sF, "ln2_g", [P, D])
    ln2_b = sb(sF, "ln2_b", [P, D])
    sF.close()

    primed = []

    def dsem(name):
        s = sem(name)
        primed.append(s)
        return s

    c_id = sem("c_id")
    c_in = sem("c_in")
    c_rin = sem("c_rin")
    c_rel = sem("c_rel")
    c_rpe = sem("c_rpe")
    c_brow = sem("c_brow")
    e_x = [sem(f"e_x{s}") for s in range(2)]
    n_sa = ssem("n_sa")
    n_st = ssem("n_st")
    n_ln = ssem("n_ln")
    n_rs = ssem("n_rs")
    n_nm = ssem("n_nm")
    n_xn = ssem("n_xn")
    n_hg = ssem("n_hg")
    n_h = ssem("n_h")
    h_out = [dsem(f"h_out{s}") for s in range(2)]
    t_T = ssem("t_T")
    t_hi = ssem("t_hi")
    t_lo = ssem("t_lo")
    e_hTo = [dsem(f"e_hTo{s}") for s in range(2)]
    e_lr = ssem("e_lr")
    e_lrd = ssem("e_lrd")

    b_gn = sem("b_gn")
    b_gk = sem("b_gk")
    b_bi = sem("b_bi")
    b_wn = sem("b_wn")
    b_hs = ssem("b_hs")
    b_hl = ssem("b_hl")
    b_bv = ssem("b_bv")
    w_raw = [sem(f"w_raw{j}") for j in range(6)]
    b_hi = ssem("b_hi")
    b_lo = ssem("b_lo")
    b_hT = [sem(f"b_hT{s}") for s in range(2)]
    b_p5 = ssem("b_p5")
    b_p4 = ssem("b_p4")
    b_vr = ssem("b_vr")
    b_gg = ssem("b_gg")
    b_sc = ssem("b_sc")
    b_A = ssem("b_A")
    b_pt = ssem("b_pt")
    b_up = ssem("b_up")
    b_o = ssem("b_o")
    b_xg = ssem("b_xg")
    b_ka = ssem("b_ka")
    b_kd = sem("b_kd")
    b_vt = ssem("b_vt")
    b_va = ssem("b_va")
    b_ax = ssem("b_ax")
    b_ex = ssem("b_ex")
    b_lx = ssem("b_lx")
    b_mn = ssem("b_mn")
    b_g16 = ssem("b_g16")
    b_b16 = ssem("b_b16")
    b_bmn = ssem("b_bmn")
    b_eq = ssem("b_eq")
    b_qa = ssem("b_qa")
    b_kk = ssem("b_kk")
    b_qq = ssem("b_qq")
    b_vrc = ssem("b_vrc")
    b_er = ssem("b_er")
    b_eg = ssem("b_eg")
    b_bs = ssem("b_bs")
    b_sz = sem("b_sz")
    b_mx = ssem("b_mx")
    b_mx2 = ssem("b_mx2")
    b_nmx = ssem("b_nmx")
    b_P = ssem("b_P")
    b_At = ssem("b_At")
    b_Sm = ssem("b_Sm")
    b_pc = ssem("b_pc")
    b_pd = ssem("b_pd")
    b_T = ssem("b_T")
    b_e2 = ssem("b_e2")
    b_den = ssem("b_den")
    b_rden = ssem("b_rden")
    b_E1 = ssem("b_E1")
    b_E2 = ssem("b_E2")
    b_R = ssem("b_R")
    b_rr = ssem("b_rr")
    b_rg = ssem("b_rg")
    b_sq = ssem("b_sq")
    b_lv = ssem("b_lv")
    b_rs = ssem("b_rs")
    b_yg = ssem("b_yg")
    b_oa = ssem("b_oa")
    b_ob = ssem("b_ob")
    b_mg = ssem("b_mg")
    b_mo = [dsem(f"b_mo{s}") for s in range(2)]
    b_sta = ssem("b_sta")
    b_std = sem("b_std")
    b_stg = sem("b_stg")
    b_fin = ssem("b_fin")
    b_kT = ssem("b_kT")
    b_ko = ssem("b_ko")
    b_gout = sem("b_gout")
    b_gfree = ssem("b_gfree")

    act_s, dve_s, pool_s = sem("act_s"), sem("dve_s"), sem("pool_s")
    s_pe = sem("s_pe")
    S_KT8, S_OUTER, S_OG, S_KT, S_SC, S_TR, S_PT, S_PV, S_OT = 1, 2, 10, 11, 19, 20, 21, 22, 23
    s_dve = sem("s_dve")
    S_KNEW, S_AQ, S_KM, S_STATE, S_SSQ, S_ST, S_NMX, S_PROB, S_PTC, S_OTC, S_MERGED = (
        1, 2, (3, 4, 7, 10), (5, 8, 11, 13), 16, 17, 18, 19, 20, 21, 22)
    s_qm = sem("s_qm")
    d_g, d_O, d_pre, d_route = (sem(n) for n in ("d_g", "d_O", "d_pre", "d_route"))
    s_in = sem("s_in")
    s_shift = sem("s_shift")
    s_new = sem("s_new")
    s_win = sem("s_win")
    s_out = sem("s_out")

    o_small = sem("o_small")
    h_in = [sem(f"h_in{s}") for s in range(2)]
    o_z = ssem("o_z")
    o_zz = ssem("o_zz")
    u_T = ssem("u_T")
    u_c = ssem("u_c")
    o_rl = ssem("o_rl")
    o_lg = ssem("o_lg")

    d_table = sem("d_table")

    m_hi = [ssem(f"m_hi{i}") for i in range(2)]
    m_loD = [ssem(f"m_loD{i}") for i in range(2)]
    m_loP = [ssem(f"m_loP{i}") for i in range(2)]
    m_used = [ssem(f"m_used{i}") for i in range(2)]
    m_xi = ssem("m_xi")
    m_x = [sem(f"m_x{s}") for s in range(2)]
    m_sg = ssem("m_sg")
    m_hm = ssem("m_hm")
    m_hlo = ssem("m_hlo")
    m_ya = ssem("m_ya")
    m_yd = ssem("m_yd")
    m_yo = [dsem(f"m_yo{s}") for s in range(2)]

    f_small = sem("f_small")
    f_i = ssem("f_i")
    f_y = [sem(f"f_y{s}") for s in range(2)]
    f_w = ssem("f_w")
    f_a = ssem("f_a")
    f_b = ssem("f_b")
    f_z = ssem("f_z")

    BF = lambda t: t.bitcast(F32)
    w_in = A["w_in"][0].rearrange("(k p) n -> p k n", p=P)

    def pipelined(eng, first, second):
        first(0, 0)
        with eng.Fori(0, 4) as i:
            first(2 * i + 1, 1)
            second(2 * i, 0)
            first(2 * i + 2, 0)
            second(2 * i + 1, 1)
        second(8, 0)

    def use(b, s):
        return b // 2 if isinstance(b, int) else (b - s) // 2

    def wait_apart(eng, s, value):
        if not isinstance(value, int):
            value = eng.to_reg(value)
        eng.wait_ge(c_id, 3)
        eng.wait_ge(s, value)

    def piece_hi(t, j):
        return (m_hi[0], upto(4 * t + j)) if j < 4 else (m_hi[1], upto(2 * t + j - 4))

    def piece_lo(t, j):
        if j in (1, 5):
            return m_loP[j // 4], upto(t)
        return (m_loD[0], upto(3 * t + (0, None, 1, 2)[j])) if j < 4 else (m_loD[1], upto(t))

    def piece_used(t, j):
        return (m_used[0], upto(4 * t + j)) if j < 4 else (m_used[1], upto(2 * t + j - 4))

    def stored(stage, s, uses):
        return 16 * (1 + stage * (5 - s) + uses)

    def stage0_done(eng):
        for s in range(2):
            eng.wait_ge(e_hTo[s], 16 * (1 + 5 - s))
            eng.wait_ge(h_out[s], stored(0, s, 5 - s))
        eng.wait_ge(c_brow, 16)
        eng.wait_ge(e_lrd, upto(8))
        for s in primed:
            eng.wait_ge(s, 16)

    def stageB_done(eng):
        eng.wait_ge(b_gfree, upto(G - 1))
        eng.wait_ge(b_sta, upto(G - 1))
        eng.wait_ge(b_mg, upto(G * NB - 1))
        for s in range(2):
            eng.wait_ge(b_mo[s], 16 * (1 + (5 - s) * G))

    def stats(dve, z, t, s_a, s_b, n):
        dve.bn_stats(t[:, 0:6], z[:, 0:512])
        dve.bn_stats(t[:, 6:12], z[:, 512:1024]).then_inc(s_a, 1)
        wait_apart(dve, s_a, n)
        dve.bn_aggr(t[:, 12:14], t[:, 0:12]).then_inc(s_b, 1)

    block = ctx.enter_context(nc.Block())

    @block.sync
    def _(sp):
        sp.dma_start(relb[:], A["rel_bias"]).then_inc(c_rin, 16)
        sp.dma_start(onehot[:], A["onehot"]).then_inc(c_rin, 16)
        sp.wait_ge(c_rel, 1)
        sp.dma_start(x_t[0][0:NS, :], A["x_sample"].rearrange("n o d -> (n o) d")).then_inc(e_x[0], 16)
        sp.dma_start(x_t[0][PAD0:P, :], A["meta_tokens"]).then_inc(e_x[0], 16)
        sp.dma_start(x_t[1][:], A["x_prompt"][0, 0:P, :]).then_inc(e_x[1], 16)
        sp.dma_start(wlr[:], w_in[:, :, IN_LR:IN_LR + RANK], allow_slow_non_contiguous=True).then_inc(c_in, 16)
        sp.dma_start(lne_g[:], A["ln_emb_g"].rearrange("(o n) -> o n", o=1).to_broadcast([P, D])).then_inc(c_in, 16)
        sp.dma_start(lne_b[:], A["ln_emb_b"].rearrange("(o n) -> o n", o=1).to_broadcast([P, D])).then_inc(c_in, 16)
        sp.wait_ge(c_id, 6)
        for i, s in enumerate(primed):
            if s in b_mo:
                continue
            sp.dma_start(prime_dram[i], prime[:]).then_inc(s, 16)

        def first(b, s):
            if isinstance(b, int) and b == 0:
                return
            if not (isinstance(b, int) and b < 2):
                sp.wait_ge(n_xn, upto(b - 2))
                sp.dma_start(x_t[s][:], A["x_prompt"][0, ds((b - 1) * P, P), :]).then_inc(e_x[s], 16)

        def second(b, s):
            sp.wait_ge(n_h, upto(b))
            sp.dma_start(h_dram[ds(b, 1)].rearrange("o p n -> p (o n)"), hn[s][:]).then_inc(h_out[s], 16)
            sp.wait_ge(t_hi, upto(b))
            sp.dma_start(hT_dram[ds(b, 1)].rearrange("o p n -> p (o n)"), hTs[s][:]).then_inc(e_hTo[s], 16)

        first(2, 0)
        sp.wait_ge(c_rel, 7)
        sp.dma_start(brow_dram.rearrange("h (p j) -> p h j", p=P), brow[:]).then_inc(c_brow, 16)
        second(0, 0)
        with sp.Fori(0, 3) as i:
            first(2 * i + 3, 1)
            second(2 * i + 1, 1)
            first(2 * i + 4, 0)
            second(2 * i + 2, 0)
        def narrow_loads(g):
            for c, w, src in ((W_KV, HD, g * HD + IN_KA), (W_KV + HD, HD, g * HD + IN_VA),
                              (W_Q, DK, g * DK + IN_Q), (W_K, DK, g * DK + IN_K), (W_QA, DV, g * DV + IN_QA)):
                sp.dma_start(wn[:, :, c:c + w], w_in[:, :, ds(src, w)]).then_inc(b_wn, 16)

        def gk_loads(g):
            sp.dma_start(gkup[:], A["gk_up"][0][:, ds(g * DK, DK)]).then_inc(b_gk, 16)
            sp.dma_start(gkb[:], A["gk_bias"][0, ds(g * DK, DK)].rearrange("(p o) -> p o", o=1)).then_inc(b_gk, 16)

        def wide_load(g, j):
            c = (IN_V, IN_R, IN_GA, IN_GB)[j]
            sp.dma_start(braw[:, j], w_in[:, :, ds(g * DV + c, DV)]).then_inc(w_raw[j], 16)

        def bias_loads(g):
            for h in range(HPG):
                sp.dma_start(bias[:, 0, h], bass.AP(tensor=brow_dram.tensor,
                                                    offset=brow_dram.offset + (g * HPG + h) * (P * LROW) + 127,
                                                    ap=[[LROW - 1, P], [1, 2 * P]])).then_inc(b_bi, 16)

        def hT_load(n, b, s):
            last = n - 1 if isinstance(b, int) else n - 2
            sp.wait_ge(b_p4, upto(last))
            sp.wait_ge(b_hl, upto(last))
            sp.dma_start(hTs[s][:], hT_dram[ds(b, 1)].rearrange("o p n -> p (o n)")).then_inc(b_hT[s], 16)

        def keys_repeat(n, s):
            sp.wait_ge(b_ka, upto(n))
            sp.dma_start(ka[s][HD:P, :], ka[s][0:HD, :]).then_inc(b_kd, 16)

        def step_loads(n0):
            with sp.Fori(0, 4) as i:
                hT_load(n0 + 2 * i + 1, 2 * i + 1, 1)
                keys_repeat(n0 + 2 * i, 0)
                hT_load(n0 + 2 * i + 2, 2 * i + 2, 0)
                keys_repeat(n0 + 2 * i + 1, 1)
            keys_repeat(n0 + 8, 0)

        gk_loads(0)
        narrow_loads(0)
        second(7, 1)
        sp.dma_start(sink[:], A["sinks"][0:1, :].to_broadcast([P, HEADS])).then_inc(b_gn, 16)
        sp.dma_start(gn[:], A["gla_norm_g"][0:1, :].to_broadcast([P, DV])).then_inc(b_gn, 16)
        second(8, 0)

        sp.wait_ge(e_lr, upto(8))
        for s in range(2):
            sp.wait_ge(e_hTo[s], 16 * (1 + 5 - s))
        hT_load(0, 0, 0)
        for j in range(WIDE):
            wide_load(0, j)
        sp.wait_ge(c_brow, 16)
        bias_loads(0)
        step_loads(0)
        with sp.Fori(1, G) as g:
            n0 = g * NB
            sp.wait_ge(b_xg, upto(n0 - 1))
            wait_apart(sp, b_p5, upto(n0 - 1))
            gk_loads(g)
            hT_load(n0, 0, 0)
            narrow_loads(g)
            for j in range(WIDE):
                wait_apart(sp, b_lo, upto(g * WIDE + j - WIDE))
                wide_load(g, j)
            wait_apart(sp, b_bs, upto(n0 - 1))
            bias_loads(g)
            step_loads(n0)
        sp.dma_start(R["swa_k_sample"][0, :, 0:WIN - 1], A["cache_swa_k"][0, :, 1:WIN]).then_inc(s_shift, 16)
        sp.dma_start(R["swa_v_sample"][0, :, 0:WIN - 1], A["cache_swa_v"][0, :, 1:WIN]).then_inc(s_shift, 16)

        sp.wait_ge(b_gg, upto(G * NB - 1))

        def state_load(g):
            sp.dma_start(st[:, g], A["state_gla"][0, :, g].rearrange("n k e -> k n e")).then_inc(s_in, 16)

        state_load(0)
        state_load(1)
        wout = A["w_out"][0].rearrange("(k p) n -> p k n", p=P)
        def wout_load(c):
            if c >= 2:
                sp.wait_ge(b_lo, upto(G * WIDE - 1 + c - 1))
            sp.dma_start(raw[:, 4 + c % 2].rearrange("p (k n) -> p k n", k=2),
                         wout[:, 2 * c:2 * c + 2, :]).then_inc(w_raw[4 + c % 2], 16)

        stageB_done(sp)

        def mg_load(k, s):
            if not (isinstance(k, int) and k < 2):
                sp.wait_ge(t_T, upto(NB + k - 2))
            sp.dma_start(mg[s][:], mg_dram[ds((k + 1) % NB, 1)].rearrange("o p n -> p (o n)")).then_inc(h_in[s], 16)

        sp.dma_start(gath[:].rearrange("n g c e -> n (g c e)"),
                     stash_dram.rearrange("n g c e -> n (g c e)")).then_inc(c_rin, 16)
        sp.dma_start(aqo[:].rearrange("d g c n -> d (g c n)"), asq[HD:P].rearrange("d g c n -> d (g c n)")).then_inc(c_rin, 16)
        state_load(2)
        state_load(3)
        wout_load(0)
        wout_load(1)
        sp.wait_ge(s_dve, S_KNEW)
        sp.dma_start(R["swa_k_sample"][0, :, WIN - 1], knew[:]).then_inc(s_new, 16)
        sp.dma_start(R["swa_v_sample"][0, :, WIN - 1], sva[:]).then_inc(s_new, 16)
        sp.wait_ge(s_new, 32)
        sp.wait_ge(s_shift, 32)
        for n in range(NS):
            sp.dma_start(Kw[:, n], R["swa_k_sample"][0, n]).then_inc(s_win, 16)
        sp.dma_start(Vw[:], R["swa_v_sample"][0].rearrange("n j g d -> j n g d")).then_inc(s_win, 16)
        for h in range(HPG):
            sp.dma_start(sbias[32 * h:32 * h + 32, :],
                         bass.AP(tensor=brow_dram.tensor, offset=brow_dram.offset + h * P * LROW + WIN,
                                 ap=[[HPG * P * LROW, G], [0, NS], [1, WIN]])).then_inc(b_gn, 16)
            sp.dma_start(ssink[32 * h:32 * h + 32, :],
                         bass.AP(tensor=A["sinks"].tensor, offset=A["sinks"].offset + h,
                                 ap=[[HPG, G], [0, NS], [1, 1]])).then_inc(b_gn, 16)
        wout_load(2)
        wout_load(3)
        sp.dma_start(ln1_g[:], A["ln1_g"][0:1, :].to_broadcast([P, D])).then_inc(o_small, 16)
        sp.dma_start(ln1_b[:], A["ln1_b"][0:1, :].to_broadcast([P, D])).then_inc(o_small, 16)
        sp.dma_start(wr[:, :, 0:4], A["w_router_group"][0].rearrange("(k p) n -> p k n", p=P)).then_inc(o_small, 16)
        sp.dma_start(wr[:, :, 4:], A["w_router_expert"][0].rearrange("(k p) n -> p k n", p=P)).then_inc(o_small, 16)
        sp.dma_start(br[:, 0:4], A["b_router_group"][0:1, :].to_broadcast([P, 4])).then_inc(o_small, 16)
        sp.dma_start(br[:, 4:], A["b_router_expert"][0:1, :].to_broadcast([P, NE])).then_inc(o_small, 16)
        for a in range(2):
            sp.dma_start(obuf_dram[(NE + a * NB) * P:(NE + (a + 1) * NB) * P, :],
                         h_dram.rearrange("b p n -> (b p) n")).then_inc(s_out, 16)
        for k in range(2):
            mg_load(k, k)
        sp.wait_ge(s_dve, S_STATE[G - 1] + 1)
        for g in range(G):
            sp.dma_start(R["gla_state_sample"][0, :, g].rearrange("n k e -> k n e"), st[:, g]).then_inc(s_out, 16)
        sp.wait_ge(s_dve, S_MERGED)
        sp.dma_start(mg_dram[0, 0:NS, :], oS.rearrange("n g e -> n (g e)")).then_inc(s_new, 16)
        sp.wait_ge(s_new, 48)

        def blk(k):
            return (k + 1) % NB if isinstance(k, int) else k + 1

        def h_load(b, s):
            if not (isinstance(b, int) and b < 2):
                sp.wait_ge(u_T, upto(b - 2))
                sp.wait_ge(h_out[s], stored(1, s, use(b, s)))
            sp.dma_start(hh[s][:], h_dram[ds(blk(b), 1)].rearrange("o p n -> p (o n)")).then_inc(e_x[s], 16)

        def h1_store(b, s):
            sp.wait_ge(n_h, upto(NB + b))
            sp.dma_start(h1_dram[ds(blk(b) * P, P), :], hh[s][:]).then_inc(h_out[s], 16)

        def o_step(b, s):
            mg_load(b + 2, s)
            h1_store(b - 1, 1 - s)
            h_load(b + 1, 1 - s)

        def m_load(t, e, j):
            src = A[("w_gate", "w_up", "w_down")[j // 2]][0]
            kc, half = (KC, j % 2) if j < 4 else (DE // P, j % 2)
            v = src[ds(e, 1)].rearrange("o (k p) n -> p (o k) n", p=P)
            v = v[:, half * kc // 2:(half + 1) * kc // 2, :]
            sp.dma_start(raw[:, j].rearrange("p (k n) -> p k n", k=kc // 2), v).then_inc(w_raw[j], 16)

        h_load(0, 0)
        h_load(1, 1)
        mg_load(2, 0)
        with sp.Fori(0, 3) as i:
            o_step(2 * i + 1, 1)
            o_step(2 * i + 2, 0)
        h1_store(6, 0)
        h_load(8, 0)
        sp.wait_ge(s_out, 16 * (G + 2))
        for j in range(6):
            m_load(0, 0, j)
        h1_store(7, 1)
        h1_store(8, 0)

        def m_up(t):
            e = t if isinstance(t, int) else sp.value_load(etab[0:1, ds(t, 1)], min_val=0, max_val=NE - 1)
            for j in range(4):
                sp.wait_ge(*piece_lo(t - 1, j))
                m_load(t, e, j)

        def m_down(t):
            e = t if isinstance(t, int) else sp.value_load(etab[0:1, ds(t, 1)], min_val=0, max_val=NE - 1)
            for j in (4, 5):
                sp.wait_ge(*piece_lo(t - 1, j))
                m_load(t, e, j)

        m_up(1)
        m_down(1)
        m_up(2)
        m_up(3)
        m_down(2)
        sp.wait_ge(d_route, 1)
        iters = 15 + (sp.value_load(novr[0:1, 0:1], min_val=0, max_val=16) + 1) // 2
        with sp.Fori(0, iters - 1) as i:
            m_up(2 * i + 4)
            m_down(2 * i + 3)
            m_up(2 * i + 5)
            m_down(2 * i + 4)
        m_down(2 * iters + 1)

        sp.wait_ge(m_yd, upto(2 * iters + 1))
        sp.wait_ge(m_x[0], 16 * (iters + 2))
        sp.wait_ge(m_yo[0], 16 * (iters + 2))
        sp.wait_ge(m_yo[1], 16 * (iters + 2))

        def f_load(b, s):
            if not (isinstance(b, int) and b < 2):
                sp.wait_ge(f_z, upto(b - 2))
            sp.dma_start(h1l[s][:], h1_dram[ds(b * P, P), :]).then_inc(h_in[s], 16)

        def f_store(b, s):
            sp.wait_ge(n_h, upto(2 * NB + b))
            if isinstance(b, int) and b == 0:
                sp.dma_start(R["y_sample"].rearrange("n o d -> (n o) d"), zo[0][0:NS, :]).then_inc(h_out[0], 16)
            else:
                sp.dma_start(R["y_prompt"][0, ds((b - 1) * P, P), :], zo[s][:]).then_inc(h_out[s], 16)

        f_load(0, 0)
        sp.dma_start(ln2_g[:], A["ln2_g"][0:1, :].to_broadcast([P, D])).then_inc(f_small, 16)
        sp.dma_start(ln2_b[:], A["ln2_b"][0:1, :].to_broadcast([P, D])).then_inc(f_small, 16)
        f_load(1, 1)
        f_load(2, 0)
        f_load(3, 1)
        f_store(0, 0)
        f_load(4, 0)
        f_store(1, 1)
        with sp.Fori(0, 2) as i:
            f_load(2 * i + 5, 1)
            f_store(2 * i + 2, 0)
            f_load(2 * i + 6, 0)
            f_store(2 * i + 3, 1)
        for b in (6, 7, 8):
            f_store(b, b % 2)
        for s in range(2):
            sp.wait_ge(h_out[s], stored(2, s, 5 - s))
        sp.wait_ge(s_out, 16 * (G + 2))
        sp.wait_ge(b_gout, 16 * 3 * G)

    @block.gpsimd
    def _(pool):
        for s in step_sems:
            pool.sem_inc(s, CREDIT)
        pool.memset(ones[:], 1.0).then_inc(c_id, 1)
        pool.memset(prime[:], 0.0).then_inc(c_id, 1)
        pool.memset(eps_c[:], EPS).then_inc(c_id, 1)
        pool.wait_ge(c_id, 3)
        pool.affine_select(out=ident[:], in_=ones[:], compare_op=ALU.is_equal, fill=0.0, base=0,
                           pattern=[[1, P]], channel_multiplier=-1).then_inc(c_id, 1)
        pool.affine_select(out=causal[:], in_=ones[:], compare_op=ALU.is_ge, fill=0.0, base=0,
                           pattern=[[1, P]], channel_multiplier=-1).then_inc(c_id, 1)
        pool.affine_select(out=strict[:], in_=ones[:], compare_op=ALU.is_gt, fill=0.0, base=0,
                           pattern=[[1, P]], channel_multiplier=-1).then_inc(c_id, 1)
        pool.wait_ge(c_id, 6)
        for s in range(2):
            pool.dma_start(prime_dram[14 + s], prime[:]).then_inc(b_mo[s], 16)
        pool.wait_ge(c_in, 48)

        def first(b, s):
            pool.wait_ge(n_hg, upto(b))
            pool.tensor_tensor(hn[s][:], hn[s][:], lne_b[:], ALU.add).then_inc(n_h, 1)

        pipelined(pool, first, lambda b, s: None)

        stage0_done(pool)
        pool.wait_ge(b_gn, 32)

        with pool.Fori(0, G) as g:
            pool.wait_ge(b_bi, 16 * HPG * (g + 1))
            wait_apart(pool, b_bs, upto(g * NB - 1))
            pool.tensor_copy(bias[:, 1], bias[:, 0]).then_inc(b_stg, 1)
            wait_apart(pool, b_stg, 2 * g + 1)
            pool.memset(bias[:, 1, :, 0:PAD0], NEG).then_inc(b_bv, 1)

            def step(n, s, uses, first):
                pool.wait_ge(b_rr, upto(n))
                if first:
                    pool.wait_ge(b_rg, upto(n - 1))
                pool.tensor_tensor(rr[:], rr[:], gn[:], ALU.mult).then_inc(b_rg, 1)
                if first:
                    wait_apart(pool, b_rg, upto(n))
                    pool.wait_ge(b_va, upto(n))
                    pool.wait_ge(b_qa, upto(n))
                    pool.wait_ge(b_vrc, upto(n))
                    pool.tensor_copy(asq[:, ds(g, 1)].rearrange("p o c n -> p (o c) n"), qa[:, :, 0:NS])
                    pool.tensor_copy(ska[:, ds(g, 1)].rearrange("p o n -> p (o n)"), ka[0][0:HD, 0:NS])
                    pool.tensor_copy(sva[:, ds(g, 1)].rearrange("p o n -> p (o n)"), va[0][0:NS, :]).then_inc(b_stg, 1)
                    for j, t in enumerate((vr[0:NS, 0:DV], rr[0:NS, :], Rt[0:NS, 1, :])):
                        pool.dma_start(stash_dram[:, ds(g, 1), j].rearrange("n o e -> n (o e)"), t).then_inc(b_std, 16)
                    pool.wait_ge(b_std, 48 * (g + 1))
                    pool.wait_ge(b_stg, 2 * g + 2)
                    pool.sem_inc(b_sta, 1)
                pool.wait_ge(b_oa, upto(n))
                pool.tensor_tensor(oa[:], oa[:], Rt[:, 1], ALU.mult).then_inc(b_ob, 1)
                pool.wait_ge(b_ob, upto(n))
                pool.wait_ge(b_mo[s], 16 * (1 + uses))
                pool.tensor_tensor(mgo[s][:], yg[:], oa[:], ALU.add).then_inc(b_mg, 1)
                wait_apart(pool, b_mg, upto(n))

            step(g * NB, 0, 5 * g, True)
            pool.dma_start(mg_dram[0, :, ds(g * DV, DV)], mgo[0][:]).then_inc(b_mo[0], 16)
            with pool.Fori(0, 4) as i:
                for s in (1, 0):
                    b = 2 * i + 1 + (1 - s)
                    step(g * NB + b, s, 4 * g + i if s else 5 * g + i + 1, False)
                    pool.dma_start(mg_dram[ds(b, 1), :, ds(g * DV, DV)].rearrange("o p n -> p (o n)"),
                                   mgo[s][:]).then_inc(b_mo[s], 16)
            wait_apart(pool, b_fin, upto(g))
            pool.dma_start(R["gla_state_prompt"][0, 0, ds(g, 1)].rearrange("o k e -> k (o e)"), Sm[:]).then_inc(b_gout, 16)
            wait_apart(pool, b_ko, upto(g))
            pool.dma_start(R["swa_k_prompt"][0, 0, :, ds(g, 1), :].rearrange("j o d -> j (o d)"), kout[:]).then_inc(b_gout, 16)
            pool.dma_start(R["swa_v_prompt"][0, 0, :, ds(g, 1), :].rearrange("j o d -> j (o d)"), va[0][:]).then_inc(b_gout, 16)
            pool.wait_ge(b_gout, 48 * (g + 1))
            pool.sem_inc(b_gfree, 1)

        stageB_done(pool)
        pool.memset(qm[:], 0.0).then_inc(s_qm, 1)
        pool.wait_ge(o_small, 96)

        def o_first(b, s):
            pool.wait_ge(n_hg, upto(NB + b))
            pool.tensor_tensor(hh[s][:], hh[s][:], ln1_b[:], ALU.add).then_inc(n_h, 1)

        pipelined(pool, o_first, lambda b, s: None)

        pool.wait_ge(o_lg, upto(8))
        pool.iota(ioti[:, 0:P], [[1, P]], base=0, channel_multiplier=0).then_inc(pool_s, 1)
        pool.iota(ioti[:, P:P + 1], [[0, 1]], base=0, channel_multiplier=1).then_inc(pool_s, 1)
        pool.iota(toki[:], [[P, NB]], base=0, channel_multiplier=1).then_inc(pool_s, 1)
        pool.iota(etab[:, 0:NE], [[1, NE]], base=0, channel_multiplier=0).then_inc(pool_s, 1)

        def low(t, j, done=m_loP):
            pool.wait_ge(*piece_hi(t, j))
            pool.tensor_tensor(wm_lo[:, j], raw[:, j], BF(wm_hi[:, j]), ALU.subtract).then_inc(done[j // 4], 1)

        low(0, 1)
        low(0, 5)
        low(0, 4, m_loD)
        pool.wait_ge(*piece_lo(0, 0))
        low(0, 2, m_loD)
        low(0, 3, m_loD)
        pool.wait_ge(d_route, 1)
        for s in range(2):
            pool.wait_ge(h_out[s], stored(1, s, 5 - s))
        iters = 15 + (pool.value_load(novr[0:1, 0:1], min_val=0, max_val=16) + 1) // 2

        def gather(t, s, free):
            if free:
                pool.wait_ge(t_T, upto(2 * NB + t - 2))
            wait_apart(pool, m_xi, upto(t - 1))
            pool.tensor_copy(xi[s][:], idx_all[:, ds(t, 1)]).then_inc(m_xi, 1)
            wait_apart(pool, m_xi, upto(t))
            pool.indirect_dma_start(out=xw[s][:], out_offset=None, in_=h1_dram,
                                    in_offset=bass.IndirectOffsetOnAxis(ap=xi[s][:, 0:1], axis=0)).then_inc(m_x[s], 16)

        gather(0, 0, False)
        gather(1, 1, False)
        low(1, 1)
        gather(2, 0, True)
        with pool.Fori(0, iters) as i:
            for s in (1, 0):
                t = 2 * i + 1 + (1 - s)
                low(t + 1, 1)
                gather(t + 2, s, True)
                low(t, 5)
        low(2 * iters + 1, 5)

        last = 2 * iters + 1
        pool.wait_ge(m_yd, upto(last))
        wait_apart(pool, m_yo[0], 16 * (iters + 2))
        pool.wait_ge(m_yo[1], 16 * (iters + 2))
        pool.wait_ge(m_x[0], 16 * (iters + 2))

        def f_first(b, s):
            wait_apart(pool, f_b, upto(b - 2))
            for c in range(2):
                pool.tensor_copy(fi[s][:, c:c + 1], ridx[:, ds(b + c * NB, 1)]).then_inc(f_i, 1)
            wait_apart(pool, f_i, upto(2 * b + 1))
            for c, t in enumerate((ya[s], yc[s])):
                pool.indirect_dma_start(out=t[:], out_offset=None, in_=obuf_dram,
                                        in_offset=bass.IndirectOffsetOnAxis(ap=fi[s][:, c:c + 1], axis=0)).then_inc(f_y[s], 16)

        def f_shift(b, s):
            pool.wait_ge(n_hg, upto(2 * NB + b))
            pool.tensor_tensor(zo[s][:], zo[s][:], ln2_b[:], ALU.add).then_inc(n_h, 1)

        f_first(0, 0)
        f_first(1, 1)
        f_first(2, 0)
        pool.wait_ge(f_small, 32)
        with pool.Fori(0, 3) as i:
            for s in (1, 0):
                b = 2 * i + 2 - s
                f_first(b + 2, s)
                f_shift(b - 1, 1 - s)
        for b in (6, 7, 8):
            f_shift(b, b % 2)

    @block.scalar
    def _(act):
        def rsqrt(src, tmp, dst, s_a, s_b, n, scale=1.0):
            act.activation(tmp, src, ACT.Ln, bias=eps_c[0:src.shape[0], :], scale=scale).then_inc(s_a, 1)
            act.wait_ge(s_a, n)
            act.activation(dst, tmp, ACT.Exp, scale=-0.5).then_inc(s_b, 1)

        act.preload_act_table_set("natural_log_exp_and_others")
        act.wait_ge(c_id, 6)
        act.wait_ge(c_in, 48)

        def first(b, s):
            act.wait_ge(n_st, upto(b))
            rsqrt(st0[s][:, 13:14], st0[s][:, 14:15], st0[s][:, 15:16], n_ln, n_rs, upto(b))
            act.wait_ge(n_nm, upto(b))
            act.wait_ge(n_rs, upto(b))
            act.wait_ge(t_T, upto(b - 2))
            act.wait_ge(h_out[s], stored(0, s, use(b, s)))
            act.activation(hn[s][:], x_t[s][:], ACT.Identity, bias=st0[s][:, 14:15], scale=st0[s][:, 15:16]).then_inc(n_xn, 1)

        def e_hT(b, s):
            act.wait_ge(t_T, upto(b))
            act.wait_ge(e_hTo[s], 16 * (1 + use(b, s)))
            act.wait_ge(e_lr, upto(b - 2))
            act.copy(hTs[s][:], PS[:, 6 * s:6 * s + 2].rearrange("p a n -> p (a n)")).then_inc(t_hi, 1)

        def e_lrT(b):
            act.wait_ge(e_lr, upto(b))
            act.copy(lrT[:, ds(b * P, P)], PS[0:RANK, 2, 0:P]).then_inc(e_lrd, 1)

        first(0, 0)
        first(1, 1)
        e_hT(0, 0)
        first(2, 0)
        e_hT(1, 1)
        with act.Fori(0, 3) as i:
            for s in (1, 0):
                b = 2 * i + 4 - s
                first(b, s)
                e_lrT(b - 3)
                e_hT(b - 1, 1 - s)
        e_lrT(6)
        e_hT(8, 0)
        e_lrT(7)
        e_lrT(8)

        stage0_done(act)
        act.wait_ge(b_gn, 32)
        with act.Fori(0, G) as g:
            n0 = g * NB

            def wide(j):
                act.wait_ge(w_raw[j], 16 * (g + 1))
                if j < 2:
                    act.wait_ge(b_vr, upto(n0 - 1))
                else:
                    act.wait_ge(b_gg, upto(n0 - 1))
                act.copy(w_hi[:, :, j * DV:(j + 1) * DV], braw[:, j]).then_inc(b_hi, 1)

            def step(n, s, uses, first):
                if first:
                    act.wait_ge(b_gk, 32 * (g + 1))
                    wide(0)
                    wide(1)
                act.wait_ge(b_gg, upto(n - 1))
                act.wait_ge(b_hT[s], 16 * (uses + 1))
                act.copy(hT_hl[:, 0], hTs[s][:]).then_inc(b_hs, 1)
                act.wait_ge(b_p5, upto(n))
                act.wait_ge(b_mn, upto(n - 1))
                if not first:
                    act.wait_ge(b_sta, upto(g))
                act.wait_ge(b_o, upto(n - 1))
                act.activation(xg[:], PS[:, 5, P:2 * P], ACT.Identity, bias=gkb[:, 0:1]).then_inc(b_xg, 1)
                act.copy(ka[s][0:HD, :], PS[0:HD, 5, 0:P])
                act.copy(vT[HD:P, :], PS[HD:P, 5, 0:P]).then_inc(b_ka, 1)
                act.wait_ge(b_xg, upto(n))
                act.wait_ge(b_g16, upto(n - 1))
                act.activation(ax[:], xg[:], ACT.Abs).then_inc(b_ax, 1)
                act.wait_ge(b_ax, upto(n))
                act.activation(ax[:], ax[:], ACT.Exp, scale=-1.0).then_inc(b_ex, 1)
                act.wait_ge(b_ex, upto(n))
                act.activation(ax[:], ax[:], ACT.Ln, bias=1.0).then_inc(b_lx, 1)
                if first:
                    wide(2)
                    wide(3)
                act.wait_ge(b_bmn, upto(n))
                act.wait_ge(b_qq, upto(n - 1))
                act.wait_ge(b_Sm, upto(n - 1))
                act.wait_ge(b_e2, upto(n - 1))
                if first:
                    act.activation(gse[:, ds(g, 1)].rearrange("p o n -> p (o n)"), g16[:, 0:NS], ACT.Exp, scale=1.0 / TAU)
                act.activation(ek[:], b16[:], ACT.Exp, bias=bm[:, 0:1], scale=-1.0 / TAU)
                act.activation(ebm[:], bm[:, 0:1], ACT.Exp)
                act.activation(eq[:], b16[:], ACT.Exp, bias=bm[:, 1:2], scale=1.0 / TAU).then_inc(b_eq, 1)
                act.wait_ge(b_vt, upto(n))
                if first:
                    act.wait_ge(b_gfree, upto(g - 1))
                act.copy(va[s][:], PS[:, 5, 2 * P:2 * P + HD]).then_inc(b_va, 1)
                act.wait_ge(b_vr, upto(n))
                act.wait_ge(b_rr, upto(n - 1))
                act.copy(vr[:], PS[:, 2]).then_inc(b_vrc, 1)
                act.wait_ge(b_vrc, upto(n))
                act.wait_ge(b_E2, upto(n - 1))
                act.activation(Et[:, 0], vr[:, DV:2 * DV], ACT.Exp, scale=-1.0).then_inc(b_er, 1)
                act.wait_ge(b_nmx, upto(n))
                act.wait_ge(b_den, upto(n - 1))
                lo = P if first else 0
                for h in range(HPG):
                    act.activation(Sc[:, h, lo:], Sc[:, h, lo:], ACT.Exp, bias=nmx[:, h:h + 1], accum_out=su[:, h:h + 1])
                act.activation(es[:], sk[:], ACT.Exp).then_inc(b_P, 1)
                act.wait_ge(b_gg, upto(n))
                act.wait_ge(b_R, upto(n - 1))
                act.activation(Et[:, 1:3].rearrange("p a n -> p (a n)"), PS[:, 3], ACT.Exp, scale=-1.0).then_inc(b_eg, 1)
                act.wait_ge(b_pt, upto(n))
                if first:
                    act.sem_inc(b_pc, 1)
                else:
                    act.copy(Pt[:, 0].rearrange("p h q -> p (h q)"), PS[:, 0]).then_inc(b_pc, 1)
                act.wait_ge(b_o, upto(n))
                act.wait_ge(b_E2, upto(n))
                act.activation(Et[:, 0], PS[:, 7, 0:DV], ACT.Square, accum_out=ssq[:]).then_inc(b_sq, 1)
                act.wait_ge(b_sq, upto(n))
                act.wait_ge(b_yg, upto(n - 1))
                rsqrt(ssq[:], lnv[:], rstd[:], b_lv, b_rs, upto(n), scale=1.0 / DV)

            step(n0, 0, 5 * g, True)
            with act.Fori(0, 4) as i:
                step(n0 + 2 * i + 1, 1, 4 * g + i, False)
                step(n0 + 2 * i + 2, 0, 5 * g + i + 1, False)

        stageB_done(act)
        for c in range(4):
            act.wait_ge(w_raw[4 + c % 2], 16 * (c // 2 + 1))
            act.copy(wo_hi[:, 2 * c:2 * c + 2].rearrange("p k n -> p (k n)"), raw[:, 4 + c % 2]).then_inc(b_hi, 1)

        for a in range(8):
            act.wait_ge(s_pe, S_KT + a)
            act.copy(KT[:].rearrange("p g n k -> p (g n k)")[:, a * 512:(a + 1) * 512], PS[0:HD, 6 + a % 2]).then_inc(act_s, 1)
        act.wait_ge(s_dve, S_NMX)
        act.activation(sS2[:], sS2[:], ACT.Exp, bias=sm8[:, 1:2], accum_out=sm8[:, 3:4]).then_inc(act_s, 1)
        act.activation(sm8[:, 4:5], sm8[:, 2:3], ACT.Exp).then_inc(act_s, 1)
        act.wait_ge(s_dve, S_SSQ)
        act.activation(s8[:, 1], s8[:, 0], ACT.Ln, bias=eps_c[0:NS, :], scale=1.0 / DV).then_inc(act_s, 1)
        act.wait_ge(act_s, 11)
        act.activation(s8[:, 2], s8[:, 1], ACT.Exp, scale=-0.5).then_inc(act_s, 1)

        act.wait_ge(s_dve, S_MERGED)

        def o_high(b, s):
            act.wait_ge(t_T, upto(NB + b))
            act.wait_ge(o_z, upto(b - 2))
            act.copy(mT_hi[s][:], PS[:, 0:2].rearrange("p a n -> p (a n)")).then_inc(t_hi, 1)

        def o_copy(b):
            act.wait_ge(u_T, upto(b))
            act.wait_ge(o_rl, upto(b - 1))
            act.copy(h1T[:], PS[:, 4:6].rearrange("p a n -> p (a n)")).then_inc(u_c, 1)

        def o_norm(b, s):
            act.wait_ge(n_st, upto(NB + b))
            rsqrt(st1[s][:, 13:14], st1[s][:, 14:15], st1[s][:, 15:16], n_ln, n_rs, upto(NB + b))
            act.wait_ge(n_nm, upto(NB + b))
            act.activation(hh[s][:], hh[s][:], ACT.Identity, bias=st1[s][:, 14:15], scale=st1[s][:, 15:16]).then_inc(n_xn, 1)

        def o_step(b, s):
            o_copy(b - 1)
            o_norm(b, s)
            o_high(b + 2, s)

        o_high(0, 0)
        o_high(1, 1)
        o_norm(0, 0)
        o_high(2, 0)
        with act.Fori(0, 3) as i:
            o_step(2 * i + 1, 1)
            o_step(2 * i + 2, 0)
        o_copy(6)
        o_norm(7, 1)
        o_copy(7)
        o_norm(8, 0)
        o_copy(8)

        act.wait_ge(d_g, 1)
        act.activation(gq[0][:], gq[0][:], ACT.Exp).then_inc(act_s, 1)
        def high(t, j):
            act.wait_ge(w_raw[j], 16 * (RAW_BASE[j] + t + 1))
            act.wait_ge(*piece_used(t - 1, j))
            act.wait_ge(*piece_lo(t - 1, j))
            act.copy(wm_hi[:, j], raw[:, j]).then_inc(m_hi[j // 4], 1)

        for j in range(6):
            high(0, j)
        act.wait_ge(d_g, 2)
        act.activation(rt["e"][:], rt["d"][:], ACT.Exp).then_inc(act_s, 1)

        act.wait_ge(d_route, 1)
        act.wait_ge(s_out, 16 * (G + 2))
        iters = 15 + (act.value_load(novr[0:1, 0:1], min_val=0, max_val=16) + 1) // 2

        def x_high(t):
            act.wait_ge(t_T, upto(2 * NB + t))
            act.wait_ge(*piece_used(t - 1, 3))
            act.copy(xT_hi[:], PS[:, 0:2].rearrange("p a n -> p (a n)")).then_inc(t_hi, 1)

        def m_step(t, s, uses, prev, more):
            if more:
                high(t + 1, 0)
            act.wait_ge(*piece_used(t, 1))
            act.wait_ge(m_hm, upto(t - 1))
            act.activation(sg_t[:], PS[:, 2], ACT.Silu).then_inc(m_sg, 1)
            if more:
                high(t + 1, 1)
                high(t + 1, 2)
                x_high(t + 1)
                high(t + 1, 3)
            if prev:
                high(t, 4)
                high(t, 5)
            act.wait_ge(u_T, upto(NB + t))
            act.copy(hT_hi[:], PS[:, 4]).then_inc(u_c, 1)
            if prev:
                y_out(t - 1, 1 - s, uses)

        def y_out(t, s, uses):
            act.wait_ge(*piece_used(t, 5))
            act.wait_ge(m_yo[s], 16 * (1 + uses))
            act.copy(yb[s][:, 0:512], PS[:, 5]).then_inc(m_ya, 1)
            act.wait_ge(m_ya, upto(t))
            act.wait_ge(m_yd, upto(t))
            act.dma_start(obuf_dram[ds(t * P, P), :], yb[s][:]).then_inc(m_yo[s], 16)

        x_high(0)
        m_step(0, 0, 0, False, True)
        with act.Fori(0, iters) as i:
            m_step(2 * i + 1, 1, i, True, True)
            m_step(2 * i + 2, 0, i, True, True)
        m_step(2 * iters + 1, 1, iters, True, False)
        y_out(2 * iters + 1, 1, iters)

        act.preload_act_table_set("natural_log_exp_and_others")
        act.wait_ge(m_yo[0], 16 * (iters + 2))
        act.wait_ge(m_yo[1], 16 * (iters + 2))

        def f_weigh(b, s):
            act.wait_ge(f_w, upto(b))
            act.wait_ge(f_y[s], 32 * (use(b, s) + 1))
            act.activation(ya[s][:], ya[s][:], ACT.Copy, scale=fw[s][:, 0:1]).then_inc(f_a, 1)

        def f_norm(b, s):
            act.wait_ge(n_st, upto(2 * NB + b))
            rsqrt(st2[s][:, 13:14], st2[s][:, 14:15], st2[s][:, 15:16], n_ln, n_rs, upto(2 * NB + b))
            act.wait_ge(n_nm, upto(2 * NB + b))
            act.activation(zz[s][:], zz[s][:], ACT.Identity, bias=st2[s][:, 14:15], scale=st2[s][:, 15:16]).then_inc(n_xn, 1)

        f_weigh(0, 0)
        with act.Fori(0, 4) as i:
            f_weigh(2 * i + 1, 1)
            f_norm(2 * i, 0)
            f_weigh(2 * i + 2, 0)
            f_norm(2 * i + 1, 1)
        f_norm(8, 0)

    @block.vector
    def _(dve):
        count = [0]

        def link(ins):
            count[0] += 1
            ins.then_inc(dve_s, 1)
            dve.wait_ge(dve_s, count[0])

        dve.memset(x_t[0][:], 0.0).then_inc(c_rel, 1)
        dve.memset(brow[:, :, 0:WIN], NEG)
        dve.memset(brow[:, :, 2 * WIN:LROW], NEG).then_inc(c_rel, 1)
        dve.wait_ge(c_rin, 32)
        dve.tensor_copy(relw[:], relb[:].rearrange("p (h o) -> p h o", o=1).to_broadcast([32, HEADS, P])).then_inc(c_rel, 1)
        for a in range(4):
            dve.wait_ge(c_rpe, a + 1)
            dve.tensor_copy(brow[:, 4 * a:4 * a + 4, WIN:2 * WIN],
                            PS[:, 4 + a].rearrange("p (h n) -> p h n", h=4)).then_inc(c_rel, 1)

        def e_stats(b, s):
            if isinstance(b, int) and b == 0:
                dve.wait_ge(e_x[0], 32)
            else:
                dve.wait_ge(e_x[s], 16 * (2 - s + use(b, s)))
            stats(dve, x_t[s], st0[s], n_sa, n_st, upto(b))

        def e_mean(b, s):
            dve.wait_ge(n_rs, upto(b))
            dve.scalar_tensor_tensor(st0[s][:, 14:15], st0[s][:, 12:13], -1.0, st0[s][:, 15:16],
                                     ALU.mult, ALU.mult).then_inc(n_nm, 1)

        def e_scale(b, s):
            dve.wait_ge(n_xn, upto(b))
            dve.tensor_tensor(hn[s][:], hn[s][:], lne_g[:], ALU.mult).then_inc(n_hg, 1)

        e_stats(0, 0)
        e_mean(0, 0)
        dve.wait_ge(c_in, 48)
        with dve.Fori(0, 4) as i:
            for s in (1, 0):
                b = 2 * i + 2 - s
                e_stats(b, s)
                e_scale(b - 1, 1 - s)
                e_mean(b, s)
        e_scale(8, 0)

        stage0_done(dve)
        dve.wait_ge(b_gn, 32)
        with dve.Fori(0, G) as g:
            n0 = g * NB

            def wide(j):
                dve.wait_ge(b_hi, upto(g * WIDE + j))
                c = slice(j * DV, (j + 1) * DV)
                dve.tensor_tensor(w_lo[:, :, c], braw[:, j], BF(w_hi[:, :, c]), ALU.subtract).then_inc(b_lo, 1)

            def step(n, s, first, variant):
                lo = P if first else 0
                if first:
                    wide(0)
                    wide(1)
                dve.wait_ge(b_hs, upto(n))
                dve.tensor_tensor(hT_hl[:, 1], hTs[s][:], BF(hT_hl[:, 0]), ALU.subtract).then_inc(b_hl, 1)
                dve.wait_ge(b_xg, upto(n))
                dve.wait_ge(b_g16, upto(n - 1))
                dve.tensor_scalar(mn[:], xg[:], 0.0, None, ALU.min).then_inc(b_mn, 1)
                dve.wait_ge(b_mn, upto(n))
                dve.wait_ge(b_lx, upto(n))
                dve.wait_ge(b_eq, upto(n - 1))
                dve.tensor_tensor(g16[:], mn[:], ax[:], ALU.subtract).then_inc(b_g16, 1)
                dve.wait_ge(b_g16, upto(n))
                dve.tensor_tensor_scan(b16[:], ones[:], g16[:], 0.0, ALU.mult, ALU.add).then_inc(b_b16, 1)
                dve.wait_ge(b_b16, upto(n))
                dve.tensor_scalar(bm[:, 0:1], b16[:, P // 2 - 1:P // 2], 1.0 / TAU, None, ALU.mult)
                dve.tensor_scalar(bm[:, 1:2], b16[:, P // 2 - 1:P // 2], -1.0 / TAU, None, ALU.mult).then_inc(b_bmn, 1)
                dve.wait_ge(b_p4, upto(n))
                dve.wait_ge(b_sc, upto(n - 1))
                if not first:
                    dve.wait_ge(b_sta, upto(g))
                dve.tensor_copy(qa[:].rearrange("p c n -> p (c n)"), PS[:, 4, 2 * P:4 * P]).then_inc(b_qa, 1)
                if first:
                    dve.tensor_scalar(gsq[:, ds(g, 1)].rearrange("p o n -> p (o n)"), PS[:, 4, 0:NS],
                                      DK ** -0.5, None, ALU.mult)
                    dve.tensor_copy(gsk[:, ds(g, 1)].rearrange("p o n -> p (o n)"), PS[:, 4, P:P + NS])
                dve.wait_ge(b_eq, upto(n))
                dve.wait_ge(b_o, upto(n - 1))
                dve.tensor_tensor(kk[:], PS[:, 4, P:2 * P], ek[:], ALU.mult).then_inc(b_kk, 1)
                if first:
                    dve.wait_ge(b_kk, upto(n))
                    dve.memset(kk[:, 0:PAD0], 0.0)
                dve.scalar_tensor_tensor(qq[:], PS[:, 4, 0:P], DK ** -0.5, eq[:], ALU.mult, ALU.mult).then_inc(b_qq, 1)
                if first:
                    wide(2)
                    wide(3)
                if first:
                    dve.wait_ge(b_gfree, upto(g - 1))
                    dve.memset(Sm[:], 0.0).then_inc(b_Sm, 1)
                else:
                    dve.wait_ge(b_T, upto(n - 1))
                    dve.tensor_scalar(Sm[:], Tn[:], e2[:, 0:1], ebm[:, 0:1], ALU.mult, ALU.mult).then_inc(b_Sm, 1)
                    dve.wait_ge(b_Sm, upto(n))
                dve.tensor_copy(e2[:], eq[:, P - 1:P]).then_inc(b_e2, 1)
                wait_apart(dve, b_sc, upto(n))
                dve.wait_ge(b_pt, upto(n - 1))
                dve.wait_ge(b_bv, upto(g))
                for half in range(2):
                    dst = Sc[:].rearrange("p (c f) k -> p c f k", f=2)[:, :, half, lo:]
                    if isinstance(variant, int):
                        bs = bias[:, variant].rearrange("p (c f) k -> p c f k", f=2)[:, :, half, lo:]
                    else:
                        bs = bias[:, ds(variant, 1)].rearrange("p o (c f) k -> p (o c) f k", f=2)[:, :, half, lo:]
                    last = dve.scalar_tensor_tensor(dst, PS[:, half].rearrange("p (c k) -> p c k", c=2)[:, :, lo:],
                                                    HD ** -0.5, bs, ALU.mult, ALU.add)
                last.then_inc(b_bs, 1)
                dve.wait_ge(b_bs, upto(n))
                if first:
                    dve.memset(Sc[:, :, P:P + PAD0], NEG).then_inc(b_sz, 1)
                    dve.wait_ge(b_sz, g + 1)
                dve.wait_ge(b_P, upto(n - 1))
                dve.reduce_max(mx[:], Sc[:, :, lo:], X).then_inc(b_mx, 1)
                dve.wait_ge(b_mx, upto(n))
                dve.tensor_tensor(mx[:], mx[:], sink[:, ds(g * HPG, HPG)], ALU.max).then_inc(b_mx2, 1)
                dve.wait_ge(b_mx2, upto(n))
                dve.tensor_tensor(sk[:], sink[:, ds(g * HPG, HPG)], mx[:], ALU.subtract)
                dve.tensor_scalar(nmx[:], mx[:], -1.0, None, ALU.mult).then_inc(b_nmx, 1)
                dve.wait_ge(b_A, upto(n))
                dve.tensor_tensor(At[:], PS[:, 6, 0:P], causal[:], ALU.mult)
                dve.tensor_copy(kd[:], PS[:, 6, P:2 * P]).then_inc(b_At, 1)
                dve.wait_ge(b_pt, upto(n))
                dve.tensor_copy(Pt[:, 1].rearrange("p h q -> p (h q)"), PS[:, 1]).then_inc(b_pd, 1)
                dve.wait_ge(b_up, upto(n))
                dve.tensor_tensor(Tn[:], PS[:, 6, DV:2 * DV], Sm[:], ALU.add).then_inc(b_T, 1)
                dve.wait_ge(b_eg, upto(n))
                dve.tensor_scalar(Et[:, 1:3], Et[:, 1:3], 1.0, None, ALU.add).then_inc(b_E1, 1)
                dve.wait_ge(b_E1, upto(n))
                dve.scalar_tensor_tensor(Et[:, 1], Et[:, 0], 1.0, Et[:, 1], ALU.add, ALU.mult).then_inc(b_E2, 1)
                dve.wait_ge(b_E2, upto(n))
                dve.wait_ge(b_ob, upto(n - 1))
                if not first:
                    dve.wait_ge(b_sta, upto(g))
                dve.reciprocal(Rt[:], Et[:, 1:3]).then_inc(b_R, 1)
                dve.wait_ge(b_R, upto(n))
                dve.tensor_tensor(rr[:], vr[:, DV:2 * DV], Rt[:, 0], ALU.mult).then_inc(b_rr, 1)
                dve.wait_ge(b_P, upto(n))
                dve.tensor_tensor(su[:], su[:], es[:], ALU.add).then_inc(b_den, 1)
                dve.wait_ge(b_den, upto(n))
                dve.reciprocal(rden[:], su[:]).then_inc(b_rden, 1)
                dve.wait_ge(b_rs, upto(n))
                dve.wait_ge(b_rg, upto(n))
                dve.wait_ge(b_mg, upto(n - 1))
                dve.scalar_tensor_tensor(yg[:], PS[:, 7, 0:DV], rstd[:, 0:1], rr[:], ALU.mult, ALU.mult).then_inc(b_yg, 1)
                dve.wait_ge(b_rden, upto(n))
                dve.tensor_tensor(oa[:].rearrange("p (h d) -> p h d", h=HPG),
                                  PS[:, 7, DV:2 * DV].rearrange("p (h d) -> p h d", h=HPG),
                                  rden[:].rearrange("p (h o) -> p h o", o=1).to_broadcast([P, HPG, HD]),
                                  ALU.mult).then_inc(b_oa, 1)

            step(n0, 0, True, 0)
            with dve.Fori(0, 4) as i:
                step(n0 + 2 * i + 1, 1, False, (3 - i) // 3)
                step(n0 + 2 * i + 2, 0, False, 0)
            dve.wait_ge(b_T, upto(n0 + 8))
            dve.wait_ge(b_o, upto(n0 + 8))
            dve.wait_ge(b_e2, upto(n0 + 8))
            dve.tensor_scalar(Sm[:], Tn[:], e2[:, 0:1], None, ALU.mult).then_inc(b_fin, 1)
            dve.wait_ge(b_kT, upto(g))
            dve.tensor_copy(kout[:], PS[:, 6, 0:HD]).then_inc(b_ko, 1)

        stageB_done(dve)

        def mark(ins, s):
            ins.then_inc(s, 1)

        dve.wait_ge(s_pe, S_KT8)
        link(dve.tensor_copy(kt8[:].rearrange("n g k -> n (g k)"), PS[0:NS, 0]))
        mark(dve.tensor_copy(knew[:].rearrange("n g d -> n (g d)"), PS[0:NS, 1, 0:G * HD]), s_dve)
        dve.wait_ge(s_qm, 1)
        for g in range(G):
            last = dve.tensor_copy(qm[:].rearrange("p g n m -> p g (n m)")[:, g, 0:NS * NS:NS + 1], gsq[:, g])
        mark(last, s_qm)
        dve.wait_ge(c_rin, 64)
        for half, src in enumerate((asq[0:HD], aqo[:])):
            for c in range(2):
                last = dve.tensor_copy(aq4[:, :, :, 2 * c + half], src[:, :, c, :])
        mark(last, s_dve)

        def key_masks(g):
            if g >= 2:
                dve.wait_ge(s_pe, S_OUTER + 2 * (g - 2) + 1)
            mark(dve.tensor_tensor(km[g % 2][:], kt8[:, g:g + 1, :].to_broadcast([NS, NS, P]),
                                   ident[0:NS, 0:NS].rearrange("t (n o) -> t n o", o=1).to_broadcast([NS, NS, P]),
                                   ALU.mult), s_dve)

        key_masks(0)
        key_masks(1)
        dve.wait_ge(s_in, 16 * G)
        for g in range(G):
            for half in range(2):
                dve.wait_ge(s_pe, S_OUTER + 2 * g + half)
                for n in range(4 * half, 4 * half + 4):
                    last = dve.scalar_tensor_tensor(st[:, g, n], st[:, g, n], gse[:, g, n:n + 1],
                                                    PS[:, 2 + n // 2, (n % 2) * DV:(n % 2 + 1) * DV], ALU.mult, ALU.add)
                mark(last, s_dve)
            if g + 2 < G:
                key_masks(g + 2)
            dve.wait_ge(b_hi, upto(G * WIDE + g))
            dve.tensor_tensor(wo_lo[:, 2 * g:2 * g + 2].rearrange("p k n -> p (k n)"), raw[:, 4 + g % 2],
                              BF(wo_hi[:, 2 * g:2 * g + 2].rearrange("p k n -> p (k n)")), ALU.subtract).then_inc(b_lo, 1)
        dve.wait_ge(s_pe, S_OG)
        link(dve.tensor_copy(oS.rearrange("n (a g) e -> n a (g e)", a=2), PS[0:NS, 0:2]))
        mark(dve.tensor_tensor(oQ, oS, oS, ALU.mult), s_dve)
        dve.wait_ge(s_dve, S_SSQ - 1)
        mark(dve.reduce_sum(s8[:, 0], oQ, X), s_dve)
        dve.wait_ge(s_pe, S_SC)
        mark(dve.tensor_copy(sT[:], PS[:, 2, 0:P]), s_dve)
        dve.wait_ge(b_gn, 32 + 16 * 8)
        dve.wait_ge(s_pe, S_TR)
        link(dve.scalar_tensor_tensor(sS2[:], PS[:, 4, 0:P], HD ** -0.5, sbias[:], ALU.mult, ALU.add))
        link(dve.reduce_max(sm8[:, 0:1], sS2[:], X))
        link(dve.tensor_tensor(sm8[:, 0:1], sm8[:, 0:1], ssink[:], ALU.max))
        link(dve.tensor_tensor(sm8[:, 2:3], ssink[:], sm8[:, 0:1], ALU.subtract))
        mark(dve.tensor_scalar(sm8[:, 1:2], sm8[:, 0:1], -1.0, None, ALU.mult), s_dve)
        dve.wait_ge(act_s, 10)
        link(dve.tensor_tensor(sm8[:, 5:6], sm8[:, 3:4], sm8[:, 4:5], ALU.add))
        link(dve.reciprocal(sm8[:, 6:7], sm8[:, 5:6]))
        mark(dve.tensor_scalar(sS2[:], sS2[:], sm8[:, 6:7], None, ALU.mult), s_dve)
        dve.wait_ge(s_pe, S_PT)
        mark(dve.tensor_copy(sPT[:], PS[:, 4, 0:P]), s_dve)
        dve.wait_ge(s_pe, S_PV)
        for h in range(HPG):
            last = dve.tensor_copy(oT[:, h].rearrange("d g n -> d (g n)"),
                                   PS[0:HD, 5, 0:P].rearrange("d (m q) -> d m q", q=HPG)[:, :, h])
        mark(last, s_dve)
        dve.wait_ge(act_s, 12)
        link(dve.tensor_tensor(oS, oS, s8[:, 2].rearrange("n (g o) -> n g o", o=1).to_broadcast([NS, G, DV]), ALU.mult))
        link(dve.tensor_tensor(oS, oS, gath[:, :, 1], ALU.mult))
        dve.wait_ge(s_pe, S_OT)
        link(dve.tensor_tensor(oQ, PS[0:NS, 0:2].rearrange("n a (g e) -> n (a g) e", e=DV), gath[:, :, 2], ALU.mult))
        mark(dve.tensor_tensor(oS, oS, oQ, ALU.add), s_dve)

        dve.wait_ge(s_dve, S_MERGED)
        dve.wait_ge(o_small, 96)

        def o_low(b, s):
            dve.wait_ge(t_hi, upto(NB + b))
            dve.tensor_tensor(mT_lo[s][:], PS[:, 0:2].rearrange("p a n -> p (a n)"), BF(mT_hi[s][:]), ALU.subtract).then_inc(t_lo, 1)

        def o_norm(b, s):
            dve.wait_ge(o_z, upto(b))
            dve.wait_ge(e_x[s], 16 * (6 - 2 * s + use(b, s) + 1))
            dve.scalar_tensor_tensor(hh[s][:], hh[s][:], ALPHA, PS[:, 2:4].rearrange("p a n -> p (a n)"),
                                     ALU.mult, ALU.add).then_inc(o_zz, 1)
            dve.wait_ge(o_zz, upto(b))
            stats(dve, hh[s], st1[s], n_sa, n_st, upto(NB + b))
            dve.wait_ge(n_rs, upto(NB + b))
            dve.scalar_tensor_tensor(st1[s][:, 14:15], st1[s][:, 12:13], -1.0, st1[s][:, 15:16],
                                     ALU.mult, ALU.mult).then_inc(n_nm, 1)
            dve.wait_ge(n_xn, upto(NB + b))
            dve.tensor_tensor(hh[s][:], hh[s][:], ln1_g[:], ALU.mult).then_inc(n_hg, 1)

        def o_logits(b):
            dve.wait_ge(o_rl, upto(b))
            dve.tensor_tensor(lg[:, ds((b + 1) % NB if isinstance(b, int) else b + 1, 1)].rearrange("p o n -> p (o n)"), PS[:, 6, 0:4 + NE], br[:], ALU.add).then_inc(o_lg, 1)

        def o_step(b, s):
            o_norm(b, s)
            o_low(b + 2, s)
            o_logits(b - 1)

        o_low(0, 0)
        o_low(1, 1)
        o_norm(0, 0)
        o_low(2, 0)
        with dve.Fori(0, 3) as i:
            o_step(2 * i + 1, 1)
            o_step(2 * i + 2, 0)
        o_norm(7, 1)
        o_logits(6)
        o_norm(8, 0)
        o_logits(7)
        o_logits(8)

        def bc(t, n):
            return t.rearrange("p (a o) -> p a o", o=1).to_broadcast([P, t.shape[1], n])

        def row(t, a):
            return t.rearrange("p (o n) -> p o n", o=1).to_broadcast([P, a, t.shape[1]])

        def first_max(x, m, n, iota, out, tmp):
            link(dve.tensor_tensor(out, x, bc(m, n), ALU.is_equal))
            link(dve.scalar_tensor_tensor(tmp, out, -100.0, row(iota, NB), ALU.mult, ALU.add))
            link(dve.tensor_reduce(rt["mi"][:], tmp, X, ALU.min))
            link(dve.tensor_tensor(out, tmp, bc(rt["mi"][:], n), ALU.is_equal))

        dve.wait_ge(o_lg, upto(8))
        dve.wait_ge(n_h, upto(NB + 8))
        for s in range(2):
            dve.wait_ge(h_out[s], stored(1, s, 5 - s))
        dve.wait_ge(pool_s, 4)
        link(dve.tensor_copy(iot[:], ioti[:]))
        link(dve.tensor_copy(tok[:], toki[:]))
        link(dve.memset(again[:], 1.0))
        link(dve.memset(again[:, :, 0], 0.0))
        i4, i18, i32, i50, i128 = (iot[:, 0:n] for n in (4, 18, NE, MAXBLK, P))
        ip = iot[:, P:P + 1]
        gl, el = lg[:, :, 0:4], lg[:, :, 4:]
        link(dve.reduce_max(rt["gm"][:], gl, X))
        mark(dve.tensor_tensor(gq[0][:], gl, bc(rt["gm"][:], 4), ALU.subtract), d_g)
        first_max(gl, rt["gm"][:], 4, i4, gq[1][:], gq[2][:])
        dve.wait_ge(act_s, 13)
        link(dve.reduce_sum(rt["sg"][:], gq[0][:], X))
        link(dve.reciprocal(rt["pg"][:], rt["sg"][:]))
        link(dve.tensor_scalar(gq[2][:], gq[1][:], -NEG, NEG, ALU.mult, ALU.add))
        link(dve.tensor_tensor(em[:].rearrange("p b (g e) -> p b g e", g=G), el.rearrange("p b (g e) -> p b g e", g=G),
                               gq[2][:].rearrange("p b (g o) -> p b g o", o=1).to_broadcast([P, NB, G, NE // G]), ALU.add))
        link(dve.reduce_max(rt["m1"][:], em[:], X))
        first_max(em[:], rt["m1"][:], NE, i32, O[1][:], tt_[:])
        link(dve.scalar_tensor_tensor(em2[:], O[1][:], 2 * NEG, em[:], ALU.mult, ALU.add))
        link(dve.reduce_max(rt["m2"][:], em2[:], X))
        first_max(em2[:], rt["m2"][:], NE, i32, O[2][:], tt_[:])
        mark(dve.tensor_tensor(rt["d"][:], rt["m2"][:], rt["m1"][:], ALU.subtract), d_g)
        link(dve.tensor_scalar(valid[:, 0:1], ip, float(NS), None, ALU.is_lt))
        link(dve.tensor_scalar(valid[:, 1:2], ip, float(PAD0), None, ALU.is_ge))
        link(dve.tensor_tensor(valid[:, 0:1], valid[:, 0:1], valid[:, 1:2], ALU.add))
        for c in (1, 2):
            link(dve.tensor_scalar(O[c][:, 0], O[c][:, 0], valid[:, 0:1], None, ALU.mult))
        mark(dve.tensor_tensor(O[0][:], O[1][:], O[2][:], ALU.add), d_O)
        dve.wait_ge(act_s, 14)
        link(dve.tensor_scalar(rt["s"][:], rt["e"][:], 1.0, None, ALU.add))
        link(dve.reciprocal(rt["r"][:], rt["s"][:]))
        link(dve.tensor_tensor(wts[:, 0:NB, 0], rt["r"][:], rt["pg"][:], ALU.mult))
        link(dve.memset(wts[:, NB], 0.0))
        link(dve.tensor_tensor(wts[:, 0:NB, 1], wts[:, 0:NB, 0], rt["e"][:], ALU.mult))
        def low(t, j):
            dve.wait_ge(*piece_hi(t, j))
            dve.tensor_tensor(wm_lo[:, j], raw[:, j], BF(wm_hi[:, j]), ALU.subtract).then_inc(m_loD[j // 4], 1)

        low(0, 0)
        dve.wait_ge(d_pre, 1)
        link(dve.tensor_copy(pre[:].rearrange("p b e -> p (b e)"), PS[:, 0, 0:NB * NE]))
        link(dve.tensor_copy(tot[:].rearrange("p b e -> p (b e)").rearrange("p (e b) -> p e b", b=NB),
                             PS[:, 1, 0:NB * NE].rearrange("p (b e) -> p e b", e=NE)))
        link(dve.tensor_tensor_scan(cumb[:], again[:].rearrange("p e b -> p (e b)"),
                                    tot[:].rearrange("p b e -> p (b e)"), 0.0, ALU.mult, ALU.add))
        cb = cumb[:].rearrange("p (e b) -> p b e", b=NB)
        link(dve.tensor_tensor(pre[:], pre[:], cb, ALU.add))
        link(dve.tensor_tensor(pre[:], pre[:], tot[:].rearrange("p b e -> p (b e)").rearrange("p (e b) -> p b e", b=NB), ALU.subtract))
        link(dve.tensor_copy(cum[:], cb[:, NB - 1]))
        link(dve.tensor_scalar(ov[:], cum[:], float(P), None, ALU.is_gt))
        for k in range(2, NB):
            link(dve.scalar_tensor_tensor(ov[:], cum[:], float(P * k), ov[:], ALU.is_gt, ALU.add))
        link(dve.tensor_tensor_scan(ove[:], ones[:, 0:NE], ov[:], 0.0, ALU.mult, ALU.add))
        link(dve.tensor_tensor(ovs[:], ove[:], ov[:], ALU.subtract))
        for c in range(2):
            oc = O[c + 1][:]
            for src, name in ((pre[:], "rk"), (row(ovs[:], NB), "bs"), (row(i32, NB), "ie")):
                link(dve.tensor_tensor(tt_[:], oc, src, ALU.mult))
                link(dve.reduce_sum(sl[name][:, c * NB:(c + 1) * NB], tt_[:], X))
        v = {n: t[:] for n, t in sl.items()}
        link(dve.tensor_scalar(v["k1"], v["rk"], float(P), None, ALU.is_ge))
        link(dve.tensor_copy(v["k"], v["k1"]))
        for k in range(2, NB):
            link(dve.scalar_tensor_tensor(v["k"], v["rk"], float(P * k), v["k"], ALU.is_ge, ALU.add))
        link(dve.tensor_tensor(v["b"], v["bs"], v["k"], ALU.add))
        link(dve.scalar_tensor_tensor(v["b"], v["b"], float(NE - 1), v["ie"], ALU.add, ALU.subtract))
        link(dve.tensor_tensor(v["b"], v["b"], v["k1"], ALU.mult))
        link(dve.tensor_tensor(v["b"], v["b"], v["ie"], ALU.add))
        link(dve.scalar_tensor_tensor(v["r"], v["k"], -float(P), v["rk"], ALU.mult, ALU.add))
        link(dve.scalar_tensor_tensor(v["w"], v["b"], float(P), v["r"], ALU.mult, ALU.add))
        link(dve.tensor_copy(ridx[:], v["w"]))
        link(dve.tensor_tensor(oh_r[:], bc(v["r"], P), row(i128, 2 * NB), ALU.is_equal))
        link(dve.tensor_tensor(oh_b[:], bc(v["b"], MAXBLK), row(i50, 2 * NB), ALU.is_equal))
        link(dve.tensor_scalar(tok[:, 0:1], tok[:, 0:1], valid[:, 0:1], None, ALU.mult))
        for c in range(2):
            last = dve.tensor_tensor(oh_b[:, c * NB:(c + 1) * NB], oh_b[:, c * NB:(c + 1) * NB], bc(tok[:], MAXBLK), ALU.mult)
        mark(last, d_O)
        link(dve.tensor_tensor(cmp_[:], row(ove[:], 18), bc(i18, NE), ALU.is_le))
        link(dve.reduce_sum(ef[:], cmp_[:], X))
        link(dve.tensor_scalar(ef[:], ef[:], float(NE - 1), None, ALU.min))
        link(dve.tensor_copy(etab[:, NE:MAXBLK], ef[:]))
        link(dve.tensor_copy(novr[:], ove[:, NE - 1:NE]))
        dve.wait_ge(d_table, 1)
        mark(dve.tensor_copy(idx_all[:], PS[:, 2, 0:MAXBLK]), d_route)

        dve.wait_ge(d_route, 1)
        iters = 15 + (dve.value_load(novr[0:1, 0:1], min_val=0, max_val=16) + 1) // 2

        def y_half(t, s, uses):
            dve.wait_ge(*piece_used(t, 5))
            dve.wait_ge(m_yo[s], 16 * (1 + uses))
            dve.tensor_copy(yb[s][:, 512:1024], PS[:, 6]).then_inc(m_yd, 1)

        def x_low(t):
            dve.wait_ge(t_hi, upto(2 * NB + t))
            dve.tensor_tensor(xT_lo[:], PS[:, 0:2].rearrange("p a n -> p (a n)"), BF(xT_hi[:]), ALU.subtract).then_inc(t_lo, 1)

        def m_step(t, s, uses, prev, more):
            if more:
                low(t + 1, 0)
                low(t + 1, 2)
            dve.wait_ge(m_sg, upto(t))
            dve.wait_ge(*piece_used(t, 3))
            dve.wait_ge(u_T, upto(NB + t - 1))
            dve.tensor_tensor(hm[:], PS[:, 3], sg_t[:], ALU.mult).then_inc(m_hm, 1)
            if more:
                x_low(t + 1)
                low(t + 1, 3)
            if prev:
                low(t, 4)
            dve.wait_ge(u_c, upto(NB + t))
            dve.tensor_tensor(hT_lo[:], PS[:, 4], BF(hT_hi[:]), ALU.subtract).then_inc(m_hlo, 1)
            if prev:
                y_half(t - 1, 1 - s, uses)

        dve.wait_ge(*piece_lo(0, 3))
        x_low(0)
        m_step(0, 0, 0, False, True)
        with dve.Fori(0, iters) as i:
            m_step(2 * i + 1, 1, i, True, True)
            m_step(2 * i + 2, 0, i, True, True)
        m_step(2 * iters + 1, 1, iters, True, False)
        y_half(2 * iters + 1, 1, iters)

        dve.wait_ge(m_yo[0], 16 * (iters + 2))
        dve.wait_ge(m_yo[1], 16 * (iters + 2))
        dve.wait_ge(*piece_lo(2 * iters + 1, 5))
        def f_weights(b, s):
            dve.wait_ge(f_b, upto(b - 2))
            dve.tensor_copy(fw[s][:], wts[:, ds(b, 1)].rearrange("p o c -> p (o c)")).then_inc(f_w, 1)

        def f_sum(b, s):
            dve.wait_ge(f_a, upto(b))
            dve.wait_ge(f_w, upto(b))
            dve.wait_ge(n_hg, upto(2 * NB + b - 2))
            dve.scalar_tensor_tensor(zz[s][:], yc[s][:], fw[s][:, 1:2], ya[s][:], ALU.mult, ALU.add).then_inc(f_b, 1)
            dve.wait_ge(f_b, upto(b))
            dve.wait_ge(h_in[s], 16 * (5 - s + use(b, s) + 1))
            dve.scalar_tensor_tensor(zz[s][:], h1l[s][:], ALPHA, zz[s][:], ALU.mult, ALU.add).then_inc(f_z, 1)
            dve.wait_ge(f_z, upto(b))
            stats(dve, zz[s], st2[s], n_sa, n_st, upto(2 * NB + b))

        def f_mean(b, s):
            dve.wait_ge(n_rs, upto(2 * NB + b))
            dve.scalar_tensor_tensor(st2[s][:, 14:15], st2[s][:, 12:13], -1.0, st2[s][:, 15:16],
                                     ALU.mult, ALU.mult).then_inc(n_nm, 1)

        def f_scale(b, s):
            dve.wait_ge(n_xn, upto(2 * NB + b))
            dve.wait_ge(h_out[s], stored(2, s, use(b, s)))
            dve.tensor_tensor(zo[s][:], zz[s][:], ln2_g[:], ALU.mult).then_inc(n_hg, 1)

        f_weights(0, 0)
        f_weights(1, 1)
        f_sum(0, 0)
        f_mean(0, 0)
        dve.wait_ge(f_small, 32)
        with dve.Fori(0, 4) as i:
            for s in (1, 0):
                b = 2 * i + 2 - s
                f_weights(b + 1, 1 - s)
                f_sum(b, s)
                f_scale(b - 1, 1 - s)
                f_mean(b, s)
        f_scale(8, 0)

    @block.tensor
    def _(pe):
        def split_product(out, x_hi, x_lo, w_hi_, w_lo_, start, stop):
            pe.matmul(out, x_hi, w_hi_, start=start, stop=False)
            pe.matmul(out, x_hi, w_lo_, start=False, stop=False)
            return pe.matmul(out, x_lo, w_hi_, start=False, stop=stop)

        def transposes(bank, src, count):
            for k in range(count):
                last = pe.transpose(PS[:, bank + k // 4, (k % 4) * P:(k % 4 + 1) * P], src[:, k * P:(k + 1) * P], ident[:])
            return last

        pe.wait_ge(c_id, 6)
        pe.wait_ge(c_rel, 3)
        for a in range(4):
            for h in range(4):
                last = pe.matmul(PS[:, 4 + a, h * P:(h + 1) * P], relw[:, 4 * a + h, :], onehot[:], start=True, stop=True)
            last.then_inc(c_rpe, 1)
        pe.wait_ge(c_in, 48)

        def e_transposes(b, s):
            pe.wait_ge(n_h, upto(b))
            pe.wait_ge(t_hi, upto(b - 2))
            transposes(6 * s, hn[s], KC).then_inc(t_T, 1)

        def e_lowrank(b, s):
            pe.wait_ge(t_hi, upto(b))
            pe.wait_ge(e_lrd, upto(b - 1))
            for k in range(KC):
                last = pe.matmul(PS[0:RANK, 2, 0:P], wlr[:, k], hTs[s][:, k * P:(k + 1) * P], start=(k == 0), stop=(k == KC - 1))
            last.then_inc(e_lr, 1)

        e_transposes(0, 0)
        pe.wait_ge(c_rel, 7)
        with pe.Fori(0, 4) as i:
            for s in (1, 0):
                b = 2 * i + 2 - s
                e_transposes(b, s)
                e_lowrank(b - 1, 1 - s)
        e_lowrank(8, 0)

        pe.wait_ge(e_lrd, upto(8))
        with pe.Fori(0, G) as g:
            n0 = g * NB

            def step(n, b, s, uses, first):
                hT = lambda k: hTs[s][:, k * P:(k + 1) * P]

                def feature_major(out, c):
                    for k in range(KC):
                        last = pe.matmul(out, wn[:, k, c:c + P], hT(k), start=(k == 0), stop=(k == KC - 1))
                    return last

                def wide(out, c):
                    for k in range(KC):
                        cols = slice(c, c + 2 * DV)
                        last = split_product(out, hT_hl[:, 0, k * P:(k + 1) * P], hT_hl[:, 1, k * P:(k + 1) * P],
                                             w_hi[:, k, cols], w_lo[:, k, cols], k == 0, k == KC - 1)
                    return last

                if first:
                    pe.wait_ge(b_gk, 32 * (g + 1))
                    pe.wait_ge(b_wn, 80 * (g + 1))
                pe.wait_ge(b_hT[s], 16 * (uses + 1))
                pe.wait_ge(b_va, upto(n - 1))
                pe.matmul(PS[:, 5, P:2 * P], gkup[:], lrT[:, ds(b * P, P)], start=True, stop=True)
                feature_major(PS[:, 5, 0:P], W_KV).then_inc(b_p5, 1)
                pe.wait_ge(b_qq, upto(n - 1))
                feature_major(PS[:, 4, 0:P], W_Q)
                feature_major(PS[:, 4, P:2 * P], W_K)
                feature_major(PS[:, 4, 2 * P:3 * P], W_QA)
                feature_major(PS[:, 4, 3 * P:4 * P], W_QA + P).then_inc(b_p4, 1)
                wait_apart(pe, b_ka, upto(n))
                pe.transpose(PS[:, 5, 2 * P:2 * P + HD], vT[HD:P, :], ident[HD:P, HD:P]).then_inc(b_vt, 1)
                pe.wait_ge(b_hl, upto(n))
                if first:
                    pe.wait_ge(b_lo, upto(g * WIDE + 1))
                pe.wait_ge(b_vrc, upto(n - 1))
                wide(PS[:, 2], W_V).then_inc(b_vr, 1)
                pe.wait_ge(b_qa, upto(n))
                pe.wait_ge(b_kd, 16 * (n + 1))
                pe.wait_ge(b_pc, upto(n - 1))
                pe.wait_ge(b_pd, upto(n - 1))
                for half in range(2):
                    r = slice(half * HD, (half + 1) * HD)
                    for c in range(2):
                        if not first:
                            pe.matmul(PS[:, half, c * 2 * P:c * 2 * P + P], qa[r, c, :], ka[1 - s][r, :], start=True, stop=True)
                        last = pe.matmul(PS[:, half, c * 2 * P + P:(c + 1) * 2 * P], qa[r, c, :], ka[s][r, :], start=True, stop=True)
                last.then_inc(b_sc, 1)
                pe.wait_ge(b_qq, upto(n))
                pe.wait_ge(b_T, upto(n - 1))
                if first:
                    pe.wait_ge(b_ko, upto(g - 1))
                pe.matmul(PS[:, 6, 0:P], kk[:], qq[:], start=True, stop=True)
                pe.transpose(PS[:, 6, P:2 * P], kk[:], ident[:]).then_inc(b_A, 1)
                if first:
                    pe.wait_ge(b_lo, upto(g * WIDE + 3))
                pe.wait_ge(b_eg, upto(n - 1))
                wide(PS[:, 3], W_GA).then_inc(b_gg, 1)
                pe.wait_ge(b_P, upto(n))
                pe.wait_ge(b_bs, upto(n))
                for h in range(HPG):
                    if not first:
                        pe.transpose(PS[:, 0, h * P:(h + 1) * P], Sc[:, h, 0:P], ident[:])
                    last = pe.transpose(PS[:, 1, h * P:(h + 1) * P], Sc[:, h, P:2 * P], ident[:])
                last.then_inc(b_pt, 1)
                pe.wait_ge(b_oa, upto(n - 1))
                pe.wait_ge(b_At, upto(n))
                pe.wait_ge(b_vrc, upto(n))
                pe.wait_ge(b_Sm, upto(n))
                pe.matmul(PS[:, 6, DV:2 * DV], kd[:], vr[:, 0:DV], start=True, stop=True).then_inc(b_up, 1)
                pe.matmul(PS[:, 7, 0:DV], At[:], vr[:, 0:DV], start=True, stop=False)
                pe.matmul(PS[:, 7, 0:DV], qq[:], Sm[:], start=False, stop=True)
                pe.wait_ge(b_va, upto(n))
                pe.wait_ge(b_pc, upto(n))
                pe.wait_ge(b_pd, upto(n))
                for h in range(HPG):
                    o = PS[:, 7, DV + h * HD:DV + (h + 1) * HD]
                    if not first:
                        pe.matmul(o, Pt[:, 0, h], va[1 - s][:], start=True, stop=False)
                    last = pe.matmul(o, Pt[:, 1, h], va[s][:], start=first, stop=True)
                last.then_inc(b_o, 1)

            step(n0, 0, 0, 5 * g, True)
            with pe.Fori(0, 4) as i:
                step(n0 + 2 * i + 1, 2 * i + 1, 1, 4 * g + i, False)
                step(n0 + 2 * i + 2, 2 * i + 2, 0, 5 * g + i + 1, False)
            wait_apart(pe, b_T, upto(n0 + 8))
            pe.transpose(PS[:, 6, 0:HD], ka[0][0:HD, :], ident[0:HD, 0:HD]).then_inc(b_kT, 1)

        stageB_done(pe)
        pe.wait_ge(b_ko, upto(G - 1))
        for g in range(G):
            pe.transpose(PS[0:NS, 0, g * P:(g + 1) * P], gsk[:, g, :], ident[:])
        for g in range(G):
            last = pe.transpose(PS[0:NS, 1, g * HD:(g + 1) * HD], ska[0:HD, g, :], ident[0:HD, 0:HD])
        last.then_inc(s_pe, 1)

        def outer(g):
            pe.wait_ge(s_dve, S_KM[g])
            for half in range(2):
                if g:
                    pe.wait_ge(s_dve, S_STATE[g - 1] + half)
                for n in range(4 * half, 4 * half + 4):
                    last = pe.matmul(PS[:, 2 + n // 2, (n % 2) * DV:(n % 2 + 1) * DV], km[g % 2][:, n, :], gath[:, g, 0, :],
                                     start=True, stop=True)
                last.then_inc(s_pe, 1)

        def read_out(g):
            pe.wait_ge(s_dve, S_STATE[g] + 1)
            for n in range(NS):
                last = pe.matmul(PS[0:NS, g // 2, (g % 2) * DV:(g % 2 + 1) * DV], qm[:, g, n, :], st[:, g, n],
                                 start=(n == 0), stop=(n == NS - 1))
            return last

        pe.wait_ge(s_qm, 2)
        pe.wait_ge(c_rin, 64)
        outer(0)
        for g in range(1, G):
            outer(g)
            read_out(g - 1)
        read_out(G - 1).then_inc(s_pe, 1)
        pe.wait_ge(s_win, 16 * 9)
        for a in range(8):
            if a >= 2:
                pe.wait_ge(act_s, a - 1)
            for m in range(4):
                g, n = (4 * a + m) // NS, (4 * a + m) % NS
                last = pe.transpose(PS[0:HD, 6 + a % 2, m * P:(m + 1) * P], Kw[:, n, g], ident[:])
            last.then_inc(s_pe, 1)
        pe.wait_ge(act_s, 8)
        for g in range(G):
            for n in range(NS):
                m = g * NS + n
                last = pe.matmul(PS[:, 2, m:m + 97:32], KT[:, g, n, :], aq4[:, g, n, :], start=True, stop=True)
        last.then_inc(s_pe, 1)
        pe.wait_ge(s_dve, S_ST)
        pe.transpose(PS[:, 4, 0:P], sT[:], ident[:]).then_inc(s_pe, 1)
        pe.wait_ge(s_dve, S_PROB)
        pe.transpose(PS[:, 4, 0:P], sS2[:], ident[:]).then_inc(s_pe, 1)
        pe.wait_ge(s_dve, S_PTC)
        for g in range(G):
            for n in range(NS):
                m = g * NS + n
                last = pe.matmul(PS[0:HD, 5, 4 * m:4 * m + 4], Vw[:, n, g, :],
                                 sPT[:].rearrange("k (q m) -> k q m", q=4)[:, :, m], start=True, stop=True)
        last.then_inc(s_pe, 1)
        pe.wait_ge(s_dve, S_OTC)
        for g in range(G):
            for h in range(HPG):
                c = (g % 2) * DV + h * HD
                last = pe.transpose(PS[0:NS, g // 2, c:c + HD], oT[:, h, g, :], ident[0:HD, 0:HD])
        last.then_inc(s_pe, 1)

        pe.wait_ge(b_lo, upto(G * WIDE - 1 + 4))
        pe.wait_ge(s_dve, S_MERGED)
        pe.wait_ge(o_small, 96)

        def o_transposes(b, s):
            pe.wait_ge(h_in[s], 16 * (use(b, s) + 1))
            pe.wait_ge(t_lo, upto(b - 1))
            transposes(0, mg[s], KC).then_inc(t_T, 1)

        def o_product(b, s):
            pe.wait_ge(t_lo, upto(b))
            pe.wait_ge(o_zz, upto(b - 1))
            for half in range(2):
                c = slice(half * 512, half * 512 + 512)
                for k in range(KC):
                    last = split_product(PS[:, 2 + half], mT_hi[s][:, k * P:(k + 1) * P], mT_lo[s][:, k * P:(k + 1) * P],
                                         wo_hi[:, k, c], wo_lo[:, k, c], k == 0, k == KC - 1)
            last.then_inc(o_z, 1)

        def o_h1T(b, s):
            pe.wait_ge(n_h, upto(NB + b))
            pe.wait_ge(u_c, upto(b - 1))
            transposes(4, hh[s], KC).then_inc(u_T, 1)

        def o_logits(b):
            pe.wait_ge(u_c, upto(b))
            pe.wait_ge(o_lg, upto(b - 1))
            for k in range(KC):
                last = pe.matmul(PS[:, 6, 0:4 + NE], h1T[:, k * P:(k + 1) * P], wr[:, k, :], start=(k == 0), stop=(k == KC - 1))
            last.then_inc(o_rl, 1)

        def o_step(b, s):
            o_product(b, s)
            o_h1T(b - 1, 1 - s)
            o_transposes(b + 2, s)
            o_logits(b - 1)

        o_transposes(0, 0)
        o_transposes(1, 1)
        o_product(0, 0)
        o_transposes(2, 0)
        with pe.Fori(0, 3) as i:
            o_step(2 * i + 1, 1)
            o_step(2 * i + 2, 0)
        o_product(7, 1)
        o_h1T(6, 0)
        o_logits(6)
        o_product(8, 0)
        o_h1T(7, 1)
        o_logits(7)
        o_h1T(8, 0)
        o_logits(8)

        pe.wait_ge(d_O, 1)
        pe.matmul(PS[:, 0, 0:NB * NE], strict[:], O[0][:].rearrange("p b e -> p (b e)"), start=True, stop=True)
        pe.matmul(PS[:, 1, 0:NB * NE], ones[:], O[0][:].rearrange("p b e -> p (b e)"), start=True, stop=True).then_inc(d_pre, 1)

        pe.wait_ge(d_O, 2)
        for a in range(2 * NB):
            last = pe.matmul(PS[:, 2, 0:MAXBLK], oh_r[:, a], oh_b[:, a], start=(a == 0), stop=(a == 2 * NB - 1))
        last.then_inc(d_table, 1)

        pe.wait_ge(d_route, 1)
        iters = 15 + (pe.value_load(novr[0:1, 0:1], min_val=0, max_val=16) + 1) // 2

        def up(t, bank, j0):
            for k in range(KC):
                j, c = j0 + k // 4, (k % 4) * DE
                if k % 4 == 0:
                    pe.wait_ge(*piece_lo(t, j))
                last = split_product(PS[:, bank], xT_hi[:, k * P:(k + 1) * P], xT_lo[:, k * P:(k + 1) * P],
                                     wm_hi[:, j, c:c + DE], wm_lo[:, j, c:c + DE], k == 0, k == KC - 1)
                if k % 4 == 3:
                    last.then_inc(m_used[j // 4], 1)

        def down(t):
            pe.wait_ge(m_hlo, upto(t))
            pe.wait_ge(m_ya, upto(t - 1))
            pe.wait_ge(m_yd, upto(t - 1))
            for k in range(DE // P):
                j = 4 + k // 2
                if k % 2 == 0:
                    pe.wait_ge(*piece_lo(t, j))
                for half in range(2):
                    c = (k % 2) * D + half * 512
                    last = split_product(PS[:, 5 + half], hT_hi[:, k * P:(k + 1) * P], hT_lo[:, k * P:(k + 1) * P],
                                         wm_hi[:, j, c:c + 512], wm_lo[:, j, c:c + 512], k == 0, k == DE // P - 1)
                if k % 2 == 1:
                    last.then_inc(m_used[j // 4], 1)

        def x_transposes(t, s, uses):
            pe.wait_ge(m_x[s], 16 * (uses + 1))
            pe.wait_ge(t_lo, upto(NB + t - 1))
            transposes(0, xw[s], KC).then_inc(t_T, 1)

        def m_step(t, s, uses, prev, more):
            pe.wait_ge(t_lo, upto(NB + t))
            pe.wait_ge(m_sg, upto(t - 1))
            up(t, 2, 0)
            pe.wait_ge(m_hm, upto(t - 1))
            up(t, 3, 2)
            if more:
                x_transposes(t + 1, 1 - s, uses)
            if prev:
                down(t - 1)
            pe.wait_ge(m_hm, upto(t))
            pe.wait_ge(m_hlo, upto(t - 1))
            transposes(4, hm, DE // P).then_inc(u_T, 1)

        x_transposes(0, 0, 0)
        m_step(0, 0, 0, False, True)
        with pe.Fori(0, iters) as i:
            m_step(2 * i + 1, 1, i + 1, True, True)
            m_step(2 * i + 2, 0, i + 1, True, True)
        m_step(2 * iters + 1, 1, None, True, False)
        down(2 * iters + 1)

    ctx.close()


INPUTS = ("x_prompt", "x_sample", "state_gla", "cache_swa_k", "cache_swa_v", "meta_tokens", "ln_emb_g", "ln_emb_b",
          "rel_bias", "w_in", "gk_up", "gk_bias", "gla_norm_g", "sinks", "w_out", "ln1_g", "ln1_b", "w_router_group",
          "b_router_group", "w_router_expert", "b_router_expert", "w_gate", "w_up", "w_down", "ln2_g", "ln2_b")
RESULTS = (("y_prompt", (1, 1024, D)), ("y_sample", (NS, 1, D)), ("gla_state_prompt", (1, 1, G, DK, DV)),
           ("swa_k_prompt", (1, 1, WIN, G, HD)), ("swa_v_prompt", (1, 1, WIN, G, HD)),
           ("gla_state_sample", (1, NS, G, DK, DV)), ("swa_k_sample", (1, NS, WIN, G, HD)),
           ("swa_v_sample", (1, NS, WIN, G, HD)))


def bucket_onehot():
    import math

    import numpy as np

    dist = np.arange(WIN - 1, -1, -1)
    large = 16 + (np.log(np.maximum(dist, 1).astype(np.float32) / 16) / math.log(128 / 16) * 16).astype(np.int32)
    bucket = np.where(dist < 16, dist, np.minimum(large, 31))
    return (np.arange(32)[:, None] == bucket[None, :]).astype(np.float32)


def kernel(**inputs):
    import numpy as np
    import concourse.bacc as bacc
    from concourse.bass_utils import run_bass_kernel_spmd

    nc = bacc.Bacc("TRN2", target_bir_lowering=False, num_devices=1)
    arrays = {name: np.ascontiguousarray(inputs[name]) for name in INPUTS}
    arrays["onehot"] = bucket_onehot()
    A = {n: nc.dram_tensor(f"in_{n}", a.shape, F32, kind="ExternalInput").ap() for n, a in arrays.items()}
    R = {n: nc.dram_tensor(f"out_{n}", shape, F32, kind="ExternalOutput").ap() for n, shape in RESULTS}
    build(nc, A, R)
    r = run_bass_kernel_spmd(nc, [{f"in_{n}": a for n, a in arrays.items()}], core_ids=[0])
    return tuple(r.results[0][f"out_{n}"] for n, _ in RESULTS)
```
